# Optimizing a Trainium2 kernel written in Bass

```python
import jax, jax.numpy as jnp
from jax import lax
import numpy as np

D_MODEL = 1024
BATCH = 1
SEQ = 1024
DEPTH = 1
DEC_BATCH = 8
DEC_SEQ = 4
PAST_LEN = 2048
PAGE_SIZE = 128

CONV_CH = 512
CONV_W = 31
N_HEADS = 8
HEAD_DIM = 64
N_KV = 2
Q_PER_KV = N_HEADS // N_KV
ROPE_DIM = HEAD_DIM // 4
ROPE_THETA = 500000.0
CMP_BLOCK = 64
SEL_BLOCK = CMP_BLOCK
N_SEL = 16
WINDOW = 512
WIN_BLOCK = 128
CMP_HID = 2 * HEAD_DIM
D_MIX = CONV_CH + N_HEADS * HEAD_DIM
COL_Q = N_HEADS * HEAD_DIM
COL_KV = 2 * N_KV * HEAD_DIM
COL_GATE = 3 * N_HEADS
D_IN = 2 * CONV_CH + COL_Q + 3 * COL_KV + COL_GATE
N_GROUPS = 4
EXPERTS_PER_GROUP = 8
N_EXPERTS = N_GROUPS * EXPERTS_PER_GROUP
TOP_K = 2
D_EXPERT = 512
MOE_CHUNK = 128

RMS_EPS = 1e-6
LN_EPS = 1e-5
NEG_INF = -1e30
ATT_SCALE = HEAD_DIM ** -0.5

kernel_name = 'hymba_conformer_nsa_hmoe_step'

def rmsnorm(x, g):
    xf = x.astype(jnp.float32)
    y = xf * lax.rsqrt(jnp.mean(xf * xf, axis=-1, keepdims=True) + RMS_EPS)
    return (y * g.astype(jnp.float32)).astype(x.dtype)

def layernorm(x, g, b):
    xf = x.astype(jnp.float32)
    mu = jnp.mean(xf, axis=-1, keepdims=True)
    var = jnp.mean(jnp.square(xf - mu), axis=-1, keepdims=True)
    y = (xf - mu) * lax.rsqrt(var + LN_EPS) * g.astype(jnp.float32) + b.astype(jnp.float32)
    return y.astype(x.dtype)

def masked_softmax(s, valid):
    s = jnp.where(valid, s, NEG_INF)
    return jnp.where(valid, jax.nn.softmax(s, axis=-1), 0.0)

def apply_rope(x, pos):
    half = ROPE_DIM // 2
    inv = ROPE_THETA ** (-jnp.arange(half, dtype=jnp.float32) / half)
    ang = pos.astype(jnp.float32)[:, None] * inv
    ang = ang.reshape((ang.shape[0],) + (1,) * (x.ndim - 3) + (half,))
    cos, sin = jnp.cos(ang), jnp.sin(ang)
    xr = x[..., :ROPE_DIM].astype(jnp.float32)
    x1, x2 = xr[..., :half], xr[..., half:]
    rot = jnp.concatenate([x1 * cos - x2 * sin, x1 * sin + x2 * cos], axis=-1).astype(x.dtype)
    return jnp.concatenate([rot, x[..., ROPE_DIM:]], axis=-1)

def mix_inputs(x, pos, ln1, w_in):
    b, t, _ = x.shape
    p = rmsnorm(x, ln1) @ w_in
    conv_in = p[..., :CONV_CH] * jax.nn.sigmoid(p[..., CONV_CH:2 * CONV_CH])
    o = 2 * CONV_CH
    q = apply_rope(p[..., o:o + COL_Q].reshape(b, t, N_KV, Q_PER_KV, HEAD_DIM), pos)
    o += COL_Q
    kvs = []
    for _ in range(3):
        kv = p[..., o:o + COL_KV].reshape(b, t, N_KV, 2, HEAD_DIM)
        kvs.append(jnp.stack([apply_rope(kv[..., 0, :], pos), kv[..., 1, :]], axis=-2))
        o += COL_KV
    gates = jax.nn.sigmoid(p[..., o:o + COL_GATE].reshape(b, t, N_KV, Q_PER_KV, 3))
    return conv_in, q, kvs[0], kvs[1], kvs[2], gates

def conv_module(a_ext, dw_w, dw_b, ln_g, ln_b):
    y = lax.conv_general_dilated(a_ext, dw_w[:, None, :], window_strides=(1,), padding='VALID',
                                 dimension_numbers=('NWC', 'WIO', 'NWC'),
                                 feature_group_count=CONV_CH) + dw_b
    return jax.nn.silu(layernorm(y, ln_g, ln_b))

def compress_blocks(rows, pos_emb, w_k1, w_k2, w_v1, w_v2):
    b, g = rows.shape[0], rows.shape[2]
    n = rows.shape[1] // CMP_BLOCK
    blocks = rows.reshape(b, n, CMP_BLOCK, g, 2, HEAD_DIM)

    def phi(x, pe, w1, w2):
        h = jnp.einsum('bnlgd,ldh->bngh', x, w1) + jnp.einsum('ld,ldh->h', pe, w1)
        return jax.nn.silu(h) @ w2

    return (phi(blocks[..., 0, :], pos_emb[:, 0], w_k1, w_k2),
            phi(blocks[..., 1, :], pos_emb[:, 1], w_v1, w_v2))

def compressed_attention(q, k_c, v_c, q_pos):
    nb = k_c.shape[1]
    s = jnp.einsum('btgrd,bngd->btgrn', q, k_c).astype(jnp.float32) * ATT_SCALE
    valid = ((jnp.arange(nb) + 1) * CMP_BLOCK - 1)[None, :] <= q_pos[:, None]
    p = masked_softmax(s, valid[None, :, None, None, :])
    o = jnp.einsum('btgrn,bngd->btgrd', p.astype(v_c.dtype), v_c)
    return o, p.sum(axis=3)

def select_blocks(importance, q_pos):
    nb = importance.shape[-1]
    own = (q_pos // SEL_BLOCK)[None, :, None, None]
    cand = jnp.arange(nb)[None, None, None, :] < own
    score = jnp.where(cand, importance, -1.0)
    _, idx = lax.top_k(score, min(N_SEL, nb))
    return idx, idx < own

def block_rows(idx, valid):
    rows = (idx[..., None] * SEL_BLOCK + jnp.arange(SEL_BLOCK)).reshape(idx.shape[:-1] + (-1,))
    return rows, jnp.repeat(valid, SEL_BLOCK, axis=-1)

def selected_attention(q, kv_sel, valid_sel, kv_own, valid_own):
    s_sel = jnp.einsum('btgrd,btgsd->btgrs', q, kv_sel[..., 0, :])
    s_own = jnp.einsum('btgrd,bsgd->btgrs', q, kv_own[..., 0, :])
    s = jnp.concatenate([s_sel, s_own], axis=-1).astype(jnp.float32) * ATT_SCALE
    valid = jnp.concatenate([jnp.broadcast_to(valid_sel[:, :, :, None, :], s_sel.shape),
                             jnp.broadcast_to(valid_own[None, :, None, None, :], s_own.shape)], axis=-1)
    p = masked_softmax(s, valid).astype(kv_sel.dtype)
    n_sel = s_sel.shape[-1]
    return (jnp.einsum('btgrs,btgsd->btgrd', p[..., :n_sel], kv_sel[..., 1, :])
            + jnp.einsum('btgrs,bsgd->btgrd', p[..., n_sel:], kv_own[..., 1, :]))

def window_attention(q, kv, q_pos, k_pos):
    s = jnp.einsum('...tgrd,...sgd->...tgrs', q, kv[..., 0, :]).astype(jnp.float32) * ATT_SCALE
    diff = q_pos[..., :, None] - k_pos[..., None, :]
    valid = (diff >= 0) & (diff < WINDOW) & (k_pos[..., None, :] >= 0)
    p = masked_softmax(s, valid[..., :, None, None, :])
    return jnp.einsum('...tgrs,...sgd->...tgrd', p.astype(kv.dtype), kv[..., 1, :])

def combine_branches(gates, o_cmp, o_sel, o_win):
    o = gates[..., 0:1] * o_cmp + gates[..., 1:2] * o_sel + gates[..., 2:3] * o_win
    return o.reshape(o.shape[:2] + (N_HEADS * HEAD_DIM,))

def nsa_prompt(q, cmp_kv, sel_kv, win_kv, gates, pos, cmp_w):
    b, t = q.shape[:2]
    k_c, v_c = compress_blocks(cmp_kv, *cmp_w)
    o_cmp, imp = compressed_attention(q, k_c, v_c, pos)
    idx, valid = select_blocks(imp, pos)
    nqb = t // SEL_BLOCK

    def to_blocks(a):
        return jnp.moveaxis(a.reshape((b, nqb, SEL_BLOCK) + a.shape[2:]), 1, 0)

    own_mask = jnp.tril(jnp.ones((SEL_BLOCK, SEL_BLOCK), dtype=bool))
    bi = jnp.arange(b)[:, None, None, None]
    gi = jnp.arange(N_KV)[None, None, :, None]

    def sel_block(args):
        qb, ib, vb, kvo = args
        rows, vrows = block_rows(ib, vb)
        return selected_attention(qb, sel_kv[bi, rows, gi], vrows, kvo, own_mask)

    o_sel = lax.map(sel_block, (to_blocks(q), to_blocks(idx), to_blocks(valid), to_blocks(sel_kv)))
    o_sel = jnp.moveaxis(o_sel, 0, 1).reshape(q.shape)
    nwb = t // WIN_BLOCK
    nback = WINDOW // WIN_BLOCK
    padded = jnp.pad(win_kv, ((0, 0), (nback * WIN_BLOCK, 0), (0, 0), (0, 0), (0, 0)))
    kv_band = jnp.concatenate(
        [padded[:, j * WIN_BLOCK:j * WIN_BLOCK + t].reshape(b, nwb, WIN_BLOCK, N_KV, 2, HEAD_DIM)
         for j in range(nback + 1)], axis=2)
    q_pos = pos.reshape(nwb, WIN_BLOCK)
    k_pos = (jnp.arange(nwb)[:, None] - nback) * WIN_BLOCK + jnp.arange((nback + 1) * WIN_BLOCK)[None, :]
    o_win = window_attention(q.reshape(b, nwb, WIN_BLOCK, N_KV, Q_PER_KV, HEAD_DIM),
                             kv_band, q_pos, k_pos).reshape(q.shape)
    return combine_branches(gates, o_cmp, o_sel, o_win)

def nsa_sample(q, cmp_kv, sel_kv, win_kv, gates, pos, cache_cmp, cache_sel, win_state, page_table, cmp_w):
    db, ds = q.shape[:2]
    past = PAST_LEN
    past_cmp = cache_cmp[page_table].reshape(db, past, N_KV, 2, HEAD_DIM)
    k_p, v_p = compress_blocks(past_cmp, *cmp_w)
    k_n, v_n = compress_blocks(cmp_kv[:, :(ds // CMP_BLOCK) * CMP_BLOCK], *cmp_w)
    k_c = jnp.concatenate([k_p, k_n], axis=1)
    v_c = jnp.concatenate([v_p, v_n], axis=1)
    o_cmp, imp = compressed_attention(q, k_c, v_c, pos)
    idx, valid = select_blocks(imp, pos)
    rows, vrows = block_rows(idx, valid)
    bi = jnp.arange(db)[:, None, None, None]
    gi = jnp.arange(N_KV)[None, None, :, None]
    r_past = jnp.minimum(rows, past - 1)
    phys = page_table[bi, r_past // PAGE_SIZE]
    kv_past = cache_sel[phys, r_past % PAGE_SIZE, gi]
    kv_new = sel_kv[bi, jnp.clip(rows - past, 0, ds - 1), gi]
    kv_g = jnp.where((rows < past)[..., None, None], kv_past, kv_new)
    own_mask = (pos[:, None] >= pos[None, :]) & (pos[:, None] // SEL_BLOCK == pos[None, :] // SEL_BLOCK)
    o_sel = selected_attention(q, kv_g, vrows, sel_kv, own_mask)
    kv_w = jnp.concatenate([win_state, win_kv], axis=1)
    win_rows = win_state.shape[1]
    k_pos = past - win_rows + jnp.arange(win_rows + ds)
    o_win = window_attention(q, kv_w, pos, k_pos)
    return combine_branches(gates, o_cmp, o_sel, o_win), kv_w[:, ds:]

def hier_moe(h, w_rg, w_re, w_g, w_u, w_d):
    n, d = h.shape
    lg = (h @ w_rg).astype(jnp.float32)
    p_grp = jax.nn.softmax(lg, axis=-1)
    grp = jnp.argmax(lg, axis=-1)
    p_top = jnp.take_along_axis(p_grp, grp[:, None], axis=1)[:, 0]
    le = (h @ w_re).astype(jnp.float32).reshape(n, N_GROUPS, EXPERTS_PER_GROUP)
    le_g = jnp.take_along_axis(le, grp[:, None, None], axis=1)[:, 0]
    top_w, top_i = lax.top_k(jax.nn.softmax(le_g, axis=-1), TOP_K)
    top_w = top_w / jnp.sum(top_w, axis=-1, keepdims=True) * p_top[:, None]
    expert = grp[:, None] * EXPERTS_PER_GROUP + top_i
    a = n * TOP_K
    flat_e = expert.reshape(a)
    flat_t = jnp.repeat(jnp.arange(n), TOP_K)
    flat_w = top_w.reshape(a)
    order = jnp.argsort(flat_e)
    se, st, sw = flat_e[order], flat_t[order], flat_w[order]
    counts = jnp.zeros((N_EXPERTS,), jnp.int32).at[flat_e].add(1)
    starts = jnp.cumsum(counts) - counts
    padded = (counts + MOE_CHUNK - 1) // MOE_CHUNK * MOE_CHUNK
    pend = jnp.cumsum(padded)
    dest = (pend - padded)[se] + (jnp.arange(a) - starts[se])
    n_chunks = -(-a // MOE_CHUNK) + N_EXPERTS
    slot_tok = jnp.full((n_chunks * MOE_CHUNK,), n, jnp.int32).at[dest].set(st)
    slot_w = jnp.zeros((n_chunks * MOE_CHUNK,), jnp.float32).at[dest].set(sw)
    chunk_e = jnp.clip(jnp.searchsorted(pend, jnp.arange(n_chunks) * MOE_CHUNK, side='right'), 0, N_EXPERTS - 1)
    xs = jnp.concatenate([h, jnp.zeros((1, d), h.dtype)], axis=0)[slot_tok].reshape(n_chunks, MOE_CHUNK, d)

    def expert_chunk(args):
        xc, e = args
        return (jax.nn.silu(xc @ w_g[e]) * (xc @ w_u[e])) @ w_d[e]

    ys = lax.map(expert_chunk, (xs, chunk_e)).reshape(n_chunks * MOE_CHUNK, d)
    out = jax.ops.segment_sum(ys.astype(jnp.float32) * slot_w[:, None], slot_tok, num_segments=n + 1)[:n]
    return out.astype(h.dtype)

def merge_and_ffn(x, conv_out, att_out, out_norm_conv, out_norm_att, w_out, ln2, w_rg, w_re, w_g, w_u, w_d):
    mix = jnp.concatenate([rmsnorm(conv_out, out_norm_conv), rmsnorm(att_out, out_norm_att)], axis=-1) @ w_out
    x = x + mix
    b, t, d = x.shape
    return x + hier_moe(rmsnorm(x, ln2).reshape(b * t, d), w_rg, w_re, w_g, w_u, w_d).reshape(b, t, d)

def setup_inputs(seed: int = 0) -> dict:
    key = jax.random.key(seed)
    ks = jax.random.split(key, 32)
    f32 = jnp.float32
    n_pages = PAST_LEN // PAGE_SIZE
    n_used = DEC_BATCH * n_pages
    n_phys = (5 * n_used + 3) // 4
    win_rows = min(WINDOW, PAST_LEN)

    def nrm(k, shape, scale):
        return jax.random.normal(k, shape, f32) * scale

    def gain(k, shape):
        return 1.0 + 0.01 * jax.random.normal(k, shape, f32)

    page_table = jax.random.permutation(ks[6], n_phys)[:n_used].reshape(DEC_BATCH, n_pages).astype(jnp.int32)
    return {
        'x_prompt': nrm(ks[0], (BATCH, SEQ, D_MODEL), 1.0),
        'x_sample': nrm(ks[1], (DEC_BATCH, DEC_SEQ, D_MODEL), 1.0),
        'cache_cmp_kv': nrm(ks[2], (DEPTH, n_phys, PAGE_SIZE, N_KV, 2, HEAD_DIM), 1.0),
        'cache_sel_kv': nrm(ks[3], (DEPTH, n_phys, PAGE_SIZE, N_KV, 2, HEAD_DIM), 1.0),
        'state_win_kv': nrm(ks[4], (DEPTH, DEC_BATCH, win_rows, N_KV, 2, HEAD_DIM), 1.0),
        'state_conv': nrm(ks[5], (DEPTH, DEC_BATCH, CONV_W - 1, CONV_CH), 0.5),
        'page_table': page_table,
        'ln1': gain(ks[7], (DEPTH, D_MODEL)),
        'w_in': nrm(ks[8], (DEPTH, D_MODEL, D_IN), D_MODEL ** -0.5),
        'conv_dw_w': nrm(ks[9], (DEPTH, CONV_W, CONV_CH), CONV_W ** -0.5),
        'conv_dw_b': nrm(ks[10], (DEPTH, CONV_CH), 0.01),
        'conv_ln_g': gain(ks[11], (DEPTH, CONV_CH)),
        'conv_ln_b': nrm(ks[12], (DEPTH, CONV_CH), 0.01),
        'cmp_pos_emb': nrm(ks[13], (DEPTH, CMP_BLOCK, 2, HEAD_DIM), 0.1),
        'w_cmp_k1': nrm(ks[14], (DEPTH, CMP_BLOCK, HEAD_DIM, CMP_HID), (CMP_BLOCK * HEAD_DIM) ** -0.5),
        'w_cmp_k2': nrm(ks[15], (DEPTH, CMP_HID, HEAD_DIM), CMP_HID ** -0.5),
        'w_cmp_v1': nrm(ks[16], (DEPTH, CMP_BLOCK, HEAD_DIM, CMP_HID), (CMP_BLOCK * HEAD_DIM) ** -0.5),
        'w_cmp_v2': nrm(ks[17], (DEPTH, CMP_HID, HEAD_DIM), CMP_HID ** -0.5),
        'out_norm_conv': gain(ks[18], (DEPTH, CONV_CH)),
        'out_norm_att': gain(ks[19], (DEPTH, N_HEADS * HEAD_DIM)),
        'w_out': nrm(ks[20], (DEPTH, D_MIX, D_MODEL), D_MIX ** -0.5),
        'ln2': gain(ks[21], (DEPTH, D_MODEL)),
        'w_router_group': nrm(ks[22], (DEPTH, D_MODEL, N_GROUPS), D_MODEL ** -0.5),
        'w_router_expert': nrm(ks[23], (DEPTH, D_MODEL, N_EXPERTS), D_MODEL ** -0.5),
        'w_exp_gate': nrm(ks[24], (DEPTH, N_EXPERTS, D_MODEL, D_EXPERT), D_MODEL ** -0.5),
        'w_exp_up': nrm(ks[25], (DEPTH, N_EXPERTS, D_MODEL, D_EXPERT), D_MODEL ** -0.5),
        'w_exp_down': nrm(ks[26], (DEPTH, N_EXPERTS, D_EXPERT, D_MODEL), D_EXPERT ** -0.5),
        'ln_final': gain(ks[27], (D_MODEL,)),
    }

def reference(x_prompt, x_sample, cache_cmp_kv, cache_sel_kv, state_win_kv, state_conv, page_table,
              ln1, w_in, conv_dw_w, conv_dw_b, conv_ln_g, conv_ln_b, cmp_pos_emb,
              w_cmp_k1, w_cmp_k2, w_cmp_v1, w_cmp_v2, out_norm_conv, out_norm_att, w_out, ln2,
              w_router_group, w_router_expert, w_exp_gate, w_exp_up, w_exp_down, ln_final):
    xp, xs = x_prompt, x_sample
    t_p = xp.shape[1]
    pos_p = jnp.arange(t_p)
    pos_s = PAST_LEN + jnp.arange(xs.shape[1])
    p_cmp, p_sel, p_win, p_conv = [], [], [], []
    s_cmp, s_sel, s_win, s_conv = [], [], [], []
    for l in range(DEPTH):
        cmp_w = (cmp_pos_emb[l], w_cmp_k1[l], w_cmp_k2[l], w_cmp_v1[l], w_cmp_v2[l])
        conv_w = (conv_dw_w[l], conv_dw_b[l], conv_ln_g[l], conv_ln_b[l])
        ffn_w = (out_norm_conv[l], out_norm_att[l], w_out[l], ln2[l], w_router_group[l],
                 w_router_expert[l], w_exp_gate[l], w_exp_up[l], w_exp_down[l])
        a, q, ckv, skv, wkv, g = mix_inputs(xp, pos_p, ln1[l], w_in[l])
        conv_out = conv_module(jnp.pad(a, ((0, 0), (CONV_W - 1, 0), (0, 0))), *conv_w)
        att = nsa_prompt(q, ckv, skv, wkv, g, pos_p, cmp_w)
        xp = merge_and_ffn(xp, conv_out, att, *ffn_w)
        p_cmp.append(ckv)
        p_sel.append(skv)
        p_win.append(wkv[:, t_p - min(WINDOW, t_p):])
        p_conv.append(a[:, t_p - (CONV_W - 1):])
        a, q, ckv, skv, wkv, g = mix_inputs(xs, pos_s, ln1[l], w_in[l])
        a_ext = jnp.concatenate([state_conv[l], a], axis=1)
        conv_out = conv_module(a_ext, *conv_w)
        att, new_win = nsa_sample(q, ckv, skv, wkv, g, pos_s, cache_cmp_kv[l], cache_sel_kv[l],
                                  state_win_kv[l], page_table, cmp_w)
        xs = merge_and_ffn(xs, conv_out, att, *ffn_w)
        s_cmp.append(ckv)
        s_sel.append(skv)
        s_win.append(new_win)
        s_conv.append(a_ext[:, a.shape[1]:])
    y_prompt = rmsnorm(xp, ln_final)
    y_sample = rmsnorm(xs, ln_final)
    return (y_prompt, y_sample,
            jnp.stack(p_cmp), jnp.stack(s_cmp),
            jnp.stack(p_sel), jnp.stack(s_sel),
            jnp.stack(p_win), jnp.stack(s_win),
            jnp.stack(p_conv), jnp.stack(s_conv))


_drawn_inputs = setup_inputs


def setup_inputs(seed=0):
    import zlib

    import numpy as np

    out = dict(_drawn_inputs(seed))
    spreads = {}
    factors = {'ln1': 4.018,
     'conv_ln_g': 2.918,
     'conv_ln_b': 2.951,
     'out_norm_conv': 2.972,
     'out_norm_att': 5.304,
     'ln2': 2.861,
     'ln_final': 6.202}
    for name, (base, spread) in spreads.items():
        noise = np.random.default_rng([zlib.crc32(name.encode()), seed]).standard_normal(out[name].shape)
        drawn = base * np.exp(spread * noise) if base else spread * noise
        out[name] = __import__('jax').numpy.asarray(drawn.astype(out[name].dtype))
    for name, factor in factors.items():
        out[name] = (out[name] * factor).astype(out[name].dtype)
    return out
```

```python
from contextlib import ExitStack

import concourse.bass as bass
import numpy as np
from concourse import mybir

ALU = mybir.AluOpType
ACT = mybir.ActivationFunctionType
AX = mybir.AxisListType
F32 = mybir.dt.float32
I32 = mybir.dt.int32
U32 = mybir.dt.uint32

P = 128
D = 1024
SEQ = 1024
NB, NS = 8, 4
PAST = 2048
PAGE = 128
CH, TAPS = 512, 31
KV, R, HD = 2, 4, 64
HALF_ROT = 8
COLS_TM = 512 + 768 + 24
KT_ = D // P
TILES = 9
NQ = 8
TOKENS = SEQ + NB * NS
SCALE = HD ** -0.5
NEG = -1e30
CMP = 64
PBLK = SEQ // CMP
SBLK = PAST // CMP
NSEL = 16
PAGES = PAST // PAGE
HALF = 4 * PAGES
EXPERTS, GROUPS, DE = 32, 4, 512
CHUNKS = (2 * TOKENS) // P + EXPERTS
RMS_EPS, LN_EPS = 1e-6, 1e-5


def rows(t):
    return P if t < NQ else NB * NS


def const_table():
    parts, at = [], {}

    def put(name, a):
        full = np.zeros((P, a.shape[1]), np.float32)
        full[:a.shape[0]] = a
        at[name] = (sum(x.shape[1] for x in parts), a.shape[1])
        parts.append(full)

    p = np.arange(P)
    put("ident", np.eye(P))
    put("causal", np.where(p[None, :] <= p[:, None], 0.0, NEG))
    put("low", np.where(p[None, :] > p[:, None], 0.0, NEG))
    pos = np.concatenate([np.arange(SEQ), np.resize(PAST + np.arange(NS), P)]).astype(np.float32)
    inv = np.float32(500000.0) ** (-np.arange(HALF_ROT, dtype=np.float32) / np.float32(HALF_ROT))
    ang = (pos[:, None] * inv.astype(np.float32)).astype(np.float32).reshape(TILES, P, HALF_ROT)
    rope = np.concatenate([np.cos(ang), np.sin(ang)], axis=2)
    put("rope", rope.transpose(1, 0, 2).reshape(P, TILES * 16))
    q = np.arange(SEQ).reshape(NQ, P).T
    valid = ((np.arange(PBLK) + 1) * CMP - 1)[None, None, :] <= q[:, :, None]
    put("cmp_ok", valid.reshape(P, NQ * PBLK))
    put("eps", np.tile(np.array([[RMS_EPS, LN_EPS]]), (P, 1)))
    b4, g, r, t = p // 32, p // 16 % 2, p // 4 % 4, p % 4
    own = np.full((P, 2, NB, NS), NEG)
    for half in range(2):
        for i in range(P):
            own[i, half, 4 * half + b4[i], :t[i] + 1] = 0.0
    put("own", own.reshape(P, 64))
    put("win", np.where(np.arange(512)[None, :] > t[:, None], 0.0, NEG))
    put("same_query", (b4[:, None] == b4) & (g[:, None] == g) & (t[:, None] == t))
    pick = np.zeros((NB * NS, 2, P))
    for half in range(2):
        pick[(4 * half + b4) * NS + t, half, p] = 1.0
    put("pick_token", pick.reshape(NB * NS, 2 * P))
    put("own_head", np.arange(8)[None, :] == (g * R + r)[:, None])
    put("rep_block", np.arange(PBLK)[:, None] == (p % PBLK)[None, :])
    put("before", p[:, None] < p[None, :])
    put("ones", np.ones((P, P)))
    put("down4", np.tile(GROUPS - np.arange(GROUPS), (P, 1)))
    put("down32", np.tile(EXPERTS - np.arange(EXPERTS), (P, 1)))
    put("token", (np.arange(TILES)[None, :] * P + p[:, None]).astype(np.float32))
    put("steps", np.tile(128.0 * np.arange(9), (P, 1)))
    put("chunk", np.tile(np.arange(CHUNKS + 1, dtype=np.float32), (P, 1)))
    small = sum(x.shape[1] for x in parts)
    put("lane", np.tile(np.arange(P, dtype=np.float32), (P, 1)))
    n = np.arange(SBLK)
    put("earlier", np.tile((n[None, :] < n[:, None]).reshape(1, -1), (P, 1)))
    put("own_block", (p // PBLK)[:, None] == (np.arange(512) // HD)[None, :])
    return np.concatenate(parts, axis=1), at, small


class Chain:

    def __init__(self, eng, sem, count):
        self.eng, self.sem, self.count = eng, sem, count

    def __call__(self, ins):
        self.count[0] += 1
        ins.then_inc(self.sem, 1)
        self.eng.wait_ge(self.sem, self.count[0])


def build(nc, a):
    _, const_at, const_small = const_table()
    with ExitStack() as ctx:
        arena = ctx.enter_context(nc.sbuf_tensor("arena", [P, 52900], F32))
        ints = ctx.enter_context(nc.sbuf_tensor("ints", [P, 72], I32))
        row_ints = ctx.enter_context(nc.sbuf_tensor("row_ints", [1, 64], I32))
        ps = ctx.enter_context(nc.psum_tensor("ps", [P, 8, 512], F32))
        scratch_h = nc.dram_tensor("scratch_h", [TOKENS, D], F32, kind="Internal").ap()
        scratch_y = nc.dram_tensor("scratch_y", [CHUNKS * P, D], F32, kind="Internal").ap()
        scratch_first = nc.dram_tensor("scratch_first", [2, 16], F32, kind="Internal").ap()
        semaphores = {}

        def sem(name):
            if name not in semaphores:
                semaphores[name] = nc.alloc_semaphore(name)
            return semaphores[name]

        def reuse_semaphores():
            done = [semaphores.pop(name) for name in list(semaphores) if not name.endswith("_chain")]
            nc.clear_and_free_semaphores(done)
            with nc.Block():
                pass

        top = [0]

        def take(n):
            top[0] += n
            return top[0] - n

        def flat(off, n):
            return arena[:, off:off + n]

        CON = flat(take(const_small), const_small)
        gain = flat(take(2560), 2560)
        small = flat(take(640), 640)
        A2 = take(8448)
        A1 = take(18688)
        A3 = take(4656)
        A4 = take(5304)
        AQ = take(8192)
        AC = take(2000)

        def con(name, n=P):
            o, w = const_at[name]
            return CON[:n, o:o + w]

        ident = con("ident")
        used = [0]

        def stat(n):
            used[0] += n
            return small[:, used[0] - n:used[0]]

        gates = stat(TILES * 24).rearrange("p (t c) -> p t c", c=24)
        xT = flat(A2, 8448).rearrange("p (k n) -> p k n", k=KT_)
        w_tm = flat(A1, KT_ * COLS_TM).rearrange("p (k n) -> p k n", k=KT_)
        w_conv = flat(A1 + KT_ * COLS_TM, KT_ * D).rearrange("p (k n) -> p k n", k=KT_)
        acc = flat(A1 + KT_ * COLS_TM, 4 * TOKENS).rearrange("p (c n) -> p c n", c=4)
        xin = flat(A3, 2048).rearrange("p (s n) -> p s n", s=2)
        p_sb = flat(A3 + 2048, 2608).rearrange("p (s n) -> p s n", s=2)
        xn = flat(AQ, 2048).rearrange("p (s n) -> p s n", s=2)
        a_p = flat(A4, 4 * (SEQ + TAPS - 1)).rearrange("p (c n) -> p c n", c=4)
        a_s = flat(A4 + 4 * (SEQ + TAPS - 1), 4 * NB * 34).rearrange("p (c n b) -> p c n b", c=4, b=NB)
        qT = flat(AQ, 4096).rearrange("p (r n) -> p r n", r=R)
        kT = flat(AQ + 4096, 2048).rearrange("p (w n) -> p w n", w=2)
        vals = flat(AQ + 6144, 2048).rearrange("p (t w n) -> p t w n", t=NQ, w=2)
        kcT_s = flat(AC, 256)
        vc_s = flat(AC + 256, 1024).rearrange("p (b n) -> p b n", b=NB)
        vc_p = flat(AC + 1296, 128)
        q_diag = flat(AC + 1424, 256).rearrange("p (b n) -> p b n", b=NB)
        kT_new = flat(AC + 1680, 64).rearrange("p (w n) -> p w n", w=2)
        v_new = flat(AC + 1744, 256).rearrange("p (w n) -> p w n", w=2)
        pages = flat(A1, 18688).rearrange("p (s n) -> p s n", n=256)
        dw = stat(128).rearrange("p (c n) -> p c n", c=4)
        kcT_p = stat(2 * PBLK)
        ms, sd, rstd = stat(TILES), stat(TILES), stat(TILES)

        out = {k: v for k, v in a.items() if k.startswith("out")}
        x_rows = [a["x_prompt"][0, P * t:P * t + P, :] for t in range(NQ)]
        x_rows.append(a["x_sample"].rearrange("b s d -> (b s) d"))

        count = {k: [0] for k in ("dve", "act", "pool")}
        rope_tmp = flat(take(256), 256)
        NW = 352
        sig = flat(A3 + 2048, 2 * NW).rearrange("p (s n) -> p s n", s=2)
        with nc.Block() as block:
            @block.sync
            def _(sp):
                sp.dma_start(CON, a["consts"][:, 0:const_small]).then_inc(sem("const_in"), 16)
                sp.dma_start(gain[:, 0:D], a["ln1"].partition_broadcast(P)).then_inc(sem("ln1_in"), 16)
                for t in range(TILES):
                    if t >= 2:
                        sp.wait_ge(sem("xn_ready"), t - 1)
                    sp.dma_start(xin[:rows(t), t % 2, :], x_rows[t]).then_inc(sem(f"x_in{t % 2}"), 16)
                    if t == 1:
                        sp.dma_start(w_conv, a["w_in"].rearrange("(p k) n -> p k n", k=KT_)[:, :, 0:D])\
                          .then_inc(sem("w_conv_in"), 16)
                sp.dma_start(dw, a["dw"].rearrange("p (c n) -> p c n", c=4)).then_inc(sem("dw_in"), 16)
                sp.dma_start(a_s[:, :, 0:TAPS - 1, :],
                             a["state_conv_T"].rearrange("p (c n b) -> p c n b", c=4, b=NB)).then_inc(sem("dw_in"), 16)
                sp.dma_start(w_tm, a["w_in"].rearrange("(p k) n -> p k n", k=KT_)[:, :, D:D + COLS_TM])\
                  .then_inc(sem("w_tm_in"), 16)
                sp.dma_start(out["out9"][:, 0:TAPS - 1 - NS, :], a["state_conv"][:, NS:TAPS - 1, :])\
                  .then_inc(sem("state_out"), 16)
                sp.dma_start(out["out7"][:, 0:512 - NS, :], a["state_win"][:, NS:512, :])\
                  .then_inc(sem("state_out"), 16)
                sp.wait_ge(sem("state_out"), 32)
                sp.wait_ge(sem("w_tm_in"), 16)
                sp.wait_ge(sem("dw_in"), 32)

            @block.tensor
            def _(pe):
                pe.wait_ge(sem("const_in"), 16)
                for t in range(TILES):
                    n = rows(t)
                    pe.wait_ge(sem("xn_ready"), t + 1)
                    if t >= 2:
                        pe.wait_ge(sem("xT_act"), t - 1)
                        pe.wait_ge(sem("xT_dve"), t - 1)
                    xv = xn[:n, t % 2, :].rearrange("p (m k) -> p k m", k=KT_)
                    for k in range(KT_):
                        mm = pe.transpose(ps[:, 2 * (t % 2) + k // 4, (k % 4) * P:(k % 4) * P + n],
                                          xv[:, k, :], ident[:n, :n])
                    mm.then_inc(sem("x_turned"), 1)
                pe.wait_ge(sem("xT_act"), TILES)
                pe.wait_ge(sem("xT_dve"), TILES)
                pe.wait_ge(sem("w_conv_in"), 16)
                for u in range(12):
                    j, c = u // 4, u % 4
                    if u >= 2:
                        pe.wait_ge(sem("glu_done"), u - 1)
                    for half in range(2):
                        for k in range(KT_):
                            mm = pe.matmul(ps[:, 4 + 2 * (u % 2) + half, 0:NW],
                                           w_conv[:, k, half * CH + c * P:half * CH + c * P + P],
                                           xT[:, k, j * NW:(j + 1) * NW], start=(k == 0), stop=(k == KT_ - 1))
                    mm.then_inc(sem("conv_projected"), 1)
                pe.wait_ge(sem("w_tm_in"), 16)
                pe.wait_ge(sem("glu_done"), 12)

                def turn(t):
                    n = rows(t)
                    pe.wait_ge(sem("roped"), t + 1)
                    if t >= 1:
                        pe.wait_ge(sem("qk_copied"), t)
                        pe.wait_ge(sem("cmp_copied"), t)
                    s = p_sb[:n, t % 2, :]
                    for r in range(R):
                        pe.transpose(ps[:, 6, r * P:r * P + n], s[:, r * P:(r + 1) * P], ident[:n, :n])
                    for w in range(2):
                        o = 512 + 256 * (w + 1)
                        mm = pe.transpose(ps[:, 7, w * P:w * P + n], s[:, o:o + P], ident[:n, :n])
                    mm.then_inc(sem("qk_turned"), 1)
                    if t < NQ:
                        pe.wait_ge(sem("qk_copied"), t + 1)
                        pe.wait_ge(sem("doubled"), t + 1)
                        for o in range(0, 512, P):
                            mm = pe.transpose(ps[:, 6, o:o + P], xin[:, t % 2, o:o + P], ident)
                        mm.then_inc(sem("cmp_turned"), 1)

                for t in range(TILES):
                    n, b = rows(t), 3 * (t % 2)
                    if t >= 2:
                        pe.wait_ge(sem("tm_copied"), t - 1)
                    for o, w in ((0, 512), (512, 512), (1024, COLS_TM - 1024)):
                        for k in range(KT_):
                            mm = pe.matmul(ps[:n, b + o // 512, 0:w], xT[:, k, t * P:t * P + n],
                                           w_tm[:, k, o:o + w], start=(k == 0), stop=(k == KT_ - 1))
                    mm.then_inc(sem("tm_projected"), 1)
                    if t >= 1:
                        turn(t - 1)
                turn(TILES - 1)
                pe.wait_ge(sem("tm_copied"), TILES)
                for c in range(4):
                    pe.transpose(ps[:TAPS - 1, 0, c * P:(c + 1) * P], a_p[:, c, SEQ:SEQ + TAPS - 1], ident)
                for c in range(4):
                    mm = pe.transpose(ps[:NB * NS, 1, c * P:(c + 1) * P], a_s[:, c, TAPS - 1:, :], ident)
                mm.then_inc(sem("state_turned"), 1)

            @block.scalar
            def _(act):
                chain = Chain(act, sem("act_chain"), count["act"])
                act.wait_ge(sem("const_in"), 16)
                for t in range(TILES + 1):
                    if t < TILES:
                        n = rows(t)
                        act.wait_ge(sem(f"x_in{t % 2}"), 16 * (t // 2 + 1))
                        chain(act.activation(p_sb[:n, 1, 0:D], xin[:n, t % 2, :], ACT.Square, scale=1 / 32,
                                             accum_out=ms[:n, t:t + 1]))
                        act.activation(sd[:n, t:t + 1], ms[:n, t:t + 1], ACT.Sqrt,
                                       bias=con("eps")[:n, 0:1]).then_inc(sem("sd_ready"), 1)
                    if t >= 1:
                        n, b = rows(t - 1), 2 * ((t - 1) % 2)
                        act.wait_ge(sem("x_turned"), t)
                        act.activation(xT[:, 0:4, (t - 1) * P:(t - 1) * P + n],
                                       ps[:, b, :].rearrange("p (k m) -> p k m", k=4)[:, :, 0:n],
                                       ACT.Copy).then_inc(sem("xT_act"), 1)
                for u in range(12):
                    act.wait_ge(sem("conv_projected"), u + 1)
                    if u >= 2:
                        act.wait_ge(sem("glu_done"), u - 1)
                    act.activation(sig[:, u % 2, :], ps[:, 5 + 2 * (u % 2), 0:NW], ACT.Sigmoid)\
                       .then_inc(sem("sig_ready"), 1)
                act.wait_ge(sem("glu_done"), 12)

                def turn_copy(t):
                    n = rows(t)
                    act.wait_ge(sem("qk_turned"), t + 1)
                    if t < NQ:
                        act.activation(qT[:, :, t * P:t * P + P], ps[:, 6, :].rearrange("p (r m) -> p r m", r=R),
                                       ACT.Copy, scale=SCALE)
                        act.activation(kT[:, :, t * P:t * P + P],
                                       ps[:, 7, 0:2 * P].rearrange("p (w m) -> p w m", w=2),
                                       ACT.Copy).then_inc(sem("qk_copied"), 1)
                    else:
                        act.wait_ge(sem("diag_zero"), 1)
                        for g in range(KV):
                            src = ps[64 * g:64 * g + 64, 6, :].rearrange("p (r m) -> p r m", r=R)[:, :, 0:n]
                            act.activation(
                                q_diag[64 * g:64 * g + 64, :, 16 * g:16 * g + 16].rearrange(
                                    "p b (r s) -> p r b s", r=R),
                                src.rearrange("p r (b s) -> p r b s", s=NS), ACT.Copy, scale=SCALE)
                        act.activation(kT_new[:, :, :],
                                       ps[:, 7, 0:2 * P].rearrange("p (w m) -> p w m", w=2)[:, :, 0:n],
                                       ACT.Copy).then_inc(sem("qk_copied"), 1)

                for t in range(TILES):
                    n, b = rows(t), 3 * (t % 2)
                    act.wait_ge(sem("tm_projected"), t + 1)
                    if t >= 2:
                        act.wait_ge(sem(f"rows_out{t % 2}"), 32 * (t // 2))
                        if t >= 6:
                            act.wait_ge(sem(f"win_out{t % 2}"), 16 * (t // 2 - 2))
                        act.wait_ge(sem("cmp_turned"), t - 1)
                        act.wait_ge(sem("v_copied"), t - 1)
                    act.activation(p_sb[:n, t % 2, 0:512], ps[:n, b, :], ACT.Copy)
                    act.activation(p_sb[:n, t % 2, 512:1024], ps[:n, b + 1, :], ACT.Copy)
                    act.activation(p_sb[:n, t % 2, 1024:1280], ps[:n, b + 2, 0:256], ACT.Copy)
                    act.activation(gates[:n, t, :], ps[:n, b + 2, 256:280], ACT.Sigmoid)\
                       .then_inc(sem("tm_copied"), 1)
                    if t >= 1:
                        turn_copy(t - 1)
                turn_copy(TILES - 1)
                act.wait_ge(sem("state_turned"), 1)
                act.wait_ge(sem("qk_turned"), TILES)
                act.activation(xin[:TAPS - 1, 0, 0:512], ps[:TAPS - 1, 0, :], ACT.Copy)
                act.activation(xin[:NB * NS, 1, 0:512], ps[:NB * NS, 1, :], ACT.Copy)\
                   .then_inc(sem("state_ready"), 1)

            def keep_as_page(dve, t):
                dve.wait_ge(sem("cmp_turned"), t + 1)
                if t == 0:
                    dve.wait_ge(sem("glu_done"), 12)
                for v in range(2):
                    for par in range(2):
                        o = pages[64 * par:64 * par + 64, HALF + t, 128 * v:128 * v + 128].rearrange(
                            "p (l b g) -> p g b l", b=2, g=KV)
                        for g in range(KV):
                            i = ps[64 * par:64 * par + 64, 6, (2 * v + g) * P:(2 * v + g + 1) * P].rearrange(
                                "p (b l q) -> p q b l", b=2, q=2)[:, par]
                            ins = dve.tensor_copy(o[:, g], i)
                ins.then_inc(sem("cmp_copied"), 1)

            @block.vector
            def _(dve):
                chain = Chain(dve, sem("dve_chain"), count["dve"])
                dve.wait_ge(sem("ln1_in"), 16)
                for t in range(TILES + 1):
                    if t < TILES:
                        n = rows(t)
                        dve.wait_ge(sem("sd_ready"), t + 1)
                        chain(dve.reciprocal(rstd[:n, t:t + 1], sd[:n, t:t + 1]))
                        if t >= 2:
                            dve.wait_ge(sem("x_turned"), t - 1)
                        dve.scalar_tensor_tensor(xn[:n, t % 2, :], xin[:n, t % 2, :], rstd[:n, t:t + 1],
                                                 gain[:n, 0:D], ALU.mult, ALU.mult).then_inc(sem("xn_ready"), 1)
                    if t >= 1:
                        n, b = rows(t - 1), 2 * ((t - 1) % 2) + 1
                        dve.wait_ge(sem("x_turned"), t)
                        dve.tensor_copy(xT[:, 4:8, (t - 1) * P:(t - 1) * P + n],
                                        ps[:, b, :].rearrange("p (k m) -> p k m", k=4)[:, :, 0:n])\
                           .then_inc(sem("xT_dve"), 1)
                dve.wait_ge(sem("dw_in"), 32)
                for u in range(12):
                    j, c = u // 4, u % 4
                    dve.wait_ge(sem("sig_ready"), u + 1)
                    m = min(SEQ - j * NW, NW)
                    gl = dve.tensor_tensor(a_p[:, c, TAPS - 1 + j * NW:TAPS - 1 + j * NW + m],
                                           ps[:, 4 + 2 * (u % 2), 0:m], sig[:, u % 2, 0:m], ALU.mult)
                    if m < NW:
                        gl = dve.tensor_tensor(a_s[:, c, TAPS - 1:, :],
                                               ps[:, 4 + 2 * (u % 2), m:NW].rearrange("p (b s) -> p s b", s=NS),
                                               sig[:, u % 2, m:NW].rearrange("p (b s) -> p s b", s=NS), ALU.mult)
                    gl.then_inc(sem("glu_done"), 1)
                dve.wait_ge(sem("pad_zero"), 1)
                dve.wait_ge(sem("glu_done"), 12)

                def tap(c, j):
                    views = ((acc[:, c, 0:SEQ], a_p[:, c, j:j + SEQ]),
                             (acc[:, c, SEQ:TOKENS].rearrange("p (b s) -> p s b", s=NS), a_s[:, c, j:j + NS, :]))
                    for o, i in views:
                        if j == 0:
                            ins = dve.tensor_scalar(o, i, dw[:, c, 0:1], dw[:, c, TAPS:TAPS + 1], ALU.mult, ALU.add)
                        else:
                            ins = dve.scalar_tensor_tensor(o, i, dw[:, c, j:j + 1], o, ALU.mult, ALU.add)
                        ins.then_inc(sem("tapped"), 1)
                    tapped[0] += 2

                tapped = [0]
                taps = [(c, j) for j in range(TAPS) for c in range(4)]
                for t in range(TILES):
                    n = rows(t)
                    dve.wait_ge(sem("tm_copied"), t + 1)
                    cs = con("rope")[:n, 16 * t:16 * t + 16]
                    heads = ((p_sb[:n, t % 2, 0:512].rearrange("p (h d) -> p h d", d=HD), 8),
                             (p_sb[:n, t % 2, 512:1280].rearrange("p (w v d) -> p v w d", w=3, v=2)[:, 0], 6))
                    for s, h in heads:
                        if h == 6:
                            s = s.rearrange("p w (g d) -> p w g d", g=KV)
                            x1, x2 = s[:, :, :, 0:8], s[:, :, :, 8:16]
                            cos = cs[:, 0:8].unsqueeze(1).unsqueeze(1).to_broadcast([n, 3, KV, 8])
                            sin = cs[:, 8:16].unsqueeze(1).unsqueeze(1).to_broadcast([n, 3, KV, 8])
                            tmp = [rope_tmp[:n, 64 * q:64 * q + 48].rearrange("p (w g d) -> p w g d", w=3, g=KV)
                                   for q in range(4)]
                        else:
                            x1, x2 = s[:, :, 0:8], s[:, :, 8:16]
                            cos = cs[:, 0:8].unsqueeze(1).to_broadcast([n, h, 8])
                            sin = cs[:, 8:16].unsqueeze(1).to_broadcast([n, h, 8])
                            tmp = [rope_tmp[:n, 64 * q:64 * q + 64].rearrange("p (h d) -> p h d", d=8)
                                   for q in range(4)]
                        dve.tensor_tensor(tmp[0], x1, cos, ALU.mult)
                        dve.tensor_tensor(tmp[1], x2, sin, ALU.mult)
                        dve.tensor_tensor(tmp[2], x1, sin, ALU.mult)
                        chain(dve.tensor_tensor(tmp[3], x2, cos, ALU.mult))
                        dve.tensor_tensor(x1, tmp[0], tmp[1], ALU.subtract)
                        ins = dve.tensor_tensor(x2, tmp[2], tmp[3], ALU.add)
                        if h == 8:
                            chain(ins)
                        else:
                            ins.then_inc(sem("roped"), 1)
                    dve.wait_ge(sem("roped"), t + 1)
                    if t >= 1:
                        keep_as_page(dve, t - 1)
                    for c, j in taps[len(taps) * t // TILES:len(taps) * (t + 1) // TILES]:
                        if tapped[0] >= 8:
                            dve.wait_ge(sem("tapped"), tapped[0] - 6)
                        tap(c, j)
                dve.wait_ge(sem("tapped"), tapped[0])

            @block.gpsimd
            def _(pool):
                pool.memset(a_p[:, :, 0:TAPS - 1], 0.0).then_inc(sem("pad_zero"), 1)
                pool.memset(q_diag, 0.0).then_inc(sem("diag_zero"), 1)
                for t in range(TILES):
                    n = rows(t)
                    pool.wait_ge(sem("roped"), t + 1)
                    s = p_sb[:n, t % 2, 512:1280].rearrange("p (w n) -> p w n", w=3)
                    vv = s.rearrange("p w (v n) -> p w v n", v=2)
                    if t < NQ:
                        if t >= 2:
                            pool.wait_ge(sem("cmp_turned"), t - 1)
                        dup = xin[:, t % 2, 0:512].rearrange("p (h q d) -> p h q d", q=2, d=HD)
                        for q in range(2):
                            ins = pool.tensor_copy(dup[:, :, q], s[:, 0, :].rearrange("p (h d) -> p h d", d=HD))
                        ins.then_inc(sem("doubled"), 1)
                        pool.tensor_copy(vals[:n, t, :, :], vv[:, 1:3, 1])\
                            .then_inc(sem("v_copied"), 1)
                        dst = [out["out2"][P * t:P * t + P], out["out4"][P * t:P * t + P],
                               out["out6"][P * (t - 4):P * (t - 3)] if t >= 4 else None]
                    else:
                        pool.tensor_copy(v_new[:n, :, :], vv[:, 1:3, 1])\
                            .then_inc(sem("v_copied"), 1)
                        dst = [out["out3"], out["out5"], out["out7"][:, 512 - NS:512, :]]
                    for w in range(3):
                        if dst[w] is not None:
                            pool.dma_start(dst[w], s[:, w, :])\
                                .then_inc(sem(f"win_out{t % 2}" if w == 2 else f"rows_out{t % 2}"), 16)
                pool.wait_ge(sem("state_ready"), 1)
                pool.dma_start(out["out8"], xin[:TAPS - 1, 0, 0:512]).then_inc(sem("conv_out"), 16)
                for s in range(NS):
                    pool.dma_start(out["out9"][:, TAPS - 1 - NS + s, :], xin[NB * s:NB * (s + 1), 1, 0:512])\
                        .then_inc(sem("conv_out"), 16)
                pool.wait_ge(sem("conv_out"), 16 * (1 + NS))
                pool.wait_ge(sem("rows_out0"), 32 * 5)
                pool.wait_ge(sem("rows_out1"), 32 * 4)
                pool.wait_ge(sem("win_out0"), 16 * 3)
                pool.wait_ge(sem("win_out1"), 16 * 2)

        conv = flat(A2, TILES * CH).rearrange("p (t n) -> p t n", n=CH)
        A2b = A2 + TILES * CH
        cg, cb, cn = gain[:, D:D + CH], gain[:, D + CH:D + 2 * CH], gain[:, D + 2 * CH:D + 3 * CH]
        bn = flat(A2b + 1500, TILES * 6).rearrange("p (t n) -> p t n", n=6)
        mv = flat(A2b + 1564, TILES * 2).rearrange("p (t n) -> p t n", n=2)
        csd, crs, css = (flat(A2b + 1596 + 16 * q, TILES) for q in range(3))
        junk = flat(A2b + 1700, CH)
        w_cmp1 = flat(A3, 8192).rearrange("p (v l h) -> p v l h", v=2, l=CMP // 2)
        sil = flat(A2b, 2 * 544).rearrange("p (v n) -> p v n", v=2)
        w_cmp2 = flat(A2b + 1088, 320)
        cmp_bias = flat(A2b + 1408, 2)

        def load_pages(eng, cache, first, b, event, part=slice(0, 256)):
            with eng.Fori(0, PAGES // 4) as s:
                places = [eng.value_load(page_row[0:1, bass.ds(s * 4 + (first + q), 1)],
                                         min_val=0, max_val=cache.shape[0] - 1) for q in range(4)]
                for q, place in enumerate(places):
                    eng.dma_start(pages_flat[:, bass.ds(s * 1024 + ((b * PAGES + q) * 256 + part.start),
                                                        part.stop - part.start)],
                                  cache[bass.ds(place, 1)].rearrange("a p n -> (a p) n")[:, part])\
                       .then_inc(sem(f"{event}{b}"), 16)

        page_row = ctx.enter_context(nc.sbuf_tensor("page_row", [1, NB * PAGES], I32))[:]
        pages_flat = flat(A1, 18688)
        with nc.Block() as block:
            @block.sync
            def _(sp):
                sp.dma_start(page_row, a["page_table"]).then_inc(sem("page_table_in"), 16)
                sp.dma_start(cg, a["conv_g"].partition_broadcast(P)).then_inc(sem("conv_gain_in"), 16)
                sp.dma_start(cb, a["conv_b"].partition_broadcast(P)).then_inc(sem("conv_gain_in"), 16)
                sp.dma_start(cn, a["norm_conv"].partition_broadcast(P)).then_inc(sem("conv_gain_in"), 16)
                sp.dma_start(w_cmp1, a["w_cmp1"].rearrange("p (v l h) -> p v l h", v=2, l=CMP // 2))\
                  .then_inc(sem("w_cmp_in"), 16)
                sp.dma_start(w_cmp2, a["w_cmp2"]).then_inc(sem("w_cmp_in"), 16)
                sp.dma_start(pages[:, HALF + NQ, :], a["pos_emb"]).then_inc(sem("w_cmp_in"), 16)
                sp.wait_ge(sem("page_table_in"), 16)
                for q in range(4):
                    if q == 1:
                        sp.wait_ge(sem("conv_turned"), TILES)
                    if q >= 2:
                        sp.wait_ge(sem("compressed"), q - 1)
                    load_pages(sp, a["cache_cmp"], 2 * q * PAGES, 2 * (q % 2), "cmp_page")
                    load_pages(sp, a["cache_cmp"], (2 * q + 1) * PAGES, 2 * (q % 2) + 1, "cmp_page")

            @block.tensor
            def _(pe):
                for t in range(TILES):
                    n = rows(t)
                    if t >= 4:
                        pe.wait_ge(sem("conv_moved"), t - 3)
                    for c in range(4):
                        mm = pe.transpose(ps[:n, t % 4, c * P:(c + 1) * P], acc[:, c, t * P:t * P + n], ident)
                    mm.then_inc(sem("conv_turned"), 1)
                pe.wait_ge(sem("w_cmp_in"), 48)
                for q in range(4):
                    n, at = (2 * PAGES + (NQ + 1 if q == 1 else 0)) * 4, 2 * PAGES * (q % 2)
                    for b in range(2):
                        pe.wait_ge(sem(f"cmp_page{2 * (q % 2) + b}"), 16 * PAGES * (q // 2 + 1))
                    for v in range(2):
                        for l in range(CMP // 2):
                            mm = pe.matmul(ps[:, 4 + q, 256 * v:256 * v + n], w_cmp1[:, v, l, :],
                                           pages[:, at:at + n // 4, 128 * v + 4 * l:128 * v + 4 * l + 4],
                                           start=(l == 0), stop=(l == CMP // 2 - 1))
                    mm.then_inc(sem("compressed"), 1)
                pe.wait_ge(sem("swished_blocks"), 1)
                pe.wait_ge(sem("conv_moved"), TILES)
                for bank, o, m in ((0, 0, 2 * P), (1, 512, PBLK)):
                    for g in range(KV):
                        mm = pe.matmul(ps[:, bank, 0:m], w_cmp2[:, 128 * g:128 * g + 128],
                                       sil[:, 0, o + g:o + 2 * m:2], start=(g == 0), stop=(g == 1))
                for b in range(NB):
                    for g in range(KV):
                        o = 64 * b + g
                        mm = pe.matmul(ps[:SBLK, 2 + b // 4, 128 * (b % 4) + 64 * g:128 * (b % 4) + 64 * g + 64],
                                       sil[:, 1, o:o + 63:2], w_cmp2[:, 256:320], start=True, stop=True)
                for g in range(KV):
                    mm = pe.matmul(ps[:PBLK, 1, P + 64 * g:P + 64 * g + 64], sil[:, 1, 512 + g:512 + g + 31:2],
                                   w_cmp2[:, 256:320], start=True, stop=True)
                mm.then_inc(sem("blocks_made"), 1)

            @block.scalar
            def _(act):
                chain = Chain(act, sem("act_chain"), count["act"])
                for t in range(TILES):
                    n = rows(t)
                    act.wait_ge(sem("conv_turned"), t + 1)
                    act.activation(conv[:n, t, :], ps[:n, t % 4, :], ACT.Copy).then_inc(sem("conv_moved"), 1)
                act.wait_ge(sem("conv_moments"), TILES)
                act.activation(csd, mv[:, :, 1], ACT.Sqrt, bias=con("eps")[:, 1:2]).then_inc(sem("conv_sd"), 1)
                for t in range(TILES):
                    n = rows(t)
                    act.wait_ge(sem("conv_shifted"), t + 1)
                    act.activation(conv[:n, t, :], conv[:n, t, :], ACT.Silu).then_inc(sem("swished"), 1)
                act.wait_ge(sem("swished"), TILES)
                act.wait_ge(sem("css_set"), 1)
                for t in range(TILES):
                    n = rows(t)
                    ins = act.activation(junk[:n, :], conv[:n, t, :], ACT.Square, scale=CH ** -0.5,
                                         accum_out=css[:n, t:t + 1])
                    chain(ins)
                act.activation(csd, css, ACT.Sqrt, bias=con("eps")[:, 0:1]).then_inc(sem("conv_sd"), 1)
                act.wait_ge(sem("compressed"), 4)
                act.wait_ge(sem("bias_ready"), 1)
                for v in range(2):
                    for q in range(4):
                        act.activation(sil[:, v, 128 * q:128 * q + 128], ps[:, 4 + q, 256 * v:256 * v + 128],
                                       ACT.Silu, bias=cmp_bias[:, v:v + 1])
                    ins = act.activation(sil[:, v, 512:544], ps[:, 5, 256 * v + 128:256 * v + 160], ACT.Silu,
                                         bias=cmp_bias[:, v:v + 1])
                ins.then_inc(sem("swished_blocks"), 1)

            @block.vector
            def _(dve):
                chain = Chain(dve, sem("dve_chain"), count["dve"])
                dve.memset(kcT_p, 0.0).then_inc(sem("kcT_zero"), 1)
                dve.memset(mv, 1.0)
                dve.memset(css, 1.0).then_inc(sem("css_set"), 1)
                dve.wait_ge(sem("css_set"), 1)
                for t in range(TILES):
                    n = rows(t)
                    dve.wait_ge(sem("conv_moved"), t + 1)
                    chain(dve.bn_stats(bn[:n, t, :], conv[:n, t, :]))
                    dve.bn_aggr(mv[:n, t, :], bn[:n, t, :]).then_inc(sem("conv_moments"), 1)
                dve.wait_ge(sem("conv_sd"), 1)
                chain(dve.reciprocal(crs, csd))
                dve.wait_ge(sem("conv_moved"), TILES)
                dve.wait_ge(sem("conv_gain_in"), 48)
                for t in range(TILES):
                    n = rows(t)
                    chain(dve.tensor_scalar(conv[:n, t, :], conv[:n, t, :], mv[:n, t, 0:1], crs[:n, t:t + 1],
                                            ALU.subtract, ALU.mult))
                    dve.tensor_tensor(conv[:n, t, :], conv[:n, t, :], cg[:n, :], ALU.mult).then_inc(sem("conv_gained"), 1)
                dve.wait_ge(sem("conv_sd"), 2)
                chain(dve.reciprocal(crs, csd))
                for t in range(TILES):
                    n = rows(t)
                    dve.scalar_tensor_tensor(conv[:n, t, :], conv[:n, t, :], crs[:n, t:t + 1], cn[:n, :],
                                             ALU.mult, ALU.mult).then_inc(sem("conv_ready"), 1)
                dve.wait_ge(sem("conv_ready"), TILES)
                dve.wait_ge(sem("compressed"), 4)
                dve.tensor_copy(cmp_bias, ps[:, 5, 160:417:256]).then_inc(sem("bias_ready"), 1)
                dve.wait_ge(sem("blocks_made"), 1)
                dve.tensor_copy(kcT_s, ps[:, 0, 0:2 * P])
                dve.wait_ge(sem("kcT_zero"), 1)
                for g in range(KV):
                    dve.tensor_copy(kcT_p[64 * g:64 * g + 64, PBLK * g:PBLK * g + PBLK],
                                    ps[64 * g:64 * g + 64, 1, 0:PBLK])
                dve.tensor_copy(vc_p[:PBLK, :], ps[:PBLK, 1, P:2 * P])
                dve.tensor_copy(vc_s[:SBLK], ps[:SBLK, 2:4, :].rearrange("p c (b n) -> p (c b) n", b=4))\
                   .then_inc(sem("blocks_out"), 1)
                dve.wait_ge(sem("blocks_out"), 1)

            @block.gpsimd
            def _(pool):
                pool.wait_ge(sem("conv_gain_in"), 48)
                for t in range(TILES):
                    n = rows(t)
                    pool.wait_ge(sem("conv_gained"), t + 1)
                    pool.tensor_tensor(conv[:n, t, :], conv[:n, t, :], cb[:n, :], ALU.add)\
                        .then_inc(sem("conv_shifted"), 1)


        att = flat(A4, TILES * 512).rearrange("p (t n) -> p t n", n=512)
        probs = flat(A2b, 2048).rearrange("p (s n) -> p s n", s=2)
        pT = flat(A3, 2048).rearrange("p (s n) -> p s n", s=2)
        block_v = flat(A3 + 2048, 512)
        own_block = flat(A3 + 2560, 512)
        cmp_s = flat(A3 + 3072, 256).rearrange("p (s n) -> p s n", s=2)
        cmp_pT = flat(A3 + 3328, 256).rearrange("p (s n) -> p s n", s=2)
        weighted = flat(A3 + 3584, 512)
        cmp_add = flat(A3 + 4096, NQ * PBLK)
        neg_max = flat(A3 + 4224, 2)
        sums = flat(A3 + 4232, 32).rearrange("p (s w h) -> p s w h", s=2, w=2)
        small4 = flat(A3 + 4264, 64).rearrange("p (s n) -> p s n", n=16)
        gate_of = gates.rearrange("p t (h c) -> p t c h", c=3)
        SEL, WIN = 0, 1
        units = [(i, w, h) for i in range(NQ) for w in (SEL, WIN) for h in range(8)]

        def span(i, w):
            first = 0 if w == SEL else max(0, i - 4)
            return first, i + 1 - first

        def copies(u):
            _, m = span(*units[u][:2])
            if m > 4:
                return [("act", 0, 4), ("dve", 4, m - 4)]
            return [("act" if u % 2 else "dve", 0, m)]

        def copied_by(engine, u):
            return sum(e == engine for v in range(u + 1) for e, _, _ in copies(v))

        with nc.Block() as block:
            @block.sync
            def _(sp):
                o, w = const_at["own_block"]
                sp.dma_start(own_block, a["consts"][:, o:o + w]).then_inc(sem("own_block_in"), 16)
                for b in range(4):
                    load_pages(sp, a["cache_sel"], b * PAGES, b, "sel_page")

            @block.tensor
            def _(pe):
                for j, g in ((0, 0), (1, 1)):
                    mm = pe.matmul(ps[:, 5, 256 * g:256 * g + 256], con("rep_block", PBLK),
                                   vc_p[:PBLK, 64 * g:64 * g + 64].unsqueeze(1).to_broadcast([PBLK, R, HD]),
                                   start=True, stop=True)
                mm.then_inc(sem("values_spread"), 1)
                for i in range(NQ + 2):
                    if i < NQ:
                        if i >= 2:
                            pe.wait_ge(sem("cmp_scored_dve"), i - 1)
                        for r in range(R):
                            mm = pe.matmul(ps[:, i % 2, 32 * r:32 * r + 32], qT[:, r, i * P:(i + 1) * P],
                                           kcT_p, start=True, stop=True)
                        mm.then_inc(sem("cmp_scored"), 1)
                    if 1 <= i <= NQ:
                        pe.wait_ge(sem("cmp_probs"), i)
                        if i >= 2:
                            pe.wait_ge(sem("cmp_p_copied"), i - 1)
                        pe.transpose(ps[:, 2, 0:P], cmp_s[:, (i - 1) % 2, :], ident).then_inc(sem("cmp_p_turned"), 1)
                    if i >= 2:
                        pe.wait_ge(sem("cmp_p_copied"), i - 1)
                        pe.wait_ge(sem("block_v_ready"), 1)
                        if i >= 3:
                            pe.wait_ge(sem("cmp_out_copied"), i - 2)
                        pe.matmul(ps[:, 3, :], cmp_pT[:, (i - 2) % 2, :], block_v, start=True, stop=True)\
                          .then_inc(sem("cmp_out"), 1)
                pe.wait_ge(sem("cmp_out_copied"), NQ)
                pe.wait_ge(sem("block_v_ready"), 1)

                def score(u):
                    i, w, h = units[u]
                    g, r = h // R, h % R
                    first, m = span(i, w)
                    if u >= 2:
                        pe.wait_ge(sem("exp_done"), u - 1)
                    for o in range(0, m, 4):
                        n = min(4, m - o) * P
                        mm = pe.matmul(ps[:, 2 * (u % 2) + o // 4, 0:n],
                                       qT[64 * g:64 * g + 64, r, i * P:(i + 1) * P],
                                       kT[64 * g:64 * g + 64, w, (first + o) * P:(first + o) * P + n],
                                       start=True, stop=True)
                    mm.then_inc(sem("scored"), 1)

                def values(u):
                    i, w, h = units[u]
                    first, m = span(i, w)
                    pe.wait_ge(sem("pT_act"), copied_by("act", u))
                    pe.wait_ge(sem("pT_dve"), copied_by("dve", u))
                    if h == 0 and i > 0:
                        pe.wait_ge(sem("combined"), 2 * (i - 1) + w + 1)
                    for j in range(m):
                        mm = pe.matmul(ps[:, 6 + w, 64 * h:64 * h + 64], pT[:, u % 2, j * P:(j + 1) * P],
                                       vals[:, first + j, w, 64 * (h // R):64 * (h // R) + 64],
                                       start=(j == 0), stop=(j == m - 1))
                    mm.then_inc(sem("valued"), 1)

                score(0)
                for u in range(len(units)):
                    if u + 1 < len(units):
                        score(u + 1)
                    if u >= 1:
                        values(u - 1)
                    _, m = span(*units[u][:2])
                    pe.wait_ge(sem("exp_done"), u + 1)
                    for j in range(m):
                        mm = pe.transpose(ps[:, 4 + j // 4, (j % 4) * P:(j % 4 + 1) * P],
                                          probs[:, u % 2, j * P:(j + 1) * P], ident)
                    mm.then_inc(sem("turned"), 1)
                values(len(units) - 1)

            def wide(u, m):
                return ps[:, 2 * (u % 2):2 * (u % 2) + 2, :].rearrange("p b n -> p (b n)")[:, 0:m * P]

            def copy_turned(eng, copy, name, u):
                for e, o, m in copies(u):
                    if e == name:
                        eng.wait_ge(sem("turned"), u + 1)
                        copy(pT[:, u % 2, o * P:(o + m) * P], ps[:, 4 + o // 4, 0:m * P])\
                            .then_inc(sem(f"pT_{name}"), 1)

            @block.scalar
            def _(act):
                for i in range(NQ + 2):
                    if i < NQ:
                        act.wait_ge(sem("cmp_scored_dve"), i + 1)
                        act.activation(cmp_s[:, i % 2, :], cmp_s[:, i % 2, :], ACT.Exp).then_inc(sem("cmp_exp"), 1)
                    if 1 <= i <= NQ:
                        act.wait_ge(sem("cmp_p_turned"), i)
                        if i >= 3:
                            act.wait_ge(sem("cmp_out"), i - 2)
                        act.activation(cmp_pT[:, (i - 1) % 2, :], ps[:, 2, 0:P], ACT.Copy)\
                           .then_inc(sem("cmp_p_copied"), 1)
                    if i >= 2:
                        act.wait_ge(sem("cmp_out"), i - 1)
                        act.activation(att[:, i - 2, :], ps[:, 3, :], ACT.Copy).then_inc(sem("cmp_out_copied"), 1)

                def exp(u):
                    i, w, h = units[u]
                    _, m = span(i, w)
                    act.wait_ge(sem("max_ready"), u + 1)
                    if i >= 2 and h == 0:
                        act.wait_ge(sem("combined"), 2 * (i - 2) + w + 1)
                    act.activation(probs[:, u % 2, 0:m * P], wide(u, m), ACT.Exp, bias=neg_max[:, u % 2:u % 2 + 1],
                                   accum_out=sums[:, i % 2, w, h:h + 1]).then_inc(sem("exp_done"), 1)

                exp(0)
                for u in range(len(units)):
                    if u + 1 < len(units):
                        exp(u + 1)
                    copy_turned(act, lambda o, i: act.activation(o, i, ACT.Copy), "act", u)

            @block.vector
            def _(dve):
                chain = Chain(dve, sem("dve_chain"), count["dve"])
                chain(dve.tensor_scalar(cmp_add, con("cmp_ok"), -NEG, NEG, ALU.mult, ALU.add))
                dve.wait_ge(sem("own_block_in"), 16)
                dve.wait_ge(sem("values_spread"), 1)
                dve.tensor_tensor(block_v, ps[:, 5, :], own_block, ALU.mult).then_inc(sem("block_v_ready"), 1)

                def per_head(v):
                    return v.rearrange("p (h n) -> p h n", h=8)

                for i in range(NQ + 1):
                    if i < NQ:
                        dve.wait_ge(sem("cmp_scored"), i + 1)
                        if i >= 2:
                            dve.wait_ge(sem("cmp_p_turned"), i - 1)
                        s = per_head(cmp_s[:, i % 2, :])
                        st = small4[:, i % 2, :]
                        add = cmp_add[:, PBLK * i:PBLK * i + PBLK].unsqueeze(1).to_broadcast([P, R, PBLK])
                        by_group = ps[:, i % 2, 0:P].rearrange("p (r g n) -> p g r n", r=R, g=KV)
                        dve.tensor_tensor(s[:, 0:4], by_group[:, 0], add, ALU.add)
                        chain(dve.tensor_tensor(s[:, 4:8], by_group[:, 1], add, ALU.add))
                        chain(dve.tensor_reduce(st[:, 0:8], s, AX.X, ALU.max))
                        dve.tensor_tensor(s, s, st[:, 0:8].unsqueeze(2).to_broadcast([P, 8, PBLK]),
                                          ALU.subtract).then_inc(sem("cmp_scored_dve"), 1)
                    if i >= 1:
                        k = i - 1
                        s = per_head(cmp_s[:, k % 2, :])
                        st = small4[:, 2 + k % 2, :]
                        dve.wait_ge(sem("cmp_exp"), k + 1)
                        chain(dve.tensor_reduce(st[:, 0:8], s, AX.X, ALU.add))
                        chain(dve.reciprocal(st[:, 0:8], st[:, 0:8]))
                        dve.tensor_tensor(st[:, 8:16], st[:, 0:8], gate_of[:, k, 0, :], ALU.mult)
                        ok = con("cmp_ok")[:, PBLK * k:PBLK * k + PBLK].unsqueeze(1).to_broadcast([P, 8, PBLK])
                        chain(dve.tensor_tensor(s, s, ok, ALU.mult))
                        dve.tensor_tensor(s, s, st[:, 8:16].unsqueeze(2).to_broadcast([P, 8, PBLK]), ALU.mult)\
                           .then_inc(sem("cmp_probs"), 1)

                def maximum(u):
                    i, w, h = units[u]
                    _, m = span(i, w)
                    dve.wait_ge(sem("scored"), u + 1)
                    if u >= 2:
                        dve.wait_ge(sem("exp_done"), u - 1)
                    s = wide(u, m)
                    if w == WIN and i >= 4:
                        dve.tensor_tensor(s[:, 0:P], s[:, 0:P], con("low"), ALU.add)
                    chain(dve.tensor_tensor(s[:, (m - 1) * P:m * P], s[:, (m - 1) * P:m * P], con("causal"), ALU.add))
                    dve.tensor_reduce(neg_max[:, u % 2:u % 2 + 1], s, AX.X, ALU.max, negate=True)\
                       .then_inc(sem("max_ready"), 1)

                def combine(i, w):
                    st = small4[:, w, :]
                    dve.wait_ge(sem("valued"), 16 * i + 8 * w + 8)
                    chain(dve.reciprocal(st[:, 0:8], sums[:, i % 2, w, :]))
                    chain(dve.tensor_tensor(st[:, 8:16], st[:, 0:8], gate_of[:, i, 1 + w, :], ALU.mult))
                    chain(dve.tensor_tensor(per_head(weighted), per_head(ps[:, 6 + w, :]),
                                            st[:, 8:16].unsqueeze(2).to_broadcast([P, 8, HD]), ALU.mult))
                    dve.tensor_tensor(att[:, i, :], att[:, i, :], weighted, ALU.add).then_inc(sem("combined"), 1)
                    dve.wait_ge(sem("combined"), 2 * i + w + 1)

                maximum(0)
                dve.wait_ge(sem("cmp_out_copied"), NQ)
                for u in range(len(units)):
                    if u + 1 < len(units):
                        maximum(u + 1)
                    copy_turned(dve, lambda o, i: dve.tensor_copy(o, i), "dve", u)
                    i, w, h = units[u]
                    if h == 0 and u > 0:
                        combine(*units[u - 1][:2])
                combine(NQ - 1, WIN)

        win_pages = flat(AQ, 4096).rearrange("p (s n) -> p s n", n=256)
        spT = flat(AQ + 4096, 23 * P).rearrange("p (s n) -> p s n", n=P)
        att_sT = flat(AQ + 4096 + 23 * P, 128).rearrange("p (r n) -> p r n", r=R)
        s_sel = flat(A3, PAST + 32)
        s_win = flat(A3 + 2080, 544)
        s_cmp = flat(A3 + 2624, 32)
        imp = flat(A3 + 2656, 32)
        rank = flat(A3 + 2688, 32)
        gate_tmp = flat(A3 + 2720, 24).rearrange("p (c h) -> p c h", c=3)
        st5 = flat(A3 + 2744, 24)
        earlier = flat(A2b, 1024).rearrange("p (i j) -> p i j", i=SBLK)
        above = flat(A2b + 1024, 1024).rearrange("p (i j) -> p i j", i=SBLK)
        equal = flat(A2b + 2048, 1024).rearrange("p (i j) -> p i j", i=SBLK)
        OWN_SEL, OWN_WIN, CMP_T = 20, 21, 22
        with nc.Block() as block:
            @block.sync
            def _(sp):
                o, w = const_at["earlier"]
                sp.dma_start(earlier.rearrange("p i j -> p (i j)"), a["consts"][:, o:o + w])\
                  .then_inc(sem("earlier_in"), 16)
                sp.dma_start(win_pages, a["state_win_use"][0:16].rearrange("s p n -> p s n"))\
                  .then_inc(sem("win_page"), 16)
                sp.wait_ge(sem("s_scored"), 1)
                sp.dma_start(win_pages[:, :, 0:P], a["state_win_use"][16:32, :, 0:P].rearrange("s p n -> p s n"))\
                  .then_inc(sem("win_page"), 16)
                for b in range(4):
                    load_pages(sp, a["cache_sel"], HALF + b * PAGES, b, "sel_keys", slice(0, P))

            @block.gpsimd
            def _(pool):
                pool.wait_ge(sem("sampled"), 1)
                pool.dma_start(win_pages[:, :, P:2 * P], a["state_win_use"][16:32, :, P:2 * P].rearrange("s p n -> p s n"))\
                    .then_inc(sem("win_values"), 16)
                for b in range(4):
                    load_pages(pool, a["cache_sel"], HALF + b * PAGES, b, "sel_values", slice(P, 2 * P))

            @block.tensor
            def _(pe):
                for half in range(2):
                    for b in range(4):
                        pe.wait_ge(sem(f"sel_keys{b}" if half else f"sel_page{b}"), 16 * PAGES)
                    pe.wait_ge(sem("win_page"), 16 * (half + 1))
                    if half:
                        pe.wait_ge(sem("sample_out_copied"), 1)
                    for b in range(4):
                        q = q_diag[:, 4 * half + b, :]
                        o = slice(32 * b, 32 * b + 32)
                        n = 4 * half + b
                        mm = pe.matmul(ps[o, 6, 0:SBLK], q, kcT_s[:, 32 * n:32 * n + 32], start=True, stop=True,
                                       tile_position=(0, 32 * b))
                    mm.then_inc(sem("s_cmp_scored"), 1)
                    pe.matmul(ps[:, 7, 0:24], con("pick_token", NB * NS)[:, P * half:P * half + P],
                              gates[:NB * NS, NQ, :], start=True, stop=True).then_inc(sem("gates_spread"), 1)
                    for c in range(4):
                        for b in range(4):
                            pe.matmul(ps[32 * b:32 * b + 32, c, :], q_diag[:, 4 * half + b, :],
                                      pages[:, PAGES * b + 4 * c:PAGES * b + 4 * c + 4, 0:P],
                                      start=True, stop=True, tile_position=(0, 32 * b))
                    for b in range(4):
                        pe.matmul(ps[32 * b:32 * b + 32, 5, :], q_diag[:, 4 * half + b, :],
                                  win_pages[:, 4 * b:4 * b + 4, 0:P], start=True, stop=True,
                                  tile_position=(0, 32 * b))
                    for w in range(2):
                        for b in range(4):
                            mm = pe.matmul(ps[32 * b:32 * b + 32, 4, 32 * w:32 * w + 32], q_diag[:, 4 * half + b, :],
                                           kT_new[:, w, :], start=True, stop=True, tile_position=(0, 32 * b))
                    mm.then_inc(sem("s_scored"), 1)
                    pe.wait_ge(sem("s_cmp_normed"), half + 1)
                    pe.wait_ge(sem("gates_taken"), half + 1)
                    pe.matmul(ps[:, 7, 0:SBLK], con("same_query"), s_cmp, start=True, stop=True)\
                      .then_inc(sem("importance"), 1)
                    pe.wait_ge(sem("s_probs"), half + 1)
                    for j in range(PAGES):
                        mm = pe.transpose(ps[:, j // 4, (j % 4) * P:(j % 4 + 1) * P], s_sel[:, j * P:(j + 1) * P], ident)
                        if j % 4 == 3:
                            mm.then_inc(sem("s_turned"), 1)
                    for j in range(4):
                        mm = pe.transpose(ps[:, 5, j * P:(j + 1) * P], s_win[:, j * P:(j + 1) * P], ident)
                    mm.then_inc(sem("s_turned"), 1)
                    pe.transpose(ps[:32, 4, 0:P], s_sel[:, PAST:PAST + 32], ident)
                    pe.transpose(ps[:32, 4, P:2 * P], s_win[:, 512:544], ident)
                    pe.transpose(ps[:32, 4, 2 * P:3 * P], s_cmp, ident).then_inc(sem("s_turned"), 1)
                    pe.wait_ge(sem("sT_act"), 3 * (half + 1))
                    pe.wait_ge(sem("sT_dve"), 3 * (half + 1))
                    pe.matmul(ps[:, 6, 0:P], v_new[:32, 0, :], spT[:32, OWN_SEL, :], start=True, stop=False,
                              skip_group_check=True)
                    pe.matmul(ps[:, 6, 0:P], v_new[:32, 1, :], spT[:32, OWN_WIN, :], start=False, stop=False,
                              skip_group_check=True)
                    if half:
                        pe.wait_ge(sem("win_values"), 16)
                    for b in range(4):
                        if half:
                            pe.wait_ge(sem(f"sel_values{b}"), 16 * PAGES)
                        o = slice(32 * b, 32 * b + 32)
                        pe.matmul(ps[:, 6, o], vc_s[:SBLK, 4 * half + b, :], spT[:32, CMP_T, o],
                                  start=False, stop=False, skip_group_check=True)
                        for j in range(PAGES):
                            pe.matmul(ps[:, 6, o], pages[:, PAGES * b + j, P:2 * P], spT[:, j, o],
                                      start=False, stop=False, skip_group_check=True)
                        for j in range(4):
                            mm = pe.matmul(ps[:, 6, o], win_pages[:, 4 * b + j, P:2 * P], spT[:, PAGES + j, o],
                                           start=False, stop=(j == 3), skip_group_check=True)
                    mm.then_inc(sem("sampled"), 1)
                pe.wait_ge(sem("sample_out_copied"), 2)
                for r in range(R):
                    mm = pe.transpose(ps[:32, 7, r * P:(r + 1) * P], att_sT[:, r, :], ident)
                mm.then_inc(sem("sample_turned"), 1)

            @block.scalar
            def _(act):
                for half in range(2):
                    act.wait_ge(sem("s_cmp_max"), half + 1)
                    act.activation(s_cmp, ps[:, 6, 0:SBLK], ACT.Exp, bias=st5[:, 0:1], accum_out=st5[:, 3:4])\
                       .then_inc(sem("s_cmp_exp"), 1)
                    act.wait_ge(sem("s_max"), half + 1)
                    act.activation(s_win, s_win, ACT.Exp, bias=st5[:, 2:3], accum_out=st5[:, 5:6])
                    act.activation(s_sel, s_sel, ACT.Exp, bias=st5[:, 1:2], accum_out=st5[:, 4:5])\
                       .then_inc(sem("s_exp"), 1)
                    for n, bank in ((0, 0), (2, 2), (4, 5)):
                        act.wait_ge(sem("s_turned"), 6 * half + n + 1)
                        o = PAGES if bank == 5 else 4 * bank
                        act.activation(spT[:, o:o + 4, :], ps[:, bank, :].rearrange("p (s n) -> p s n", n=P),
                                       ACT.Copy).then_inc(sem("sT_act"), 1)
                act.wait_ge(sem("sample_turned"), 1)
                act.activation(att[:32, NQ, :].rearrange("p (g r d) -> p r g d", g=KV, r=R),
                               ps[:32, 7, :].rearrange("p (r g d) -> p r g d", r=R, g=KV), ACT.Copy)\
                   .then_inc(sem("att_done"), 1)

            @block.vector
            def _(dve):
                chain = Chain(dve, sem("dve_chain"), count["dve"])
                dve.wait_ge(sem("earlier_in"), 16)
                for half in range(2):
                    dve.wait_ge(sem("s_cmp_scored"), half + 1)
                    dve.tensor_reduce(st5[:, 0:1], ps[:, 6, 0:SBLK], AX.X, ALU.max, negate=True)\
                       .then_inc(sem("s_cmp_max"), 1)
                    dve.wait_ge(sem("gates_spread"), half + 1)
                    chain(dve.tensor_tensor(gate_tmp, ps[:, 7, 0:24].rearrange("p (h c) -> p c h", c=3),
                                            con("own_head").unsqueeze(1).to_broadcast([P, 3, 8]), ALU.mult))
                    dve.tensor_reduce(st5[:, 6:9], gate_tmp, AX.X, ALU.add).then_inc(sem("gates_taken"), 1)
                    dve.wait_ge(sem("s_cmp_exp"), half + 1)
                    chain(dve.reciprocal(st5[:, 9:10], st5[:, 3:4]))
                    dve.tensor_scalar(s_cmp, s_cmp, st5[:, 9:10], None, ALU.mult).then_inc(sem("s_cmp_normed"), 1)
                    dve.wait_ge(sem("importance"), half + 1)
                    dve.tensor_scalar(s_cmp, s_cmp, st5[:, 6:7], None, ALU.mult)
                    chain(dve.tensor_copy(imp, ps[:, 7, 0:SBLK]))
                    other = imp.unsqueeze(1).to_broadcast([P, SBLK, SBLK])
                    itself = imp.unsqueeze(2).to_broadcast([P, SBLK, SBLK])
                    chain(dve.tensor_tensor(above, other, itself, ALU.is_gt))
                    chain(dve.tensor_tensor(equal, other, itself, ALU.is_equal))
                    chain(dve.tensor_tensor(equal, equal, earlier, ALU.mult))
                    chain(dve.tensor_tensor(above, above, equal, ALU.add))
                    chain(dve.tensor_reduce(rank, above, AX.X, ALU.add))
                    chain(dve.tensor_scalar(rank, rank, float(NSEL), NEG, ALU.is_ge, ALU.mult))
                    dve.wait_ge(sem("s_scored"), half + 1)
                    for c in range(4):
                        chosen = rank[:, 8 * c:8 * c + 8].unsqueeze(2).to_broadcast([P, 8, CMP])
                        dve.tensor_tensor(s_sel[:, 512 * c:512 * c + 512].rearrange("p (b n) -> p b n", b=8),
                                          ps[:, c, :].rearrange("p (b n) -> p b n", b=8), chosen, ALU.add)
                    own = con("own")[:, 32 * half:32 * half + 32]
                    dve.tensor_tensor(s_sel[:, PAST:PAST + 32], ps[:, 4, 0:32], own, ALU.add)
                    dve.tensor_tensor(s_win[:, 512:544], ps[:, 4, 32:64], own, ALU.add)
                    chain(dve.tensor_tensor(s_win[:, 0:512], ps[:, 5, :], con("win"), ALU.add))
                    dve.tensor_reduce(st5[:, 2:3], s_win, AX.X, ALU.max, negate=True)
                    dve.tensor_reduce(st5[:, 1:2], s_sel, AX.X, ALU.max, negate=True).then_inc(sem("s_max"), 1)
                    dve.wait_ge(sem("s_exp"), half + 1)
                    chain(dve.reciprocal(st5[:, 10:12], st5[:, 4:6]))
                    chain(dve.tensor_tensor(st5[:, 12:14], st5[:, 10:12], st5[:, 7:9], ALU.mult))
                    dve.tensor_scalar(s_win, s_win, st5[:, 13:14], None, ALU.mult)
                    dve.tensor_scalar(s_sel, s_sel, st5[:, 12:13], None, ALU.mult).then_inc(sem("s_probs"), 1)
                    for n, bank in ((1, 1), (3, 3)):
                        dve.wait_ge(sem("s_turned"), 6 * half + n + 1)
                        dve.tensor_copy(spT[:, 4 * bank:4 * bank + 4, :],
                                        ps[:, bank, :].rearrange("p (s n) -> p s n", n=P)).then_inc(sem("sT_dve"), 1)
                    dve.wait_ge(sem("s_turned"), 6 * half + 6)
                    dve.tensor_copy(spT[:32, OWN_SEL:OWN_SEL + 3, :],
                                    ps[:32, 4, 0:3 * P].rearrange("p (s n) -> p s n", n=P)).then_inc(sem("sT_dve"), 1)
                    dve.wait_ge(sem("sampled"), half + 1)
                    for g in range(KV):
                        src = ps[64 * g:64 * g + 64, 6, 0:P].rearrange("p (b g r s) -> p g r b s", b=4, g=KV, r=R)
                        ins = dve.tensor_copy(
                            att_sT[64 * g:64 * g + 64, :, 16 * half:16 * half + 16].rearrange(
                                "p r (b s) -> p r b s", b=4), src[:, g])
                    ins.then_inc(sem("sample_out_copied"), 1)
        reuse_semaphores()


        x_res = flat(AQ, TILES * D).rearrange("p (t n) -> p t n", n=D)
        ln2_g, att_g, final_g = gain[:, 0:D], gain[:, D:D + 512], gain[:, D + 512:2 * D + 512]
        w_out = flat(A1, 8192).rearrange("p (k n) -> p k n", k=KT_)
        mixT = flat(A1 + 8192, 2048).rearrange("p (s k n) -> p s k n", s=2, k=KT_)
        xt = flat(A1 + 10240, 2048).rearrange("p (s n) -> p s n", s=2)
        h_sb = flat(A1 + 12288, 2048).rearrange("p (s n) -> p s n", s=2)
        hT = flat(A1 + 14336, 2048).rearrange("p (s k n) -> p s k n", s=2, k=KT_)
        w_router = flat(A1 + 16384, KT_ * 36).rearrange("p (k n) -> p k n", k=KT_)
        junk6 = flat(A3, D)
        logits = flat(A3 + 1024, TILES * 36).rearrange("p (t n) -> p t n", n=36)
        st6 = flat(A3 + 1352, 72).rearrange("p (q n) -> p q n", q=8)
        with nc.Block() as block:
            @block.sync
            def _(sp):
                sp.dma_start(att_g, a["norm_att"].partition_broadcast(P)).then_inc(sem("att_gain_in"), 16)
                sp.dma_start(w_out[:, 0:4, :], a["w_out"][0:512].rearrange("(p c) n -> p c n", c=4))\
                  .then_inc(sem("w_out_in"), 16)
                sp.dma_start(w_out[:, 4:8, :], a["w_out"][512:1024].rearrange("(p c) n -> p c n", c=4))\
                  .then_inc(sem("w_out_in"), 16)
                sp.dma_start(ln2_g, a["ln2"].partition_broadcast(P)).then_inc(sem("late_gain_in"), 16)
                sp.dma_start(final_g, a["ln_final"].partition_broadcast(P)).then_inc(sem("late_gain_in"), 16)
                sp.dma_start(w_router, a["w_router"].rearrange("p (k n) -> p k n", k=KT_)).then_inc(sem("w_router_in"), 16)
                for t in range(TILES):
                    if t >= 2:
                        sp.wait_ge(sem("merged"), t - 1)
                    sp.dma_start(xt[:rows(t), t % 2, :], x_rows[t]).then_inc(sem(f"xt_in{t % 2}"), 16)
                    if t >= 1:
                        sp.wait_ge(sem("h_ready"), t)
                        sp.dma_start(scratch_h[P * (t - 1):P * (t - 1) + rows(t - 1), :],
                                     h_sb[:rows(t - 1), (t - 1) % 2, :]).then_inc(sem(f"h_out{(t - 1) % 2}"), 16)
                sp.wait_ge(sem("h_ready"), TILES)
                sp.dma_start(scratch_h[SEQ:TOKENS, :], h_sb[:rows(NQ), 0, :]).then_inc(sem("h_out0"), 16)
                sp.wait_ge(sem("h_out0"), 16 * 5)
                sp.wait_ge(sem("h_out1"), 16 * 4)

            @block.tensor
            def _(pe):
                def router(t):
                    n = rows(t)
                    pe.wait_ge(sem("h_ready"), t + 1)
                    if t >= 1:
                        pe.wait_ge(sem("hT_act"), t)
                        pe.wait_ge(sem("hT_dve"), t)
                    hv = h_sb[:n, t % 2, :].rearrange("p (m k) -> p k m", k=KT_)
                    for k in range(KT_):
                        mm = pe.transpose(ps[:, 4 + k // 4, (k % 4) * P:(k % 4) * P + n], hv[:, k, :], ident[:n, :n])
                    mm.then_inc(sem("h_turned"), 1)
                    pe.wait_ge(sem("hT_act"), t + 1)
                    pe.wait_ge(sem("hT_dve"), t + 1)
                    if t == 0:
                        pe.wait_ge(sem("w_router_in"), 16)
                    else:
                        pe.wait_ge(sem("logits_taken"), t)
                    for k in range(KT_):
                        mm = pe.matmul(ps[:n, 6, 0:36], hT[:, t % 2, k, 0:n], w_router[:, k, :],
                                       start=(k == 0), stop=(k == KT_ - 1))
                    mm.then_inc(sem("routed"), 1)

                for t in range(TILES):
                    n = rows(t)
                    pe.wait_ge(sem("att_normed"), t + 1)
                    if t >= 1:
                        pe.wait_ge(sem("mixT_act"), t)
                        pe.wait_ge(sem("mixT_dve"), t)
                    for half, src in enumerate((conv, att)):
                        sv = src[:n, t, :].rearrange("p (m c) -> p c m", c=4)
                        for c in range(4):
                            mm = pe.transpose(ps[:, half, c * P:c * P + n], sv[:, c, :], ident[:n, :n])
                    mm.then_inc(sem("mix_turned"), 1)
                    pe.wait_ge(sem("mixT_act"), t + 1)
                    pe.wait_ge(sem("mixT_dve"), t + 1)
                    if t == 0:
                        pe.wait_ge(sem("w_out_in"), 32)
                    else:
                        pe.wait_ge(sem("merged"), t)
                    for half in range(2):
                        for k in range(KT_):
                            mm = pe.matmul(ps[:n, 2 + half, :], mixT[:, t % 2, k, 0:n],
                                           w_out[:, k, 512 * half:512 * half + 512],
                                           start=(k == 0), stop=(k == KT_ - 1))
                    mm.then_inc(sem("mixed"), 1)
                    if t >= 1:
                        router(t - 1)
                router(TILES - 1)

            @block.scalar
            def _(act):
                chain = Chain(act, sem("act_chain"), count["act"])
                act.wait_ge(sem("st6_set"), 1)
                for t in range(TILES):
                    chain(act.activation(junk6[:rows(t), 0:512], att[:rows(t), t, :], ACT.Square, scale=512 ** -0.5,
                                         accum_out=st6[:rows(t), 0, t:t + 1]))
                act.activation(st6[:, 1, :], st6[:, 0, :], ACT.Sqrt, bias=con("eps")[:, 0:1])\
                   .then_inc(sem("att_sd"), 1)
                for t in range(TILES + 1):
                    if t < TILES:
                        n = rows(t)
                        act.wait_ge(sem("mix_turned"), t + 1)
                        if t >= 2:
                            act.wait_ge(sem("mixed"), t - 1)
                        act.activation(mixT[:, t % 2, 0:4, 0:n],
                                       ps[:, 0, :].rearrange("p (c m) -> p c m", c=4)[:, :, 0:n], ACT.Copy)\
                           .then_inc(sem("mixT_act"), 1)
                    if t >= 1:
                        q, n = t - 1, rows(t - 1)
                        act.wait_ge(sem("h_turned"), q + 1)
                        if q >= 2:
                            act.wait_ge(sem("routed"), q - 1)
                        act.activation(hT[:, q % 2, 0:4, 0:n],
                                       ps[:, 4, :].rearrange("p (c m) -> p c m", c=4)[:, :, 0:n], ACT.Copy)\
                           .then_inc(sem("hT_act"), 1)
                    if t < TILES:
                        n = rows(t)
                        act.wait_ge(sem("merged"), t + 1)
                        chain(act.activation(junk6[:n, :], x_res[:n, t, :], ACT.Square, scale=1 / 32,
                                             accum_out=st6[:n, 3, t:t + 1]))
                        act.activation(st6[:n, 4, t:t + 1], st6[:n, 3, t:t + 1], ACT.Sqrt,
                                       bias=con("eps")[:n, 0:1]).then_inc(sem("x_sd"), 1)

            @block.vector
            def _(dve):
                chain = Chain(dve, sem("dve_chain"), count["dve"])
                dve.memset(logits, 0.0)
                dve.memset(st6, 1.0).then_inc(sem("st6_set"), 1)
                dve.wait_ge(sem("att_sd"), 1)
                chain(dve.reciprocal(st6[:, 2, :], st6[:, 1, :]))
                dve.wait_ge(sem("att_gain_in"), 16)
                for t in range(TILES):
                    n = rows(t)
                    dve.scalar_tensor_tensor(att[:n, t, :], att[:n, t, :], st6[:n, 2, t:t + 1], att_g[:n, :],
                                             ALU.mult, ALU.mult).then_inc(sem("att_normed"), 1)
                dve.wait_ge(sem("late_gain_in"), 32)
                for t in range(TILES + 1):
                    if t < TILES:
                        n = rows(t)
                        dve.wait_ge(sem("mix_turned"), t + 1)
                        if t >= 2:
                            dve.wait_ge(sem("mixed"), t - 1)
                        dve.tensor_copy(mixT[:, t % 2, 4:8, 0:n],
                                        ps[:, 1, :].rearrange("p (c m) -> p c m", c=4)[:, :, 0:n])\
                           .then_inc(sem("mixT_dve"), 1)
                    if t >= 1:
                        q, n = t - 1, rows(t - 1)
                        dve.wait_ge(sem("h_turned"), q + 1)
                        if q >= 2:
                            dve.wait_ge(sem("routed"), q - 1)
                        dve.tensor_copy(hT[:, q % 2, 4:8, 0:n],
                                        ps[:, 5, :].rearrange("p (c m) -> p c m", c=4)[:, :, 0:n])\
                           .then_inc(sem("hT_dve"), 1)
                        dve.wait_ge(sem("routed"), q + 1)
                        dve.tensor_copy(logits[:n, q, :], ps[:n, 6, 0:36]).then_inc(sem("logits_taken"), 1)
                    if t < TILES:
                        n = rows(t)
                        dve.wait_ge(sem("mixed"), t + 1)
                        dve.wait_ge(sem(f"xt_in{t % 2}"), 16 * (t // 2 + 1))
                        dve.tensor_tensor(x_res[:n, t, :], ps[:n, 2:4, :].rearrange("p b n -> p (b n)"),
                                          xt[:n, t % 2, :], ALU.add).then_inc(sem("merged"), 1)
                        dve.wait_ge(sem("x_sd"), t + 1)
                        chain(dve.reciprocal(st6[:n, 5, t:t + 1], st6[:n, 4, t:t + 1]))
                        if t >= 2:
                            dve.wait_ge(sem(f"h_out{t % 2}"), 16 * (t // 2))
                            dve.wait_ge(sem("h_turned"), t - 1)
                        dve.scalar_tensor_tensor(h_sb[:n, t % 2, :], x_res[:n, t, :], st6[:n, 5, t:t + 1],
                                                 ln2_g[:n, :], ALU.mult, ALU.mult).then_inc(sem("h_ready"), 1)
                dve.wait_ge(sem("logits_taken"), TILES)

        E_, G_ = EXPERTS, GROUPS
        r7 = [A3 + 1424]

        def tmp7(n, shape=None):
            r7[0] += n
            v = flat(r7[0] - n, n)
            return v if shape is None else v.rearrange("p (t n) -> p t n", n=shape)

        first_w, second_w = stat(TILES), stat(TILES)
        dest = ints[:, 0:2 * TILES]
        row_of = ints[:, 2 * TILES:2 * TILES + CHUNKS + 1]
        wide7 = A4
        one_slot = flat(A3 + 2048, 2 * TILES * P).rearrange("p (q n) -> p q n", n=P)
        one_chunk = flat(A1 + 16384, 2 * TILES * (CHUNKS + 1)).rearrange("p (q n) -> p q n", n=CHUNKS + 1)
        lane = flat(A1 + 16384 + 960, P)
        chosen1 = flat(wide7, 288).rearrange("p (t n) -> p t n", n=E_)
        chosen2 = flat(wide7 + 288, 288).rearrange("p (t n) -> p t n", n=E_)
        le_m = flat(wide7 + 576, 288).rearrange("p (t n) -> p t n", n=E_)
        cand = flat(wide7 + 864, 288).rearrange("p (t n) -> p t n", n=E_)
        both = flat(wide7 + 1152, 288).rearrange("p (t n) -> p t n", n=E_)
        slot = flat(wide7 + 1440, 288).rearrange("p (t n) -> p t n", n=E_)
        base = flat(wide7 + 1728, 320).rearrange("p (t n) -> p t n", n=E_)
        steps7 = flat(wide7 + 2048, 288).rearrange("p (e k) -> p e k", e=E_)
        ends_le = flat(wide7 + 2336, (CHUNKS + 1) * E_).rearrange("p (c e) -> p c e", e=E_)
        group4 = tmp7(36, 4)
        cand4 = tmp7(36, 4)
        exp4 = tmp7(36, 4)
        g_max, c_max, p_top, m1, m2, diff, inv_d, sum4 = (tmp7(TILES) for _ in range(8))
        n_chunk, cum, cum0, ones32 = (tmp7(E_) for _ in range(4))
        valid7 = tmp7(TILES)
        chunk_f = tmp7(CHUNKS + 2)
        destf, dest_q, dest_c = (tmp7(2 * TILES) for _ in range(3))
        w_gate = [flat(A2 + 12288 * s, 4096).rearrange("p (k n) -> p k n", k=KT_) for s in range(2)]
        w_up = [flat(A2 + 12288 * s + 4096, 4096).rearrange("p (k n) -> p k n", k=KT_) for s in range(2)]
        w_down = [flat(A2 + 12288 * s + 8192, 4096).rearrange("p (h k n) -> p h k n", h=2, k=2) for s in range(2)]
        xg = [flat(A3 + 1024 * s, D) for s in range(2)]
        xgT = [flat(A3 + 2048 + 1024 * s, D).rearrange("p (k n) -> p k n", k=KT_) for s in range(2)]
        hid = [flat(A4 + 512 * s, DE) for s in range(2)]
        hidT = flat(A4 + 1024, 512).rearrange("p (k n) -> p k n", k=4)
        y_sb = [flat(A4 + 1536 + 1024 * s, D) for s in range(2)]
        zero_rows = flat(A4 + 3584, D)
        ids = [ints[:, 68 + s:69 + s] for s in range(2)]
        N_AT = CHUNKS + 1
        HH = DE // 2
        GATE_BANK, UP_BANK = (0, 7), (1, 5)

        def chunk_count(eng):
            eng.wait_ge(sem("plan_ready"), 1)
            return eng.value_load(row_ints[0:1, N_AT:N_AT + 1], min_val=1, max_val=CHUNKS)

        def expert_weights(sp):
            n_chunks = chunk_count(sp)
            with sp.Fori(0, CHUNKS // 2) as i:
                for s in range(2):
                    with sp.If(i * 2 + s < n_chunks):
                        e = sp.value_load(row_ints[0:1, bass.ds(i * 2 + s, 1)], min_val=0, max_val=EXPERTS - 1)
                        sp.wait_ge(sem(f"upped{s}"), i + 1)
                        for w, name in ((w_gate, "w_gate"), (w_up, "w_up")):
                            sp.dma_start(w[s], a[name][bass.ds(e, 1)].rearrange("a (p k) n -> (a p) k n", k=KT_))\
                              .then_inc(sem(f"{name}_in{s}"), 16)
                        sp.wait_ge(sem(f"downed{s}"), i + 1)
                        sp.dma_start(w_down[s],
                                     a["w_down"][bass.ds(e, 1)].rearrange("a (h p k) n -> (a p) h k n", h=2, k=2))\
                          .then_inc(sem(f"w_down_in{s}"), 16)
            sp.wait_ge(sem("rows_zero"), 1)
            with sp.Fori(0, CHUNKS) as i:
                with sp.If(n_chunks <= i):
                    sp.dma_start(scratch_y[bass.ds(i * P, P), :], zero_rows).then_inc(sem("unused_zeroed"), 16)

        def expert_rows(pool):
            def take_ids(c, s, n):
                pool.tensor_copy(ids[s], row_of[:, bass.ds(c, 1)]).then_inc(sem(f"ids_ready{s}"), 1)
                pool.wait_ge(sem(f"xg_turned{s}"), n + 1)
                pool.wait_ge(sem(f"ids_ready{s}"), n + 1)

            def gather(s, n):
                pool.indirect_dma_start(xg[s], None, scratch_h,
                                        bass.IndirectOffsetOnAxis(ap=ids[s].bitcast(U32), axis=0))\
                    .then_inc(sem(f"xg_in{s}"), 16)
                pool.wait_ge(sem(f"xg_in{s}"), n * 16 + 16)

            n_chunks = chunk_count(pool)
            take_ids(0, 0, 0)
            gather(0, 0)
            pool.memset(zero_rows, 0.0).then_inc(sem("rows_zero"), 1)
            with pool.Fori(0, CHUNKS // 2) as i:
                for s in range(2):
                    with pool.If(i * 2 + s < n_chunks):
                        take_ids(i * 2 + s + 1, 1 - s, i + s)
                    with pool.If(i * 2 + s < n_chunks):
                        gather(1 - s, i + s)
            for s in range(2):
                with pool.Fori(0, CHUNKS // 2) as i:
                    with pool.If(i * 2 + s < n_chunks):
                        pool.wait_ge(sem(f"y_out{s}"), i * 16 + 32)
            with pool.Fori(0, CHUNKS) as i:
                with pool.If(i + n_chunks == CHUNKS - 1):
                    pool.wait_ge(sem("unused_zeroed"), i * 16 + 16)

        def expert_products(pe):
            def turn(s, n):
                pe.wait_ge(sem(f"xg_in{s}"), n * 16 + 16)
                v = xg[s].rearrange("p (m k) -> p k m", k=KT_)
                for k in range(KT_):
                    mm = pe.transpose(ps[:, 2 + k // 4, (k % 4) * P:(k % 4 + 1) * P], v[:, k, :], ident)
                mm.then_inc(sem(f"xg_turned{s}"), 1)

            def project(w, s, half, bank):
                for k in range(KT_):
                    mm = pe.matmul(ps[:, bank, 0:HH], xgT[s][:, k, :], w[s][:, k, HH * half:HH * half + HH],
                                   start=(k == 0), stop=(k == KT_ - 1))
                return mm

            def turn_hidden(s, half, bank):
                v = hid[s][:, HH * half:HH * half + HH].rearrange("p (m k) -> p k m", k=2)
                for k in range(2):
                    mm = pe.transpose(ps[:, bank, k * P:(k + 1) * P], v[:, k, :], ident)
                return mm

            for name in ("upped0", "upped1", "downed0", "downed1", "xg_turned0", "xg_turned1"):
                pe.sem_inc(sem(name), 1)
            n_chunks = chunk_count(pe)
            pe.wait_ge(sem("table_ready"), 1)
            turn(0, 0)
            with pe.Fori(0, CHUNKS // 2) as i:
                for s in range(2):
                    with pe.If(i * 2 + s < n_chunks):
                        pe.wait_ge(sem(f"xgT_act{s}"), i + 1)
                        pe.wait_ge(sem(f"xgT_dve{s}"), i + 1)
                        pe.wait_ge(sem(f"w_gate_in{s}"), i * 16 + 16)
                        project(w_gate, s, 0, GATE_BANK[0]).then_inc(sem("gated"), 1)
                        pe.wait_ge(sem(f"w_up_in{s}"), i * 16 + 16)
                        project(w_up, s, 0, UP_BANK[0]).then_inc(sem("half_upped"), 1)
                        project(w_gate, s, 1, GATE_BANK[1]).then_inc(sem("gated"), 1)
                        pe.wait_ge(sem("y_act"), i * 2 + s + 1)
                        project(w_up, s, 1, UP_BANK[1]).then_inc(sem(f"upped{s}"), 1)
                        pe.wait_ge(sem("hid_done"), i * 4 + 2 * s + 2)
                        turn_hidden(s, 0, 4).then_inc(sem("first_turned"), 1)
                        turn(1 - s, i + s)
                        pe.wait_ge(sem("hid_done"), i * 4 + 2 * s + 3)
                        turn_hidden(s, 1, 0).then_inc(sem("second_turned"), 1)
                        pe.wait_ge(sem("y_dve"), i * 2 + s + 1)
                        pe.wait_ge(sem(f"w_down_in{s}"), i * 16 + 16)
                        for h in range(2):
                            pe.wait_ge(sem("hidT_dve" if h else "hidT_act"), i * 2 + s + 1)
                            for half in range(2):
                                for k in range(2):
                                    mm = pe.matmul(ps[:, 5 + half, :], hidT[:, 2 * h + k, :],
                                                   w_down[s][:, h, k, 512 * half:512 * half + 512],
                                                   start=(h == 0 and k == 0), stop=(h == 1 and k == 1))
                        mm.then_inc(sem(f"downed{s}"), 1)

        def expert_silu(act):
            def copy_x(s, n):
                act.wait_ge(sem(f"upped{s}"), n + 1)
                act.wait_ge(sem(f"xg_turned{s}"), n + 2)
                act.activation(xgT[s][:, 0:4, :].rearrange("p k n -> p (k n)"), ps[:, 2, :], ACT.Copy)\
                   .then_inc(sem(f"xgT_act{s}"), 1)

            act.sem_inc(sem("y_act"), 1)
            for s in range(2):
                act.dma_start(scratch_first[s:s + 1, :], CON[0:1, 0:16]).then_inc(sem(f"y_out{s}"), 16)
            n_chunks = chunk_count(act)
            copy_x(0, 0)
            with act.Fori(0, CHUNKS // 2) as i:
                for s in range(2):
                    with act.If(i * 2 + s < n_chunks):
                        for h in range(2):
                            act.wait_ge(sem("gated"), i * 4 + 2 * s + h + 1)
                            act.activation(hid[s][:, HH * h:HH * h + HH], ps[:, GATE_BANK[h], 0:HH], ACT.Silu)\
                               .then_inc(sem("silu_done"), 1)
                        act.wait_ge(sem("first_turned"), i * 2 + s + 1)
                        act.activation(hidT[:, 0:2, :].rearrange("p k n -> p (k n)"), ps[:, 4, 0:HH], ACT.Copy)\
                           .then_inc(sem("hidT_act"), 1)
                        copy_x(1 - s, i + s)
                        act.wait_ge(sem(f"y_out{s}"), i * 16 + 16)
                        act.wait_ge(sem(f"downed{s}"), i + 2)
                        act.activation(y_sb[s][:, 0:512], ps[:, 5, :], ACT.Copy).then_inc(sem("y_act"), 1)
                        act.wait_ge(sem("y_act"), i * 2 + s + 2)
                        act.wait_ge(sem("y_dve"), i * 2 + s + 2)
                        act.dma_start(scratch_y[bass.ds((i * 2 + s) * P, P), :], y_sb[s]).then_inc(sem(f"y_out{s}"), 16)

        def expert_copies(dve):
            def copy_x(s, n):
                dve.wait_ge(sem(f"upped{s}"), n + 1)
                dve.wait_ge(sem(f"xg_turned{s}"), n + 2)
                dve.tensor_copy(xgT[s][:, 4:8, :].rearrange("p k n -> p (k n)"), ps[:, 3, :])\
                   .then_inc(sem(f"xgT_dve{s}"), 1)

            for name in ("hid_done", "y_dve"):
                dve.sem_inc(sem(name), 1)
            n_chunks = chunk_count(dve)
            copy_x(0, 0)
            with dve.Fori(0, CHUNKS // 2) as i:
                for s in range(2):
                    with dve.If(i * 2 + s < n_chunks):
                        for h in range(2):
                            dve.wait_ge(sem(f"upped{s}" if h else "half_upped"), i + 2 if h else i * 2 + s + 1)
                            dve.wait_ge(sem("silu_done"), i * 4 + 2 * s + h + 1)
                            o = hid[s][:, HH * h:HH * h + HH]
                            dve.tensor_tensor(o, o, ps[:, UP_BANK[h], 0:HH], ALU.mult).then_inc(sem("hid_done"), 1)
                        copy_x(1 - s, i + s)
                        dve.wait_ge(sem("second_turned"), i * 2 + s + 1)
                        dve.tensor_copy(hidT[:, 2:4, :].rearrange("p k n -> p (k n)"), ps[:, 0, 0:HH])\
                           .then_inc(sem("hidT_dve"), 1)
                        dve.wait_ge(sem(f"y_out{s}"), i * 16 + 16)
                        dve.wait_ge(sem(f"downed{s}"), i + 2)
                        dve.tensor_copy(y_sb[s][:, 512:1024], ps[:, 6, :]).then_inc(sem("y_dve"), 1)

        with nc.Block() as block:
            @block.sync
            def _(sp):
                o, w = const_at["lane"]
                sp.dma_start(lane, a["consts"][:, o:o + w]).then_inc(sem("lane_in"), 16)
                expert_weights(sp)

            @block.tensor
            def _(pe):
                pe.wait_ge(sem("counted"), 1)
                fb = both.rearrange("p t n -> p (t n)")
                pe.matmul(ps[:, 0, 0:288], con("before"), fb, start=True, stop=True)
                pe.matmul(ps[:, 1, 0:288], con("ones"), fb, start=True, stop=True).then_inc(sem("prefixed"), 1)
                pe.wait_ge(sem("one_hots"), 1)
                for q in range(2 * TILES):
                    n = rows(q % TILES)
                    mm = pe.matmul(ps[:, 2, 0:CHUNKS + 1], one_slot[:n, q, :], one_chunk[:n, q, :],
                                   start=(q == 0), stop=(q == 2 * TILES - 1))
                mm.then_inc(sem("table_made"), 1)
                expert_products(pe)

            @block.scalar
            def _(act):
                act.wait_ge(sem("group_shifted"), 1)
                act.activation(exp4, exp4, ACT.Exp).then_inc(sem("group_exp"), 1)
                act.wait_ge(sem("diff_ready"), 1)
                act.activation(diff, diff, ACT.Exp).then_inc(sem("diff_exp"), 1)
                expert_silu(act)

            @block.vector
            def _(dve):
                chain = Chain(dve, sem("dve_chain"), count["dve"])

                def wide(v, n):
                    return v.unsqueeze(2).to_broadcast([P, TILES, n])

                def first_max(out, vals_, top, order, n):
                    c = cand4 if n == G_ else cand
                    chain(dve.tensor_reduce(top, vals_, AX.X, ALU.max))
                    chain(dve.tensor_tensor(c, vals_, wide(top, n), ALU.is_equal))
                    chain(dve.tensor_tensor(c, c, con(order).unsqueeze(1).to_broadcast([P, TILES, n]), ALU.mult))
                    chain(dve.tensor_reduce(c_max, c, AX.X, ALU.max))
                    chain(dve.tensor_tensor(out, c, wide(c_max, n), ALU.is_equal))

                lg, le = logits[:, :, 0:G_], logits[:, :, G_:G_ + E_]
                first_max(group4, lg, g_max, "down4", G_)
                dve.tensor_tensor(exp4, lg, wide(g_max, G_), ALU.subtract).then_inc(sem("group_shifted"), 1)
                chain(dve.tensor_scalar(cand4, group4, -NEG, NEG, ALU.mult, ALU.add))
                for t in range(TILES):
                    ins = dve.tensor_tensor(le_m[:, t].rearrange("p (g e) -> p g e", g=G_),
                                            le[:, t].rearrange("p (g e) -> p g e", g=G_),
                                            cand4[:, t].unsqueeze(2).to_broadcast([P, G_, E_ // G_]), ALU.add)
                chain(ins)
                first_max(chosen1, le_m, m1, "down32", E_)
                chain(dve.tensor_scalar(slot, chosen1, NEG, None, ALU.mult))
                chain(dve.tensor_tensor(le_m, le_m, slot, ALU.add))
                first_max(chosen2, le_m, m2, "down32", E_)
                dve.tensor_tensor(diff, m2, m1, ALU.subtract).then_inc(sem("diff_ready"), 1)
                chain(dve.tensor_scalar(valid7, con("token"), float(TOKENS), None, ALU.is_lt))
                chain(dve.tensor_tensor(both, chosen1, chosen2, ALU.add))
                dve.tensor_tensor(both, both, wide(valid7, E_), ALU.mult).then_inc(sem("counted"), 1)
                dve.wait_ge(sem("group_exp"), 1)
                chain(dve.tensor_reduce(sum4, exp4, AX.X, ALU.add))
                chain(dve.reciprocal(p_top, sum4))
                dve.wait_ge(sem("diff_exp"), 1)
                chain(dve.tensor_scalar(inv_d, diff, 1.0, None, ALU.add))
                chain(dve.reciprocal(inv_d, inv_d))
                chain(dve.tensor_tensor(first_w, inv_d, p_top, ALU.mult))
                chain(dve.tensor_tensor(second_w, first_w, diff, ALU.mult))
                dve.wait_ge(sem("prefixed"), 1)
                chain(dve.memset(base[:, 0, :], 0.0))
                for t in range(TILES):
                    chain(dve.tensor_tensor(base[:, t + 1, :], base[:, t, :], ps[:, 1, E_ * t:E_ * t + E_], ALU.add))
                chain(dve.tensor_tensor(steps7, base[:, TILES, :].unsqueeze(2).to_broadcast([P, E_, 9]),
                                        con("steps").unsqueeze(1).to_broadcast([P, E_, 9]), ALU.is_gt))
                chain(dve.tensor_reduce(n_chunk, steps7, AX.X, ALU.add))
                chain(dve.memset(ones32, 1.0))
                chain(dve.tensor_tensor_scan(cum, ones32, n_chunk, 0.0, ALU.mult, ALU.add))
                chain(dve.tensor_tensor(cum0, cum, n_chunk, ALU.subtract))
                chain(dve.tensor_scalar(cum0, cum0, float(P), None, ALU.mult))
                chain(dve.tensor_tensor(slot, base[:, 0:TILES, :],
                                        ps[:, 0, 0:288].rearrange("p (t n) -> p t n", n=E_), ALU.add))
                chain(dve.tensor_tensor(slot, slot, cum0.unsqueeze(1).to_broadcast([P, TILES, E_]), ALU.add))
                chain(dve.tensor_tensor(cand, slot, chosen1, ALU.mult))
                chain(dve.tensor_reduce(destf[:, 0:TILES], cand, AX.X, ALU.add))
                chain(dve.tensor_tensor(cand, slot, chosen2, ALU.mult))
                chain(dve.tensor_reduce(destf[:, TILES:2 * TILES], cand, AX.X, ALU.add))
                chain(dve.tensor_tensor(ends_le[0:1], cum[0:1].unsqueeze(1).to_broadcast([1, CHUNKS + 1, E_]),
                                        con("chunk", 1).unsqueeze(2).to_broadcast([1, CHUNKS + 1, E_]), ALU.is_le))
                chain(dve.tensor_reduce(chunk_f[0:1, 0:CHUNKS + 1], ends_le[0:1], AX.X, ALU.add))
                chain(dve.tensor_scalar(chunk_f[0:1, 0:CHUNKS + 1], chunk_f[0:1, 0:CHUNKS + 1], float(E_ - 1), None,
                                        ALU.min))
                dve.tensor_copy(row_ints[0:1, CHUNKS + 1:CHUNKS + 2], cum[0:1, E_ - 1:E_])
                dve.tensor_copy(row_ints[0:1, 0:CHUNKS + 1], chunk_f[0:1, 0:CHUNKS + 1]).then_inc(sem("plan_ready"), 1)
                dve.tensor_copy(dest, destf)
                chain(dve.tensor_scalar(dest_q, destf, 1.0 / P, None, ALU.mult))
                chunks = con("chunk").unsqueeze(1).to_broadcast([P, 2 * TILES, CHUNKS + 1])

                def every(v, n):
                    return v.unsqueeze(2).to_broadcast([P, 2 * TILES, n])

                chain(dve.tensor_tensor(one_chunk, chunks, every(dest_q, CHUNKS + 1), ALU.is_le))
                chain(dve.tensor_reduce(dest_c, one_chunk, AX.X, ALU.add))
                chain(dve.tensor_scalar(dest_c, dest_c, -1.0, None, ALU.add))
                chain(dve.tensor_tensor(one_chunk, chunks, every(dest_c, CHUNKS + 1), ALU.is_equal))
                for j in range(2):
                    o = slice(j * TILES, (j + 1) * TILES)
                    ins = dve.tensor_tensor(one_chunk[:, o], one_chunk[:, o],
                                            con("token").unsqueeze(2).to_broadcast([P, TILES, CHUNKS + 1]), ALU.mult)
                chain(dve.scalar_tensor_tensor(dest_q, dest_c, -float(P), destf, ALU.mult, ALU.add))
                dve.wait_ge(sem("lane_in"), 16)
                dve.tensor_tensor(one_slot, lane.unsqueeze(1).to_broadcast([P, 2 * TILES, P]),
                                  every(dest_q, P), ALU.is_equal).then_inc(sem("one_hots"), 1)
                dve.wait_ge(sem("table_made"), 1)
                dve.tensor_copy(row_of, ps[:, 2, 0:CHUNKS + 1]).then_inc(sem("table_ready"), 1)
                dve.wait_ge(sem("table_ready"), 1)
                expert_copies(dve)

            @block.gpsimd
            def _(pool):
                pool.wait_ge(sem("table_ready"), 1)
                expert_rows(pool)

        y_rows = flat(A1, 4096).rearrange("p (s j n) -> p s j n", s=2, j=2)
        final = flat(A1 + 4096, 2048).rearrange("p (s n) -> p s n", s=2)
        junk9 = flat(A1 + 6144, D)
        st9 = flat(A1 + 7168, 32).rearrange("p (q n) -> p q n", n=16)
        sd9, rs9 = st9[:, 0, :], st9[:, 1, :]
        ms9 = flat(A1 + 7200, 16)
        with nc.Block() as block:
            @block.gpsimd
            def _(pool):
                for t in range(TILES):
                    n = rows(t)
                    if t >= 2:
                        pool.wait_ge(sem("rows_summed"), t - 1)
                    for j in range(2):
                        idx = dest[:n, j * TILES + t:j * TILES + t + 1].bitcast(U32)
                        pool.indirect_dma_start(y_rows[:n, t % 2, j, :], None, scratch_y,
                                                bass.IndirectOffsetOnAxis(ap=idx, axis=0))\
                            .then_inc(sem(f"y_rows_in{t % 2}"), 16)

            @block.vector
            def _(dve):
                chain = Chain(dve, sem("dve_chain"), count["dve"])
                for t in range(TILES + 1):
                    if t < TILES:
                        n = rows(t)
                        dve.wait_ge(sem(f"y_rows_in{t % 2}"), 32 * (t // 2 + 1))
                        for j, w in enumerate((first_w, second_w)):
                            ins = dve.scalar_tensor_tensor(x_res[:n, t, :], y_rows[:n, t % 2, j, :], w[:n, t:t + 1],
                                                           x_res[:n, t, :], ALU.mult, ALU.add)
                            if j == 0:
                                chain(ins)
                        ins.then_inc(sem("rows_summed"), 1)
                    if t >= 1:
                        q, n = t - 1, rows(t - 1)
                        dve.wait_ge(sem("sd9_ready"), q + 1)
                        chain(dve.reciprocal(rs9[:n, q:q + 1], sd9[:n, q:q + 1]))
                        if q >= 2:
                            dve.wait_ge(sem(f"final_out{q % 2}"), 16 * (q // 2))
                        dve.scalar_tensor_tensor(final[:n, q % 2, :], x_res[:n, q, :], rs9[:n, q:q + 1],
                                                 final_g[:n, :], ALU.mult, ALU.mult).then_inc(sem("final_ready"), 1)

            @block.scalar
            def _(act):
                chain = Chain(act, sem("act_chain"), count["act"])
                for t in range(TILES):
                    n = rows(t)
                    act.wait_ge(sem("rows_summed"), t + 1)
                    chain(act.activation(junk9[:n, :], x_res[:n, t, :], ACT.Square, scale=1 / 32,
                                         accum_out=ms9[:n, t:t + 1]))
                    act.activation(sd9[:n, t:t + 1], ms9[:n, t:t + 1], ACT.Sqrt, bias=con("eps")[:n, 0:1])\
                       .then_inc(sem("sd9_ready"), 1)

            @block.sync
            def _(sp):
                for t in range(TILES):
                    sp.wait_ge(sem("final_ready"), t + 1)
                    dst = out["out0"][P * t:P * t + P, :] if t < NQ else out["out1"]
                    sp.dma_start(dst, final[:rows(t), t % 2, :]).then_inc(sem(f"final_out{t % 2}"), 16)
                sp.wait_ge(sem("final_out0"), 16 * 5)
                sp.wait_ge(sem("final_out1"), 16 * 4)


OUT_SHAPES = {
    "out0": (SEQ, D), "out1": (NB * NS, D),
    "out2": (SEQ, 256), "out3": (NB * NS, 256), "out4": (SEQ, 256), "out5": (NB * NS, 256),
    "out6": (512, 256), "out7": (NB, 512, 256), "out8": (TAPS - 1, CH), "out9": (NB, TAPS - 1, CH),
}


def kernel(**inputs):
    import concourse.bacc as bacc
    from concourse.bass_utils import run_bass_kernel_spmd

    x = {k: np.asarray(v) for k, v in inputs.items()}
    d = {
        "x_prompt": x["x_prompt"], "x_sample": x["x_sample"], "consts": const_table()[0],
        "ln1": x["ln1"][0], "ln2": x["ln2"][0], "ln_final": x["ln_final"],
        "w_in": x["w_in"][0], "w_out": x["w_out"][0],
        "conv_g": x["conv_ln_g"][0], "conv_b": x["conv_ln_b"][0],
        "norm_conv": x["out_norm_conv"][0], "norm_att": x["out_norm_att"][0],
        "w_gate": x["w_exp_gate"][0], "w_up": x["w_exp_up"][0], "w_down": x["w_exp_down"][0],
        "state_conv": x["state_conv"][0], "state_win": x["state_win_kv"][0].reshape(NB, 512, 256),
        "page_table": x["page_table"].reshape(1, NB * PAGES),
    }
    taps = np.concatenate([x["conv_dw_w"][0], x["conv_dw_b"]], axis=0)
    d["dw"] = taps.reshape(TAPS + 1, 4, P).transpose(2, 1, 0).reshape(P, 4 * (TAPS + 1))
    d["state_conv_T"] = d["state_conv"].reshape(NB, TAPS - 1, 4, P).transpose(3, 2, 1, 0).reshape(P, -1)

    w = d["w_in"]
    q = w[:, D:D + 512].reshape(D, KV, R, HD).transpose(0, 2, 1, 3).reshape(D, 512)
    kv = w[:, D + 512:D + 1280].reshape(D, 3, KV, 2, HD).transpose(0, 1, 3, 2, 4).reshape(D, 768)
    d["w_in"] = np.concatenate([w[:, :D], q, kv, w[:, D + 1280:]], axis=1)

    def by_use(kv):
        kv = kv.reshape(-1, P, KV, 2, HD)
        keys = kv[:, :, :, 0].transpose(0, 2, 3, 1).reshape(-1, P, P)
        return np.concatenate([keys, kv[:, :, :, 1].reshape(-1, P, P)], axis=2)

    d["cache_sel"] = by_use(x["cache_sel_kv"][0])
    d["state_win_use"] = by_use(d["state_win"])
    cmp = x["cache_cmp_kv"][0].reshape(-1, 2, CMP // 2, 2, KV, 2, HD)
    d["cache_cmp"] = cmp.transpose(0, 3, 6, 5, 2, 1, 4).reshape(-1, P, 256)
    d["state_win"] = d["state_win"].reshape(NB, 512, KV, 2, HD).transpose(0, 1, 3, 2, 4).reshape(NB, 512, 256)
    w1 = np.stack([x["w_cmp_k1"][0], x["w_cmp_v1"][0]]).reshape(2, CMP // 2, 2, HD, P)
    d["w_cmp1"] = w1.transpose(2, 3, 0, 1, 4).reshape(P, 2 * CMP // 2 * P)
    pe = x["cmp_pos_emb"][0].reshape(CMP // 2, 2, 2, HD).transpose(1, 3, 2, 0).reshape(P, 64)
    d["pos_emb"] = np.repeat(pe, 4, axis=1)
    wk2 = x["w_cmp_k2"][0]
    zero = np.zeros_like(wk2)
    d["w_cmp2"] = np.concatenate([wk2, zero, zero, wk2, x["w_cmp_v2"][0]], axis=1)
    router = np.concatenate([x["w_router_group"][0], x["w_router_expert"][0]], axis=1)
    d["w_router"] = router.reshape(P, KT_ * 36)

    nc = bacc.Bacc("TRN2", target_bir_lowering=False, num_devices=1)
    arrays, args = {}, {}
    for name, v in d.items():
        v = np.ascontiguousarray(v)
        arrays[f"in_{name}"] = v
        args[name] = nc.dram_tensor(f"in_{name}", v.shape, mybir.dt.from_np(v.dtype), kind="ExternalInput").ap()
    for name, shape in OUT_SHAPES.items():
        args[name] = nc.dram_tensor(name, shape, F32, kind="ExternalOutput").ap()
    build(nc, args)
    r = run_bass_kernel_spmd(nc, [arrays], core_ids=[0]).results[0]
    shapes = [(1, SEQ, D), (NB, NS, D), (1, 1, SEQ, KV, 2, HD), (1, NB, NS, KV, 2, HD),
              (1, 1, SEQ, KV, 2, HD), (1, NB, NS, KV, 2, HD), (1, 1, 512, KV, 2, HD),
              (1, NB, 512, KV, 2, HD), (1, 1, TAPS - 1, CH), (1, NB, TAPS - 1, CH)]
    outs = []
    for i, s in enumerate(shapes):
        o = np.asarray(r[f"out{i}"])
        if s[-1] == HD:
            o = o.reshape(s[:-3] + (2, KV, HD)).swapaxes(-3, -2)
        outs.append(o.reshape(s))
    return tuple(outs)
```

```python
from contextlib import ExitStack

import concourse.bass as bass
import numpy as np
from concourse import mybir

ALU = mybir.AluOpType
ACT = mybir.ActivationFunctionType
AX = mybir.AxisListType
F32 = mybir.dt.float32
I32 = mybir.dt.int32
U32 = mybir.dt.uint32

P = 128
D = 1024
SEQ = 1024
NB, NS = 8, 4
PAST = 2048
PAGE = 128
CH, TAPS = 512, 31
KV, R, HD = 2, 4, 64
HALF_ROT = 8
COLS_TM = 512 + 768 + 24
KT_ = D // P
TILES = 9
NQ = 8
TOKENS = SEQ + NB * NS
SCALE = HD ** -0.5
NEG = -1e30
CMP = 64
PBLK = SEQ // CMP
SBLK = PAST // CMP
NSEL = 16
PAGES = PAST // PAGE
HALF = 4 * PAGES
EXPERTS, GROUPS, DE = 32, 4, 512
CHUNKS = (2 * TOKENS) // P + EXPERTS
RMS_EPS, LN_EPS = 1e-6, 1e-5


def rows(t):
    return P if t < NQ else NB * NS


def const_table():
    parts, at = [], {}

    def put(name, a):
        full = np.zeros((P, a.shape[1]), np.float32)
        full[:a.shape[0]] = a
        at[name] = (sum(x.shape[1] for x in parts), a.shape[1])
        parts.append(full)

    p = np.arange(P)
    put("ident", np.eye(P))
    put("causal", np.where(p[None, :] <= p[:, None], 0.0, NEG))
    put("low", np.where(p[None, :] > p[:, None], 0.0, NEG))
    pos = np.concatenate([np.arange(SEQ), np.resize(PAST + np.arange(NS), P)]).astype(np.float32)
    inv = np.float32(500000.0) ** (-np.arange(HALF_ROT, dtype=np.float32) / np.float32(HALF_ROT))
    ang = (pos[:, None] * inv.astype(np.float32)).astype(np.float32).reshape(TILES, P, HALF_ROT)
    rope = np.concatenate([np.cos(ang), np.sin(ang)], axis=2)
    put("rope", rope.transpose(1, 0, 2).reshape(P, TILES * 16))
    q = np.arange(SEQ).reshape(NQ, P).T
    valid = ((np.arange(PBLK) + 1) * CMP - 1)[None, None, :] <= q[:, :, None]
    put("cmp_ok", valid.reshape(P, NQ * PBLK))
    put("eps", np.tile(np.array([[RMS_EPS, LN_EPS]]), (P, 1)))
    b4, g, r, t = p // 32, p // 16 % 2, p // 4 % 4, p % 4
    own = np.full((P, 2, NB, NS), NEG)
    for half in range(2):
        for i in range(P):
            own[i, half, 4 * half + b4[i], :t[i] + 1] = 0.0
    put("own", own.reshape(P, 64))
    put("win", np.where(np.arange(512)[None, :] > t[:, None], 0.0, NEG))
    put("same_query", (b4[:, None] == b4) & (g[:, None] == g) & (t[:, None] == t))
    pick = np.zeros((NB * NS, 2, P))
    for half in range(2):
        pick[(4 * half + b4) * NS + t, half, p] = 1.0
    put("pick_token", pick.reshape(NB * NS, 2 * P))
    put("own_head", np.arange(8)[None, :] == (g * R + r)[:, None])
    put("rep_block", np.arange(PBLK)[:, None] == (p % PBLK)[None, :])
    put("before", p[:, None] < p[None, :])
    put("ones", np.ones((P, P)))
    put("down4", np.tile(GROUPS - np.arange(GROUPS), (P, 1)))
    put("down32", np.tile(EXPERTS - np.arange(EXPERTS), (P, 1)))
    put("token", (np.arange(TILES)[None, :] * P + p[:, None]).astype(np.float32))
    put("steps", np.tile(128.0 * np.arange(9), (P, 1)))
    put("chunk", np.tile(np.arange(CHUNKS + 1, dtype=np.float32), (P, 1)))
    small = sum(x.shape[1] for x in parts)
    put("lane", np.tile(np.arange(P, dtype=np.float32), (P, 1)))
    n = np.arange(SBLK)
    put("earlier", np.tile((n[None, :] < n[:, None]).reshape(1, -1), (P, 1)))
    put("own_block", (p // PBLK)[:, None] == (np.arange(512) // HD)[None, :])
    return np.concatenate(parts, axis=1), at, small


class Chain:

    def __init__(self, eng, sem, count):
        self.eng, self.sem, self.count = eng, sem, count

    def __call__(self, ins):
        self.count[0] += 1
        ins.then_inc(self.sem, 1)
        self.eng.wait_ge(self.sem, self.count[0])


def build(nc, a):
    _, const_at, const_small = const_table()
    with ExitStack() as ctx:
        arena = ctx.enter_context(nc.sbuf_tensor("arena", [P, 52900], F32))
        ints = ctx.enter_context(nc.sbuf_tensor("ints", [P, 104], I32))
        page_row = ctx.enter_context(nc.sbuf_tensor("page_row", [1, NB * PAGES], I32))[:]
        row_ints = ctx.enter_context(nc.sbuf_tensor("row_ints", [1, 64], I32))
        ps = ctx.enter_context(nc.psum_tensor("ps", [P, 8, 512], F32))
        scratch_h = nc.dram_tensor("scratch_h", [TOKENS, D], F32, kind="Internal").ap()
        scratch_y = nc.dram_tensor("scratch_y", [1 + 2 * TOKENS, D], F32, kind="Internal").ap()
        scratch_first = nc.dram_tensor("scratch_first", [2, 16], F32, kind="Internal").ap()
        semaphores = {}

        def sem(name):
            if name not in semaphores:
                semaphores[name] = nc.alloc_semaphore(name)
            return semaphores[name]

        def reuse_semaphores():
            done = [semaphores.pop(name) for name in list(semaphores) if not name.endswith("_chain")]
            nc.clear_and_free_semaphores(done)
            with nc.Block():
                pass

        top = [0]

        def take(n):
            top[0] += n
            return top[0] - n

        def flat(off, n):
            return arena[:, off:off + n]

        CON = flat(take(const_small), const_small)
        gain = flat(take(2560), 2560)
        small = flat(take(640), 640)
        A2 = take(8448)
        A1 = take(18688)
        A3 = take(4656)
        A4 = take(5304)
        AQ = take(8192)
        AC = take(2000)

        def con(name, n=P):
            o, w = const_at[name]
            return CON[:n, o:o + w]

        ident = con("ident")
        used = [0]

        def stat(n):
            used[0] += n
            return small[:, used[0] - n:used[0]]

        gates = stat(TILES * 24).rearrange("p (t c) -> p t c", c=24)
        xT = flat(A2, 8448).rearrange("p (k n) -> p k n", k=KT_)
        w_tm = flat(A1, KT_ * COLS_TM).rearrange("p (k n) -> p k n", k=KT_)
        x_all = flat(A1, TILES * D).rearrange("p (t n) -> p t n", n=D)
        w_conv = flat(A1 + KT_ * COLS_TM, KT_ * D).rearrange("p (k n) -> p k n", k=KT_)
        acc = flat(A1 + KT_ * COLS_TM, 4 * TOKENS).rearrange("p (c n) -> p c n", c=4)
        tap_product = flat(A1 + KT_ * COLS_TM + 4 * TOKENS, TOKENS)
        xin = flat(A3, 2048).rearrange("p (s n) -> p s n", s=2)
        p_sb = flat(A3 + 2048, 2608).rearrange("p (s n) -> p s n", s=2)
        xn = flat(AQ, 2048).rearrange("p (s n) -> p s n", s=2)
        a_p = flat(A4, 4 * (SEQ + TAPS - 1)).rearrange("p (c n) -> p c n", c=4)
        a_s = flat(A4 + 4 * (SEQ + TAPS - 1), 4 * NB * 34).rearrange("p (c n b) -> p c n b", c=4, b=NB)
        qT = flat(AQ, 4096).rearrange("p (r n) -> p r n", r=R)
        kT = flat(AQ + 4096, 2048).rearrange("p (w n) -> p w n", w=2)
        vals = flat(AQ + 6144, 2048).rearrange("p (t w n) -> p t w n", t=NQ, w=2)
        kcT_s = flat(AC, 256)
        vc_s = flat(AC + 256, 1024).rearrange("p (b n) -> p b n", b=NB)
        vc_p = flat(AC + 1296, 128)
        q_diag = flat(AC + 1424, 256).rearrange("p (b n) -> p b n", b=NB)
        kT_new = flat(AC + 1680, 64).rearrange("p (w n) -> p w n", w=2)
        v_new = flat(AC + 1744, 256).rearrange("p (w n) -> p w n", w=2)
        pages = flat(A1, 18688).rearrange("p (s n) -> p s n", n=256)
        dw = stat(128).rearrange("p (c n) -> p c n", c=4)
        kcT_p = stat(2 * PBLK)
        ms, sd, rstd = stat(TILES), stat(TILES), stat(TILES)

        out = {k: v for k, v in a.items() if k.startswith("out")}
        x_rows = [a["x_prompt"][0, P * t:P * t + P, :] for t in range(NQ)]
        x_rows.append(a["x_sample"].rearrange("b s d -> (b s) d"))

        count = {k: [0] for k in ("dve", "act", "pool")}
        rope_tmp = flat(take(256), 256)
        NW = 352
        sig = flat(A3 + 2048, 2 * NW).rearrange("p (s n) -> p s n", s=2)
        with nc.Block() as block:
            @block.sync
            def _(sp):
                for t in range(TILES):
                    sp.dma_start(x_all[:rows(t), t, :], x_rows[t]).then_inc(sem(f"x_in{t}"), 16)
                    if t == 1:
                        sp.dma_start(CON, a["consts"][:, 0:const_small]).then_inc(sem("const_in"), 16)
                        sp.dma_start(gain[:, 0:D], a["ln1"].partition_broadcast(P)).then_inc(sem("ln1_in"), 16)
                sp.dma_start(w_conv, a["w_in"].rearrange("(p k) n -> p k n", k=KT_)[:, :, 0:D])\
                  .then_inc(sem("w_conv_in"), 16)
                sp.dma_start(dw, a["dw"].rearrange("p (c n) -> p c n", c=4)).then_inc(sem("dw_in"), 16)
                sp.dma_start(a_s[:, :, 0:TAPS - 1, :],
                             a["state_conv_T"].rearrange("p (c n b) -> p c n b", c=4, b=NB)).then_inc(sem("dw_in"), 16)
                sp.dma_start(page_row, a["page_table"]).then_inc(sem("page_table_in"), 16)
                sp.wait_ge(sem("xn_ready"), TILES)
                sp.dma_start(w_tm, a["w_in"].rearrange("(p k) n -> p k n", k=KT_)[:, :, D:D + COLS_TM])\
                  .then_inc(sem("w_tm_in"), 16)
                sp.dma_start(out["out9"][:, 0:TAPS - 1 - NS, :], a["state_conv"][:, NS:TAPS - 1, :])\
                  .then_inc(sem("state_out"), 16)
                sp.dma_start(out["out7"][:, 0:512 - NS, :], a["state_win"][:, NS:512, :])\
                  .then_inc(sem("state_out"), 16)
                sp.wait_ge(sem("state_out"), 32)
                sp.wait_ge(sem("w_tm_in"), 16)
                sp.wait_ge(sem("dw_in"), 32)

            @block.tensor
            def _(pe):
                pe.wait_ge(sem("const_in"), 16)
                for t in range(TILES):
                    n = rows(t)
                    pe.wait_ge(sem("xn_ready"), t + 1)
                    if t >= 2:
                        pe.wait_ge(sem("xT_act"), t - 1)
                        pe.wait_ge(sem("xT_dve"), t - 1)
                    xv = xn[:n, t % 2, :].rearrange("p (m k) -> p k m", k=KT_)
                    for k in range(KT_):
                        mm = pe.transpose(ps[:, 2 * (t % 2) + k // 4, (k % 4) * P:(k % 4) * P + n],
                                          xv[:, k, :], ident[:n, :n])
                    mm.then_inc(sem("x_turned"), 1)
                pe.wait_ge(sem("xT_act"), TILES)
                pe.wait_ge(sem("xT_dve"), TILES)
                pe.wait_ge(sem("w_conv_in"), 16)
                for u in range(12):
                    j, c = u // 4, u % 4
                    if u >= 2:
                        pe.wait_ge(sem("glu_done"), u - 1)
                    for half in range(2):
                        for k in range(KT_):
                            mm = pe.matmul(ps[:, 4 + 2 * (u % 2) + half, 0:NW],
                                           w_conv[:, k, half * CH + c * P:half * CH + c * P + P],
                                           xT[:, k, j * NW:(j + 1) * NW], start=(k == 0), stop=(k == KT_ - 1))
                    mm.then_inc(sem("conv_projected"), 1)
                pe.wait_ge(sem("w_tm_in"), 16)
                pe.wait_ge(sem("glu_done"), 12)

                def turn(t):
                    n = rows(t)
                    pe.wait_ge(sem("roped"), t + 1)
                    if t >= 1:
                        pe.wait_ge(sem("qk_copied"), t)
                        pe.wait_ge(sem("cmp_copied"), t)
                    s = p_sb[:n, t % 2, :]
                    for r in range(R):
                        pe.transpose(ps[:, 6, r * P:r * P + n], s[:, r * P:(r + 1) * P], ident[:n, :n])
                    for w in range(2):
                        o = 512 + 256 * (w + 1)
                        mm = pe.transpose(ps[:, 7, w * P:w * P + n], s[:, o:o + P], ident[:n, :n])
                    mm.then_inc(sem("qk_turned"), 1)
                    if t < NQ:
                        pe.wait_ge(sem("qk_copied"), t + 1)
                        pe.wait_ge(sem("doubled"), t + 1)
                        for o in range(0, 512, P):
                            mm = pe.transpose(ps[:, 6, o:o + P], xin[:, t % 2, o:o + P], ident)
                        mm.then_inc(sem("cmp_turned"), 1)

                for t in range(TILES):
                    n, b = rows(t), 3 * (t % 2)
                    if t >= 2:
                        pe.wait_ge(sem("tm_copied"), t - 1)
                    for o, w in ((0, 512), (512, 512), (1024, COLS_TM - 1024)):
                        for k in range(KT_):
                            mm = pe.matmul(ps[:n, b + o // 512, 0:w], xT[:, k, t * P:t * P + n],
                                           w_tm[:, k, o:o + w], start=(k == 0), stop=(k == KT_ - 1))
                    mm.then_inc(sem("tm_projected"), 1)
                    if t >= 1:
                        turn(t - 1)
                turn(TILES - 1)
                pe.wait_ge(sem("tm_copied"), TILES)
                for c in range(4):
                    pe.transpose(ps[:TAPS - 1, 0, c * P:(c + 1) * P], a_p[:, c, SEQ:SEQ + TAPS - 1], ident)
                for c in range(4):
                    mm = pe.transpose(ps[:NB * NS, 1, c * P:(c + 1) * P], a_s[:, c, TAPS - 1:, :], ident)
                mm.then_inc(sem("state_turned"), 1)

            DVE_CHANNELS = 3

            def last_channel_taps(t):
                return range(min(TAPS, 4 * t), min(TAPS, 4 * t + 4))

            def scale_tap(act, j):
                c = DVE_CHANNELS
                o = acc[:, c, :] if j == 0 else tap_product
                bias = dw[:, c, TAPS:TAPS + 1] if j == 0 else 0.0
                if j == 0:
                    act.wait_ge(sem("dw_in"), 32)
                    act.wait_ge(sem("pad_zero"), 1)
                if j >= 2:
                    act.wait_ge(sem("tap_added"), j - 1)
                act.activation(o[:, 0:SEQ], a_p[:, c, j:j + SEQ], ACT.Identity, bias=bias, scale=dw[:, c, j:j + 1])
                act.activation(o[:, SEQ:TOKENS].rearrange("p (b s) -> p s b", s=NS), a_s[:, c, j:j + NS, :],
                               ACT.Identity, bias=bias, scale=dw[:, c, j:j + 1]).then_inc(sem("tap_scaled"), 1)

            @block.scalar
            def _(act):
                chain = Chain(act, sem("act_chain"), count["act"])
                act.wait_ge(sem("const_in"), 16)
                for t in range(TILES + 1):
                    if t < TILES:
                        n = rows(t)
                        act.wait_ge(sem(f"x_in{t}"), 16)
                        chain(act.activation(p_sb[:n, 1, 0:D], x_all[:n, t, :], ACT.Square, scale=1 / 32,
                                             accum_out=ms[:n, t:t + 1]))
                        act.activation(sd[:n, t:t + 1], ms[:n, t:t + 1], ACT.Sqrt,
                                       bias=con("eps")[:n, 0:1]).then_inc(sem("sd_ready"), 1)
                    if t >= 1:
                        n, b = rows(t - 1), 2 * ((t - 1) % 2)
                        act.wait_ge(sem("x_turned"), t)
                        act.activation(xT[:, 0:4, (t - 1) * P:(t - 1) * P + n],
                                       ps[:, b, :].rearrange("p (k m) -> p k m", k=4)[:, :, 0:n],
                                       ACT.Copy).then_inc(sem("xT_act"), 1)
                for u in range(12):
                    act.wait_ge(sem("conv_projected"), u + 1)
                    if u >= 2:
                        act.wait_ge(sem("glu_done"), u - 1)
                    act.activation(sig[:, u % 2, :], ps[:, 5 + 2 * (u % 2), 0:NW], ACT.Sigmoid)\
                       .then_inc(sem("sig_ready"), 1)
                act.wait_ge(sem("glu_done"), 12)

                def turn_copy(t):
                    n = rows(t)
                    act.wait_ge(sem("qk_turned"), t + 1)
                    if t < NQ:
                        act.activation(qT[:, :, t * P:t * P + P], ps[:, 6, :].rearrange("p (r m) -> p r m", r=R),
                                       ACT.Copy, scale=SCALE)
                        act.activation(kT[:, :, t * P:t * P + P],
                                       ps[:, 7, 0:2 * P].rearrange("p (w m) -> p w m", w=2),
                                       ACT.Copy).then_inc(sem("qk_copied"), 1)
                    else:
                        act.wait_ge(sem("diag_zero"), 1)
                        for g in range(KV):
                            src = ps[64 * g:64 * g + 64, 6, :].rearrange("p (r m) -> p r m", r=R)[:, :, 0:n]
                            act.activation(
                                q_diag[64 * g:64 * g + 64, :, 16 * g:16 * g + 16].rearrange(
                                    "p b (r s) -> p r b s", r=R),
                                src.rearrange("p r (b s) -> p r b s", s=NS), ACT.Copy, scale=SCALE)
                        act.activation(kT_new[:, :, :],
                                       ps[:, 7, 0:2 * P].rearrange("p (w m) -> p w m", w=2)[:, :, 0:n],
                                       ACT.Copy).then_inc(sem("qk_copied"), 1)

                for t in range(TILES):
                    n, b = rows(t), 3 * (t % 2)
                    act.wait_ge(sem("tm_projected"), t + 1)
                    if t >= 2:
                        act.wait_ge(sem(f"rows_out{t % 2}"), 32 * (t // 2))
                        if t >= 6:
                            act.wait_ge(sem(f"win_out{t % 2}"), 16 * (t // 2 - 2))
                        act.wait_ge(sem("cmp_turned"), t - 1)
                        act.wait_ge(sem("v_copied"), t - 1)
                    act.activation(p_sb[:n, t % 2, 0:512], ps[:n, b, :], ACT.Copy)
                    act.activation(p_sb[:n, t % 2, 512:1024], ps[:n, b + 1, :], ACT.Copy)
                    act.activation(p_sb[:n, t % 2, 1024:1280], ps[:n, b + 2, 0:256], ACT.Copy)
                    act.activation(gates[:n, t, :], ps[:n, b + 2, 256:280], ACT.Sigmoid)\
                       .then_inc(sem("tm_copied"), 1)
                    if t >= 1:
                        turn_copy(t - 1)
                    for j in last_channel_taps(t):
                        scale_tap(act, j)
                turn_copy(TILES - 1)
                act.wait_ge(sem("state_turned"), 1)
                act.wait_ge(sem("qk_turned"), TILES)
                act.activation(xin[:TAPS - 1, 0, 0:512], ps[:TAPS - 1, 0, :], ACT.Copy)
                act.activation(xin[:NB * NS, 1, 0:512], ps[:NB * NS, 1, :], ACT.Copy)\
                   .then_inc(sem("state_ready"), 1)

            def keep_as_page(dve, t):
                dve.wait_ge(sem("cmp_turned"), t + 1)
                if t == 0:
                    dve.wait_ge(sem("glu_done"), 12)
                for v in range(2):
                    for par in range(2):
                        o = pages[64 * par:64 * par + 64, HALF + t, 128 * v:128 * v + 128].rearrange(
                            "p (l b g) -> p g b l", b=2, g=KV)
                        for g in range(KV):
                            i = ps[64 * par:64 * par + 64, 6, (2 * v + g) * P:(2 * v + g + 1) * P].rearrange(
                                "p (b l q) -> p q b l", b=2, q=2)[:, par]
                            ins = dve.tensor_copy(o[:, g], i)
                ins.then_inc(sem("cmp_copied"), 1)

            @block.vector
            def _(dve):
                chain = Chain(dve, sem("dve_chain"), count["dve"])
                dve.wait_ge(sem("ln1_in"), 16)
                for t in range(TILES + 1):
                    if t < TILES:
                        n = rows(t)
                        dve.wait_ge(sem("sd_ready"), t + 1)
                        chain(dve.reciprocal(rstd[:n, t:t + 1], sd[:n, t:t + 1]))
                        if t >= 2:
                            dve.wait_ge(sem("x_turned"), t - 1)
                        dve.scalar_tensor_tensor(xn[:n, t % 2, :], x_all[:n, t, :], rstd[:n, t:t + 1],
                                                 gain[:n, 0:D], ALU.mult, ALU.mult).then_inc(sem("xn_ready"), 1)
                    if t >= 1:
                        n, b = rows(t - 1), 2 * ((t - 1) % 2) + 1
                        dve.wait_ge(sem("x_turned"), t)
                        dve.tensor_copy(xT[:, 4:8, (t - 1) * P:(t - 1) * P + n],
                                        ps[:, b, :].rearrange("p (k m) -> p k m", k=4)[:, :, 0:n])\
                           .then_inc(sem("xT_dve"), 1)
                dve.wait_ge(sem("dw_in"), 32)
                for u in range(12):
                    j, c = u // 4, u % 4
                    dve.wait_ge(sem("sig_ready"), u + 1)
                    m = min(SEQ - j * NW, NW)
                    gl = dve.tensor_tensor(a_p[:, c, TAPS - 1 + j * NW:TAPS - 1 + j * NW + m],
                                           ps[:, 4 + 2 * (u % 2), 0:m], sig[:, u % 2, 0:m], ALU.mult)
                    if m < NW:
                        gl = dve.tensor_tensor(a_s[:, c, TAPS - 1:, :],
                                               ps[:, 4 + 2 * (u % 2), m:NW].rearrange("p (b s) -> p s b", s=NS),
                                               sig[:, u % 2, m:NW].rearrange("p (b s) -> p s b", s=NS), ALU.mult)
                    gl.then_inc(sem("glu_done"), 1)
                dve.wait_ge(sem("pad_zero"), 1)
                dve.wait_ge(sem("glu_done"), 12)

                def tap(c, j):
                    views = ((acc[:, c, 0:SEQ], a_p[:, c, j:j + SEQ]),
                             (acc[:, c, SEQ:TOKENS].rearrange("p (b s) -> p s b", s=NS), a_s[:, c, j:j + NS, :]))
                    for o, i in views:
                        if j == 0:
                            ins = dve.tensor_scalar(o, i, dw[:, c, 0:1], dw[:, c, TAPS:TAPS + 1], ALU.mult, ALU.add)
                        else:
                            ins = dve.scalar_tensor_tensor(o, i, dw[:, c, j:j + 1], o, ALU.mult, ALU.add)
                        ins.then_inc(sem("tapped"), 1)
                    tapped[0] += 2

                tapped = [0]
                taps = [(c, j) for j in range(TAPS) for c in range(DVE_CHANNELS)]
                for t in range(TILES):
                    n = rows(t)
                    dve.wait_ge(sem("tm_copied"), t + 1)
                    cs = con("rope")[:n, 16 * t:16 * t + 16]
                    heads = ((p_sb[:n, t % 2, 0:512].rearrange("p (h d) -> p h d", d=HD), 8),
                             (p_sb[:n, t % 2, 512:1280].rearrange("p (w v d) -> p v w d", w=3, v=2)[:, 0], 6))
                    for s, h in heads:
                        if h == 6:
                            s = s.rearrange("p w (g d) -> p w g d", g=KV)
                            x1, x2 = s[:, :, :, 0:8], s[:, :, :, 8:16]
                            cos = cs[:, 0:8].unsqueeze(1).unsqueeze(1).to_broadcast([n, 3, KV, 8])
                            sin = cs[:, 8:16].unsqueeze(1).unsqueeze(1).to_broadcast([n, 3, KV, 8])
                            tmp = [rope_tmp[:n, 64 * q:64 * q + 48].rearrange("p (w g d) -> p w g d", w=3, g=KV)
                                   for q in range(4)]
                        else:
                            x1, x2 = s[:, :, 0:8], s[:, :, 8:16]
                            cos = cs[:, 0:8].unsqueeze(1).to_broadcast([n, h, 8])
                            sin = cs[:, 8:16].unsqueeze(1).to_broadcast([n, h, 8])
                            tmp = [rope_tmp[:n, 64 * q:64 * q + 64].rearrange("p (h d) -> p h d", d=8)
                                   for q in range(4)]
                        dve.tensor_tensor(tmp[0], x1, cos, ALU.mult)
                        dve.tensor_tensor(tmp[1], x2, sin, ALU.mult)
                        dve.tensor_tensor(tmp[2], x1, sin, ALU.mult)
                        chain(dve.tensor_tensor(tmp[3], x2, cos, ALU.mult))
                        dve.tensor_tensor(x1, tmp[0], tmp[1], ALU.subtract)
                        ins = dve.tensor_tensor(x2, tmp[2], tmp[3], ALU.add)
                        if h == 8:
                            chain(ins)
                        else:
                            ins.then_inc(sem("roped"), 1)
                    dve.wait_ge(sem("roped"), t + 1)
                    if t >= 1:
                        keep_as_page(dve, t - 1)
                    for c, j in taps[12 * t:12 * t + 12]:
                        if tapped[0] >= 2 * DVE_CHANNELS:
                            dve.wait_ge(sem("tapped"), tapped[0] - 2 * DVE_CHANNELS + 2)
                        tap(c, j)
                dve.wait_ge(sem("tapped"), tapped[0])

            @block.gpsimd
            def _(pool):
                pool.memset(a_p[:, :, 0:TAPS - 1], 0.0).then_inc(sem("pad_zero"), 1)
                pool.memset(q_diag, 0.0).then_inc(sem("diag_zero"), 1)
                for t in range(TILES):
                    n = rows(t)
                    pool.wait_ge(sem("roped"), t + 1)
                    s = p_sb[:n, t % 2, 512:1280].rearrange("p (w n) -> p w n", w=3)
                    vv = s.rearrange("p w (v n) -> p w v n", v=2)
                    if t < NQ:
                        if t >= 2:
                            pool.wait_ge(sem("cmp_turned"), t - 1)
                        dup = xin[:, t % 2, 0:512].rearrange("p (h q d) -> p h q d", q=2, d=HD)
                        for q in range(2):
                            ins = pool.tensor_copy(dup[:, :, q], s[:, 0, :].rearrange("p (h d) -> p h d", d=HD))
                        ins.then_inc(sem("doubled"), 1)
                        pool.tensor_copy(vals[:n, t, :, :], vv[:, 1:3, 1])\
                            .then_inc(sem("v_copied"), 1)
                        dst = [out["out2"][P * t:P * t + P], out["out4"][P * t:P * t + P],
                               out["out6"][P * (t - 4):P * (t - 3)] if t >= 4 else None]
                    else:
                        pool.tensor_copy(v_new[:n, :, :], vv[:, 1:3, 1])\
                            .then_inc(sem("v_copied"), 1)
                        dst = [out["out3"], out["out5"], out["out7"][:, 512 - NS:512, :]]
                    for w in range(3):
                        if dst[w] is not None:
                            pool.dma_start(dst[w], s[:, w, :])\
                                .then_inc(sem(f"win_out{t % 2}" if w == 2 else f"rows_out{t % 2}"), 16)
                    for j in last_channel_taps(t):
                        if j >= 1:
                            pool.wait_ge(sem("tap_scaled"), j + 1)
                            if j >= 2:
                                pool.wait_ge(sem("tap_added"), j - 1)
                            pool.tensor_tensor(acc[:, DVE_CHANNELS, :], acc[:, DVE_CHANNELS, :], tap_product, ALU.add)\
                                .then_inc(sem("tap_added"), 1)
                pool.wait_ge(sem("tap_added"), TAPS - 1)
                pool.wait_ge(sem("state_ready"), 1)
                pool.dma_start(out["out8"], xin[:TAPS - 1, 0, 0:512]).then_inc(sem("conv_out"), 16)
                for s in range(NS):
                    pool.dma_start(out["out9"][:, TAPS - 1 - NS + s, :], xin[NB * s:NB * (s + 1), 1, 0:512])\
                        .then_inc(sem("conv_out"), 16)
                pool.wait_ge(sem("conv_out"), 16 * (1 + NS))
                pool.wait_ge(sem("rows_out0"), 32 * 5)
                pool.wait_ge(sem("rows_out1"), 32 * 4)
                pool.wait_ge(sem("win_out0"), 16 * 3)
                pool.wait_ge(sem("win_out1"), 16 * 2)

        conv = flat(A2, TILES * CH).rearrange("p (t n) -> p t n", n=CH)
        A2b = A2 + TILES * CH
        cg, cb, cn = gain[:, D:D + CH], gain[:, D + CH:D + 2 * CH], gain[:, D + 2 * CH:D + 3 * CH]
        bn = flat(A2b + 1500, TILES * 6).rearrange("p (t n) -> p t n", n=6)
        mv = flat(A2b + 1564, TILES * 2).rearrange("p (t n) -> p t n", n=2)
        csd, crs, css = (flat(A2b + 1596 + 16 * q, TILES) for q in range(3))
        junk = flat(A2b + 1700, CH)
        w_cmp1 = flat(A3, 8192).rearrange("p (v l h) -> p v l h", v=2, l=CMP // 2)
        sil = flat(A2b, 2 * 544).rearrange("p (v n) -> p v n", v=2)
        w_cmp2 = flat(A2b + 1088, 320)
        cmp_bias = flat(A2b + 1408, 2)

        def load_pages(eng, cache, first, b, event, part=slice(0, 256), spare=None):
            into, step, base = (pages_flat, 256, b * PAGES * 256 + part.start) if spare is None else (spare, 128, 0)
            with eng.Fori(0, PAGES // 4) as s:
                places = [eng.value_load(page_row[0:1, bass.ds(s * 4 + (first + q), 1)],
                                         min_val=0, max_val=cache.shape[0] - 1) for q in range(4)]
                for q, place in enumerate(places):
                    eng.dma_start(into[:, bass.ds(s * (4 * step) + (base + q * step), part.stop - part.start)],
                                  cache[bass.ds(place, 1)].rearrange("a p n -> (a p) n")[:, part])\
                       .then_inc(sem(f"{event}{b}"), 16)

        def cmp_pages(eng, q, odd):
            if q == 0:
                eng.wait_ge(sem("page_table_in"), 16)
            if q == 1:
                eng.wait_ge(sem("conv_turned"), TILES)
            if q >= 2:
                eng.wait_ge(sem("compressed"), q - 1)
            load_pages(eng, a["cache_cmp"], (2 * q + odd) * PAGES, 2 * (q % 2) + odd, "cmp_page")

        pages_flat = flat(A1, 18688)
        with nc.Block() as block:
            @block.sync
            def _(sp):
                sp.dma_start(cg, a["conv_g"].partition_broadcast(P)).then_inc(sem("conv_gain_in"), 16)
                sp.dma_start(cb, a["conv_b"].partition_broadcast(P)).then_inc(sem("conv_gain_in"), 16)
                sp.dma_start(cn, a["norm_conv"].partition_broadcast(P)).then_inc(sem("conv_gain_in"), 16)
                sp.dma_start(w_cmp1, a["w_cmp1"].rearrange("p (v l h) -> p v l h", v=2, l=CMP // 2))\
                  .then_inc(sem("w_cmp_in"), 16)
                sp.dma_start(w_cmp2, a["w_cmp2"]).then_inc(sem("w_cmp_in"), 16)
                sp.dma_start(pages[:, HALF + NQ, :], a["pos_emb"]).then_inc(sem("w_cmp_in"), 16)
                for q in range(4):
                    cmp_pages(sp, q, 0)

            @block.tensor
            def _(pe):
                for t in range(TILES):
                    n = rows(t)
                    if t >= 4:
                        pe.wait_ge(sem("conv_moved"), t - 3)
                    for c in range(4):
                        mm = pe.transpose(ps[:n, t % 4, c * P:(c + 1) * P], acc[:, c, t * P:t * P + n], ident)
                    mm.then_inc(sem("conv_turned"), 1)
                pe.wait_ge(sem("w_cmp_in"), 48)
                for q in range(4):
                    n, at = (2 * PAGES + (NQ + 1 if q == 1 else 0)) * 4, 2 * PAGES * (q % 2)
                    for b in range(2):
                        pe.wait_ge(sem(f"cmp_page{2 * (q % 2) + b}"), 16 * PAGES * (q // 2 + 1))
                    for v in range(2):
                        for l in range(CMP // 2):
                            mm = pe.matmul(ps[:, 4 + q, 256 * v:256 * v + n], w_cmp1[:, v, l, :],
                                           pages[:, at:at + n // 4, 128 * v + 4 * l:128 * v + 4 * l + 4],
                                           start=(l == 0), stop=(l == CMP // 2 - 1))
                    mm.then_inc(sem("compressed"), 1)
                pe.wait_ge(sem("swished_blocks"), 1)
                pe.wait_ge(sem("conv_moved"), TILES)
                for bank, o, m in ((0, 0, 2 * P), (1, 512, PBLK)):
                    for g in range(KV):
                        mm = pe.matmul(ps[:, bank, 0:m], w_cmp2[:, 128 * g:128 * g + 128],
                                       sil[:, 0, o + g:o + 2 * m:2], start=(g == 0), stop=(g == 1))
                for b in range(NB):
                    for g in range(KV):
                        o = 64 * b + g
                        mm = pe.matmul(ps[:SBLK, 2 + b // 4, 128 * (b % 4) + 64 * g:128 * (b % 4) + 64 * g + 64],
                                       sil[:, 1, o:o + 63:2], w_cmp2[:, 256:320], start=True, stop=True)
                for g in range(KV):
                    mm = pe.matmul(ps[:PBLK, 1, P + 64 * g:P + 64 * g + 64], sil[:, 1, 512 + g:512 + g + 31:2],
                                   w_cmp2[:, 256:320], start=True, stop=True)
                mm.then_inc(sem("blocks_made"), 1)

            @block.scalar
            def _(act):
                chain = Chain(act, sem("act_chain"), count["act"])
                for t in range(TILES):
                    n = rows(t)
                    act.wait_ge(sem("conv_turned"), t + 1)
                    act.activation(conv[:n, t, :], ps[:n, t % 4, :], ACT.Copy).then_inc(sem("conv_moved"), 1)
                act.wait_ge(sem("conv_moments"), TILES)
                act.activation(csd, mv[:, :, 1], ACT.Sqrt, bias=con("eps")[:, 1:2]).then_inc(sem("conv_sd"), 1)
                for t in range(TILES):
                    n = rows(t)
                    act.wait_ge(sem("conv_shifted"), t + 1)
                    act.activation(conv[:n, t, :], conv[:n, t, :], ACT.Silu).then_inc(sem("swished"), 1)
                act.wait_ge(sem("swished"), TILES)
                act.wait_ge(sem("css_set"), 1)
                for t in range(TILES):
                    n = rows(t)
                    ins = act.activation(junk[:n, :], conv[:n, t, :], ACT.Square, scale=CH ** -0.5,
                                         accum_out=css[:n, t:t + 1])
                    chain(ins)
                act.activation(csd, css, ACT.Sqrt, bias=con("eps")[:, 0:1]).then_inc(sem("conv_sd"), 1)
                act.wait_ge(sem("compressed"), 4)
                act.wait_ge(sem("bias_ready"), 1)
                for v in range(2):
                    for q in range(4):
                        act.activation(sil[:, v, 128 * q:128 * q + 128], ps[:, 4 + q, 256 * v:256 * v + 128],
                                       ACT.Silu, bias=cmp_bias[:, v:v + 1])
                    ins = act.activation(sil[:, v, 512:544], ps[:, 5, 256 * v + 128:256 * v + 160], ACT.Silu,
                                         bias=cmp_bias[:, v:v + 1])
                ins.then_inc(sem("swished_blocks"), 1)

            @block.vector
            def _(dve):
                chain = Chain(dve, sem("dve_chain"), count["dve"])
                dve.memset(kcT_p, 0.0).then_inc(sem("kcT_zero"), 1)
                dve.memset(mv, 1.0)
                dve.memset(css, 1.0).then_inc(sem("css_set"), 1)
                dve.wait_ge(sem("css_set"), 1)
                for t in range(TILES):
                    n = rows(t)
                    dve.wait_ge(sem("conv_moved"), t + 1)
                    chain(dve.bn_stats(bn[:n, t, :], conv[:n, t, :]))
                    dve.bn_aggr(mv[:n, t, :], bn[:n, t, :]).then_inc(sem("conv_moments"), 1)
                dve.wait_ge(sem("conv_sd"), 1)
                chain(dve.reciprocal(crs, csd))
                dve.wait_ge(sem("conv_moved"), TILES)
                dve.wait_ge(sem("conv_gain_in"), 48)
                for t in range(TILES):
                    n = rows(t)
                    chain(dve.tensor_scalar(conv[:n, t, :], conv[:n, t, :], mv[:n, t, 0:1], crs[:n, t:t + 1],
                                            ALU.subtract, ALU.mult))
                    dve.tensor_tensor(conv[:n, t, :], conv[:n, t, :], cg[:n, :], ALU.mult).then_inc(sem("conv_gained"), 1)
                dve.wait_ge(sem("conv_sd"), 2)
                chain(dve.reciprocal(crs, csd))
                for t in range(TILES):
                    n = rows(t)
                    dve.scalar_tensor_tensor(conv[:n, t, :], conv[:n, t, :], crs[:n, t:t + 1], cn[:n, :],
                                             ALU.mult, ALU.mult).then_inc(sem("conv_ready"), 1)
                dve.wait_ge(sem("conv_ready"), TILES)
                dve.wait_ge(sem("compressed"), 4)
                dve.tensor_copy(cmp_bias, ps[:, 5, 160:417:256]).then_inc(sem("bias_ready"), 1)
                dve.wait_ge(sem("blocks_made"), 1)
                dve.tensor_copy(kcT_s, ps[:, 0, 0:2 * P])
                dve.wait_ge(sem("kcT_zero"), 1)
                for g in range(KV):
                    dve.tensor_copy(kcT_p[64 * g:64 * g + 64, PBLK * g:PBLK * g + PBLK],
                                    ps[64 * g:64 * g + 64, 1, 0:PBLK])
                dve.tensor_copy(vc_p[:PBLK, :], ps[:PBLK, 1, P:2 * P])
                dve.tensor_copy(vc_s[:SBLK], ps[:SBLK, 2:4, :].rearrange("p c (b n) -> p (c b) n", b=4))\
                   .then_inc(sem("blocks_out"), 1)
                dve.wait_ge(sem("blocks_out"), 1)

            @block.gpsimd
            def _(pool):
                cmp_pages(pool, 0, 1)
                cmp_pages(pool, 1, 1)
                pool.wait_ge(sem("conv_gain_in"), 48)
                for t in range(TILES):
                    n = rows(t)
                    pool.wait_ge(sem("conv_gained"), t + 1)
                    pool.tensor_tensor(conv[:n, t, :], conv[:n, t, :], cb[:n, :], ALU.add)\
                        .then_inc(sem("conv_shifted"), 1)
                cmp_pages(pool, 2, 1)
                cmp_pages(pool, 3, 1)


        att = flat(A4, TILES * 512).rearrange("p (t n) -> p t n", n=512)
        probs = flat(A2b, 3072).rearrange("p (s n) -> p s n", s=3)
        pT = flat(A3, 2048).rearrange("p (s n) -> p s n", s=2)
        block_v = flat(A3 + 2048, 512)
        own_block = flat(A3 + 2560, 512)
        cmp_s = flat(A3 + 3072, 256).rearrange("p (s n) -> p s n", s=2)
        cmp_pT = flat(A3 + 3328, 256).rearrange("p (s n) -> p s n", s=2)
        weighted = flat(A3 + 3584, 512)
        cmp_add = flat(A3 + 4096, NQ * PBLK)
        neg_max = flat(A3 + 4224, 3)
        sums = flat(A3 + 4232, 32).rearrange("p (s w h) -> p s w h", s=2, w=2)
        small4 = flat(A3 + 4264, 64).rearrange("p (s n) -> p s n", n=16)
        gate_of = gates.rearrange("p t (h c) -> p t c h", c=3)
        outT = flat(A2b + 3072, 512)
        SEL, WIN = 0, 1
        units = [(i, w, h) for i in range(NQ) for w in (SEL, WIN) for h in range(8)]

        def span(i, w):
            first = 0 if w == SEL else max(0, i - 4)
            return first, i + 1 - first

        def copies(u):
            _, m = span(*units[u][:2])
            if m > 4:
                return [("act", 0, 4), ("dve", 4, m - 4)]
            return [("act" if u % 2 else "dve", 0, m)]

        def copied_by(engine, u):
            return sum(e == engine for v in range(u + 1) for e, _, _ in copies(v))

        last_values = flat(A1 + 16384, PAGES * P)
        with nc.Block() as block:
            @block.sync
            def _(sp):
                o, w = const_at["own_block"]
                sp.dma_start(own_block, a["consts"][:, o:o + w]).then_inc(sem("own_block_in"), 16)
                for b in range(4):
                    load_pages(sp, a["cache_sel"], b * PAGES, b, "sel_page")

            @block.tensor
            def _(pe):
                for j, g in ((0, 0), (1, 1)):
                    mm = pe.matmul(ps[:, 5, 256 * g:256 * g + 256], con("rep_block", PBLK),
                                   vc_p[:PBLK, 64 * g:64 * g + 64].unsqueeze(1).to_broadcast([PBLK, R, HD]),
                                   start=True, stop=True)
                mm.then_inc(sem("values_spread"), 1)
                for i in range(NQ + 2):
                    if i < NQ:
                        if i >= 2:
                            pe.wait_ge(sem("cmp_scored_dve"), i - 1)
                        for r in range(R):
                            mm = pe.matmul(ps[:, i % 2, 32 * r:32 * r + 32], qT[:, r, i * P:(i + 1) * P],
                                           kcT_p, start=True, stop=True)
                        mm.then_inc(sem("cmp_scored"), 1)
                    if 1 <= i <= NQ:
                        pe.wait_ge(sem("cmp_probs"), i)
                        if i >= 2:
                            pe.wait_ge(sem("cmp_p_copied"), i - 1)
                        pe.transpose(ps[:, 2, 0:P], cmp_s[:, (i - 1) % 2, :], ident).then_inc(sem("cmp_p_turned"), 1)
                    if i >= 2:
                        pe.wait_ge(sem("cmp_p_copied"), i - 1)
                        pe.wait_ge(sem("block_v_ready"), 1)
                        if i >= 3:
                            pe.wait_ge(sem("cmp_out_copied"), i - 2)
                        pe.matmul(ps[:, 3, :], cmp_pT[:, (i - 2) % 2, :], block_v, start=True, stop=True)\
                          .then_inc(sem("cmp_out"), 1)
                pe.wait_ge(sem("cmp_out_copied"), NQ)
                pe.wait_ge(sem("block_v_ready"), 1)

                def used(u):
                    pe.wait_ge(sem("pT_act"), copied_by("act", u))
                    pe.wait_ge(sem("pT_dve"), copied_by("dve", u))

                def score(u):
                    i, w, h = units[u]
                    g, r = h // R, h % R
                    first, m = span(i, w)
                    if u >= 3:
                        used(u - 3)
                    for o in range(0, m, 4):
                        n = min(4, m - o) * P
                        mm = pe.matmul(ps[:, 2 * (u % 3) + o // 4, 0:n],
                                       qT[64 * g:64 * g + 64, r, i * P:(i + 1) * P],
                                       kT[64 * g:64 * g + 64, w, (first + o) * P:(first + o) * P + n],
                                       start=True, stop=True)
                    mm.then_inc(sem("scored"), 1)

                def values(u):
                    i, w, h = units[u]
                    first, m = span(i, w)
                    used(u)
                    if h == 0 and i > 0:
                        pe.wait_ge(sem("combined"), 2 * (i - 1) + w + 1)
                    g, r = h // R, h % R
                    for j in range(m):
                        mm = pe.matmul(ps[64 * g:64 * g + 64, 6 + w, r * P:(r + 1) * P],
                                       vals[:, first + j, w, 64 * g:64 * g + 64],
                                       pT[:, u % 2, j * P:(j + 1) * P],
                                       start=(j == 0), stop=(j == m - 1), tile_position=(0, 64 * g))
                    mm.then_inc(sem("valued"), 1)

                def turn_back(tile, w):
                    pe.wait_ge(sem("out_copied"), 2 * tile + w + 1)
                    for r in range(R):
                        mm = pe.transpose(ps[:, 6 + w, r * P:(r + 1) * P], outT[:, r * P:(r + 1) * P], ident)
                    mm.then_inc(sem("turned_back"), 1)

                score(0)
                score(1)
                for u in range(len(units)):
                    _, m = span(*units[u][:2])
                    pe.wait_ge(sem("exp_done"), u + 1)
                    for j in range(m):
                        mm = pe.transpose(ps[:, 2 * (u % 3) + j // 4, (j % 4) * P:(j % 4 + 1) * P],
                                          probs[:, u % 3, j * P:(j + 1) * P], ident)
                    mm.then_inc(sem("turned"), 1)
                    if u + 2 < len(units):
                        score(u + 2)
                    if u >= 1:
                        values(u - 1)
                    if u >= 8 and u % 8 == 2:
                        turn_back((u - 8) // 16, (u - 8) // 8 % 2)
                values(len(units) - 1)
                turn_back(NQ - 1, WIN)

            def wide(u, m):
                return ps[:, 2 * (u % 3):2 * (u % 3) + 2, :].rearrange("p b n -> p (b n)")[:, 0:m * P]

            def copy_turned(eng, copy, name, u):
                for e, o, m in copies(u):
                    if e == name:
                        eng.wait_ge(sem("turned"), u + 1)
                        copy(pT[:, u % 2, o * P:(o + m) * P], ps[:, 2 * (u % 3) + o // 4, 0:m * P])\
                            .then_inc(sem(f"pT_{name}"), 1)

            @block.gpsimd
            def _(pool):
                load_pages(pool, a["cache_sel"], HALF + 3 * PAGES, 3, "sel_values", slice(P, 2 * P), last_values)

            @block.scalar
            def _(act):
                for i in range(NQ + 2):
                    if i < NQ:
                        act.wait_ge(sem("cmp_scored_dve"), i + 1)
                        act.activation(cmp_s[:, i % 2, :], cmp_s[:, i % 2, :], ACT.Exp).then_inc(sem("cmp_exp"), 1)
                    if 1 <= i <= NQ:
                        act.wait_ge(sem("cmp_p_turned"), i)
                        if i >= 3:
                            act.wait_ge(sem("cmp_out"), i - 2)
                        act.activation(cmp_pT[:, (i - 1) % 2, :], ps[:, 2, 0:P], ACT.Copy)\
                           .then_inc(sem("cmp_p_copied"), 1)
                    if i >= 2:
                        act.wait_ge(sem("cmp_out"), i - 1)
                        act.activation(att[:, i - 2, :], ps[:, 3, :], ACT.Copy).then_inc(sem("cmp_out_copied"), 1)

                def exp(u):
                    i, w, h = units[u]
                    _, m = span(i, w)
                    act.wait_ge(sem("max_ready"), u + 1)
                    if i >= 2 and h == 0:
                        act.wait_ge(sem("combined"), 2 * (i - 2) + w + 1)
                    act.activation(probs[:, u % 3, 0:m * P], wide(u, m), ACT.Exp, bias=neg_max[:, u % 3:u % 3 + 1],
                                   accum_out=sums[:, i % 2, w, h:h + 1]).then_inc(sem("exp_done"), 1)

                def copy_out(b):
                    act.wait_ge(sem("valued"), 8 * b + 8)
                    if b >= 1:
                        act.wait_ge(sem("turned_back"), b)
                    act.activation(outT, ps[:, 6 + b % 2, :], ACT.Copy).then_inc(sem("out_copied"), 1)

                exp(0)
                exp(1)
                for u in range(len(units)):
                    copy_turned(act, lambda o, i: act.activation(o, i, ACT.Copy), "act", u)
                    if u + 2 < len(units):
                        exp(u + 2)
                    if u >= 8 and u % 8 == 0:
                        copy_out(u // 8 - 1)
                copy_out(2 * NQ - 1)

            @block.vector
            def _(dve):
                chain = Chain(dve, sem("dve_chain"), count["dve"])
                chain(dve.tensor_scalar(cmp_add, con("cmp_ok"), -NEG, NEG, ALU.mult, ALU.add))
                dve.wait_ge(sem("own_block_in"), 16)
                dve.wait_ge(sem("values_spread"), 1)
                dve.tensor_tensor(block_v, ps[:, 5, :], own_block, ALU.mult).then_inc(sem("block_v_ready"), 1)

                def per_head(v):
                    return v.rearrange("p (h n) -> p h n", h=8)

                for i in range(NQ + 1):
                    if i < NQ:
                        dve.wait_ge(sem("cmp_scored"), i + 1)
                        if i >= 2:
                            dve.wait_ge(sem("cmp_p_turned"), i - 1)
                        s = per_head(cmp_s[:, i % 2, :])
                        st = small4[:, i % 2, :]
                        add = cmp_add[:, PBLK * i:PBLK * i + PBLK].unsqueeze(1).to_broadcast([P, R, PBLK])
                        by_group = ps[:, i % 2, 0:P].rearrange("p (r g n) -> p g r n", r=R, g=KV)
                        dve.tensor_tensor(s[:, 0:4], by_group[:, 0], add, ALU.add)
                        chain(dve.tensor_tensor(s[:, 4:8], by_group[:, 1], add, ALU.add))
                        chain(dve.tensor_reduce(st[:, 0:8], s, AX.X, ALU.max))
                        dve.tensor_tensor(s, s, st[:, 0:8].unsqueeze(2).to_broadcast([P, 8, PBLK]),
                                          ALU.subtract).then_inc(sem("cmp_scored_dve"), 1)
                    if i >= 1:
                        k = i - 1
                        s = per_head(cmp_s[:, k % 2, :])
                        st = small4[:, 2 + k % 2, :]
                        dve.wait_ge(sem("cmp_exp"), k + 1)
                        chain(dve.tensor_reduce(st[:, 0:8], s, AX.X, ALU.add))
                        chain(dve.reciprocal(st[:, 0:8], st[:, 0:8]))
                        dve.tensor_tensor(st[:, 8:16], st[:, 0:8], gate_of[:, k, 0, :], ALU.mult)
                        ok = con("cmp_ok")[:, PBLK * k:PBLK * k + PBLK].unsqueeze(1).to_broadcast([P, 8, PBLK])
                        chain(dve.tensor_tensor(s, s, ok, ALU.mult))
                        dve.tensor_tensor(s, s, st[:, 8:16].unsqueeze(2).to_broadcast([P, 8, PBLK]), ALU.mult)\
                           .then_inc(sem("cmp_probs"), 1)

                def maximum(u):
                    i, w, h = units[u]
                    _, m = span(i, w)
                    dve.wait_ge(sem("scored"), u + 1)
                    s = wide(u, m)
                    if w == WIN and i >= 4:
                        dve.tensor_tensor(s[:, 0:P], s[:, 0:P], con("low"), ALU.add)
                    chain(dve.tensor_tensor(s[:, (m - 1) * P:m * P], s[:, (m - 1) * P:m * P], con("causal"), ALU.add))
                    dve.tensor_reduce(neg_max[:, u % 3:u % 3 + 1], s, AX.X, ALU.max, negate=True)\
                       .then_inc(sem("max_ready"), 1)

                def combine(i, w):
                    st = small4[:, w, :]
                    dve.wait_ge(sem("turned_back"), 2 * i + w + 1)
                    chain(dve.reciprocal(st[:, 0:8], sums[:, i % 2, w, :]))
                    chain(dve.tensor_tensor(st[:, 8:16], st[:, 0:8], gate_of[:, i, 1 + w, :], ALU.mult))
                    chain(dve.tensor_tensor(weighted.rearrange("p (g r d) -> p r g d", g=KV, r=R),
                                            ps[:, 6 + w, :].rearrange("p (r g d) -> p r g d", r=R, g=KV),
                                            st[:, 8:16].rearrange("p (g r) -> p r g", g=KV).unsqueeze(3)
                                            .to_broadcast([P, R, KV, HD]), ALU.mult))
                    dve.tensor_tensor(att[:, i, :], att[:, i, :], weighted, ALU.add).then_inc(sem("combined"), 1)
                    dve.wait_ge(sem("combined"), 2 * i + w + 1)

                maximum(0)
                maximum(1)
                dve.wait_ge(sem("cmp_out_copied"), NQ)
                for u in range(len(units)):
                    copy_turned(dve, lambda o, i: dve.tensor_copy(o, i), "dve", u)
                    if u + 2 < len(units):
                        maximum(u + 2)
                    i, w, h = units[u]
                    if u >= 8 and u % 8 == 3:
                        combine((u - 8) // 16, (u - 8) // 8 % 2)
                combine(NQ - 1, WIN)

        win_pages = flat(AQ, 4096).rearrange("p (s n) -> p s n", n=256)
        spT = flat(AQ + 4096, 23 * P).rearrange("p (s n) -> p s n", n=P)
        att_sT = flat(AQ + 4096 + 23 * P, 128).rearrange("p (r n) -> p r n", r=R)
        sample_rows = flat(AQ + 4096 + 23 * P + 128, P)
        s_sel = flat(A3, PAST + 32)
        s_win = flat(A3 + 2080, 544)
        s_cmp = flat(A3 + 2624, 32)
        imp = flat(A3 + 2656, 32)
        rank = flat(A3 + 2688, 32)
        gate_tmp = flat(A3 + 2720, 24).rearrange("p (c h) -> p c h", c=3)
        st5 = flat(A3 + 2744, 24)
        earlier = flat(A2b, 1024).rearrange("p (i j) -> p i j", i=SBLK)
        above = flat(A2b + 1024, 1024).rearrange("p (i j) -> p i j", i=SBLK)
        equal = flat(A2b + 2048, 1024).rearrange("p (i j) -> p i j", i=SBLK)
        OWN_SEL, OWN_WIN, CMP_T = 20, 21, 22

        att_g = gain[:, D:D + 512]
        junk5 = flat(A2b + 3072, 512)
        att_ss, att_sd, att_rs = stat(TILES), stat(TILES), stat(TILES)

        def last_pages(eng, event, part, batches):
            for b in batches:
                load_pages(eng, a["cache_sel"], HALF + b * PAGES, b, event, part)

        with nc.Block() as block:
            @block.sync
            def _(sp):
                o, w = const_at["earlier"]
                sp.dma_start(earlier.rearrange("p i j -> p (i j)"), a["consts"][:, o:o + w])\
                  .then_inc(sem("earlier_in"), 16)
                sp.dma_start(att_g, a["norm_att"].partition_broadcast(P)).then_inc(sem("att_gain_in"), 16)
                sp.dma_start(win_pages, a["state_win_use"][0:16].rearrange("s p n -> p s n"))\
                  .then_inc(sem("win_page"), 16)
                sp.wait_ge(sem("s_scored"), 1)
                sp.dma_start(win_pages[:, :, 0:P], a["state_win_use"][16:32, :, 0:P].rearrange("s p n -> p s n"))\
                  .then_inc(sem("win_page"), 16)
                last_pages(sp, "sel_keys", slice(0, P), (0, 2))
                sp.wait_ge(sem("sampled"), 1)
                sp.dma_start(win_pages[:, :, P:2 * P], a["state_win_use"][16:32, :, P:2 * P].rearrange("s p n -> p s n"))\
                  .then_inc(sem("win_values"), 16)
                last_pages(sp, "sel_values", slice(P, 2 * P), (0,))

            @block.gpsimd
            def _(pool):
                pool.wait_ge(sem("s_scored"), 1)
                last_pages(pool, "sel_keys", slice(0, P), (1, 3))
                pool.wait_ge(sem("sampled"), 1)
                last_pages(pool, "sel_values", slice(P, 2 * P), (1,))

            @block.tensor
            def _(pe):
                def importance(half):
                    pe.wait_ge(sem("s_cmp_normed"), half + 1)
                    pe.wait_ge(sem("gates_taken"), half + 1)
                    pe.matmul(ps[:, 7, 0:SBLK], con("same_query"), s_cmp, start=True, stop=True)\
                      .then_inc(sem("importance"), 1)

                for half in range(2):
                    if half:
                        pe.wait_ge(sem("sample_out_copied"), 1)
                    for b in range(4):
                        q = q_diag[:, 4 * half + b, :]
                        o = slice(32 * b, 32 * b + 32)
                        n = 4 * half + b
                        mm = pe.matmul(ps[o, 6, 0:SBLK], q, kcT_s[:, 32 * n:32 * n + 32], start=True, stop=True,
                                       tile_position=(0, 32 * b))
                    mm.then_inc(sem("s_cmp_scored"), 1)
                    pe.matmul(ps[:, 7, 0:24], con("pick_token", NB * NS)[:, P * half:P * half + P],
                              gates[:NB * NS, NQ, :], start=True, stop=True).then_inc(sem("gates_spread"), 1)
                    if half:
                        importance(half)
                    for b in range(4):
                        pe.wait_ge(sem(f"sel_keys{b}" if half else f"sel_page{b}"), 16 * PAGES)
                    pe.wait_ge(sem("win_page"), 16 * (half + 1))
                    for c in range(4):
                        for b in range(4):
                            pe.matmul(ps[32 * b:32 * b + 32, c, :], q_diag[:, 4 * half + b, :],
                                      pages[:, PAGES * b + 4 * c:PAGES * b + 4 * c + 4, 0:P],
                                      start=True, stop=True, tile_position=(0, 32 * b))
                    for b in range(4):
                        pe.matmul(ps[32 * b:32 * b + 32, 5, :], q_diag[:, 4 * half + b, :],
                                  win_pages[:, 4 * b:4 * b + 4, 0:P], start=True, stop=True,
                                  tile_position=(0, 32 * b))
                    for w in range(2):
                        for b in range(4):
                            mm = pe.matmul(ps[32 * b:32 * b + 32, 4, 32 * w:32 * w + 32], q_diag[:, 4 * half + b, :],
                                           kT_new[:, w, :], start=True, stop=True, tile_position=(0, 32 * b))
                    mm.then_inc(sem("s_scored"), 1)
                    if not half:
                        importance(half)
                    pe.wait_ge(sem("s_probs"), half + 1)
                    for j in range(PAGES):
                        mm = pe.transpose(ps[:, j // 4, (j % 4) * P:(j % 4 + 1) * P], s_sel[:, j * P:(j + 1) * P], ident)
                        if j % 4 == 3:
                            mm.then_inc(sem("s_turned"), 1)
                    for j in range(4):
                        mm = pe.transpose(ps[:, 5, j * P:(j + 1) * P], s_win[:, j * P:(j + 1) * P], ident)
                    mm.then_inc(sem("s_turned"), 1)
                    pe.transpose(ps[:32, 4, 0:P], s_sel[:, PAST:PAST + 32], ident)
                    pe.transpose(ps[:32, 4, P:2 * P], s_win[:, 512:544], ident)
                    pe.transpose(ps[:32, 4, 2 * P:3 * P], s_cmp, ident).then_inc(sem("s_turned"), 1)
                    pe.wait_ge(sem("sT_act"), 3 * (half + 1))
                    pe.wait_ge(sem("sT_dve"), 3 * (half + 1))
                    if half:
                        pe.wait_ge(sem("win_values"), 16)
                        for b in range(4):
                            pe.wait_ge(sem(f"sel_values{b}"), 16 * PAGES)
                    terms = [(spT[:32, OWN_SEL], lambda b: v_new[:32, 0, :]), (spT[:32, OWN_WIN], lambda b: v_new[:32, 1, :]),
                             (spT[:32, CMP_T], lambda b: vc_s[:SBLK, 4 * half + b, :])]
                    for j in range(PAGES):
                        terms.append((spT[:, j], lambda b, j=j: last_values[:, P * j:P * j + P] if half and b == 3
                                      else pages[:, PAGES * b + j, P:2 * P]))
                    for j in range(4):
                        terms.append((spT[:, PAGES + j], lambda b, j=j: win_pages[:, 4 * b + j, P:2 * P]))
                    for k, (left, right) in enumerate(terms):
                        for b in range(4):
                            o = slice(32 * b, 32 * b + 32)
                            mm = pe.matmul(ps[o, 6, 0:P], left[:, o], right(b), start=(k == 0),
                                           stop=(k == len(terms) - 1), tile_position=(0, 32 * b))
                    mm.then_inc(sem("sampled"), 1)
                    pe.wait_ge(sem("sampled_copied"), half + 1)
                    pe.transpose(ps[:, 7, 0:P], sample_rows, ident).then_inc(sem("sampled_turned"), 1)
                pe.wait_ge(sem("sample_out_copied"), 2)
                for r in range(R):
                    mm = pe.transpose(ps[:32, 7, r * P:(r + 1) * P], att_sT[:, r, :], ident)
                mm.then_inc(sem("sample_turned"), 1)

            @block.scalar
            def _(act):
                chain = Chain(act, sem("act_chain"), count["act"])
                act.wait_ge(sem("att_ss_set"), 1)
                for t in range(NQ):
                    chain(act.activation(junk5, att[:, t, :], ACT.Square, scale=512 ** -0.5,
                                         accum_out=att_ss[:, t:t + 1]))
                act.activation(att_sd[:, 0:NQ], att_ss[:, 0:NQ], ACT.Sqrt, bias=con("eps")[:, 0:1])\
                   .then_inc(sem("att_sd"), 1)
                for half in range(2):
                    act.wait_ge(sem("s_cmp_max"), half + 1)
                    act.activation(s_cmp, ps[:, 6, 0:SBLK], ACT.Exp, bias=st5[:, 0:1], accum_out=st5[:, 3:4])\
                       .then_inc(sem("s_cmp_exp"), 1)
                    if half:
                        act.wait_ge(sem("sampled"), 1)
                        last_pages(act, "sel_values", slice(P, 2 * P), (2,))
                    act.wait_ge(sem("s_max"), half + 1)
                    act.activation(s_win, s_win, ACT.Exp, bias=st5[:, 2:3], accum_out=st5[:, 5:6])
                    act.activation(s_sel, s_sel, ACT.Exp, bias=st5[:, 1:2], accum_out=st5[:, 4:5])\
                       .then_inc(sem("s_exp"), 1)
                    for n, bank in ((0, 0), (2, 2), (4, 5)):
                        act.wait_ge(sem("s_turned"), 6 * half + n + 1)
                        o = PAGES if bank == 5 else 4 * bank
                        act.activation(spT[:, o:o + 4, :], ps[:, bank, :].rearrange("p (s n) -> p s n", n=P),
                                       ACT.Copy).then_inc(sem("sT_act"), 1)
                act.wait_ge(sem("sample_turned"), 1)
                act.activation(att[:32, NQ, :].rearrange("p (g r d) -> p r g d", g=KV, r=R),
                               ps[:32, 7, :].rearrange("p (r g d) -> p r g d", r=R, g=KV), ACT.Copy)\
                   .then_inc(sem("att_done"), 1)

            @block.vector
            def _(dve):
                chain = Chain(dve, sem("dve_chain"), count["dve"])
                dve.memset(att_ss, 1.0).then_inc(sem("att_ss_set"), 1)
                dve.wait_ge(sem("earlier_in"), 16)
                for half in range(2):
                    dve.wait_ge(sem("s_cmp_scored"), half + 1)
                    dve.tensor_reduce(st5[:, 0:1], ps[:, 6, 0:SBLK], AX.X, ALU.max, negate=True)\
                       .then_inc(sem("s_cmp_max"), 1)
                    dve.wait_ge(sem("gates_spread"), half + 1)
                    chain(dve.tensor_tensor(gate_tmp, ps[:, 7, 0:24].rearrange("p (h c) -> p c h", c=3),
                                            con("own_head").unsqueeze(1).to_broadcast([P, 3, 8]), ALU.mult))
                    dve.tensor_reduce(st5[:, 6:9], gate_tmp, AX.X, ALU.add).then_inc(sem("gates_taken"), 1)
                    dve.wait_ge(sem("s_cmp_exp"), half + 1)
                    chain(dve.reciprocal(st5[:, 9:10], st5[:, 3:4]))
                    dve.tensor_scalar(s_cmp, s_cmp, st5[:, 9:10], None, ALU.mult).then_inc(sem("s_cmp_normed"), 1)
                    dve.wait_ge(sem("importance"), half + 1)
                    dve.tensor_scalar(s_cmp, s_cmp, st5[:, 6:7], None, ALU.mult)
                    chain(dve.tensor_copy(imp, ps[:, 7, 0:SBLK]))
                    other = imp.unsqueeze(1).to_broadcast([P, SBLK, SBLK])
                    itself = imp.unsqueeze(2).to_broadcast([P, SBLK, SBLK])
                    chain(dve.tensor_tensor(above, other, itself, ALU.is_gt))
                    chain(dve.tensor_tensor(equal, other, itself, ALU.is_equal))
                    chain(dve.tensor_tensor(equal, equal, earlier, ALU.mult))
                    chain(dve.tensor_tensor(above, above, equal, ALU.add))
                    chain(dve.tensor_reduce(rank, above, AX.X, ALU.add))
                    chain(dve.tensor_scalar(rank, rank, float(NSEL), NEG, ALU.is_ge, ALU.mult))
                    if half:
                        dve.wait_ge(sem("att_gain_in"), 16)
                        dve.wait_ge(sem("att_sd"), 1)
                        chain(dve.reciprocal(att_rs[:, 0:NQ], att_sd[:, 0:NQ]))
                        for t in range(NQ):
                            dve.scalar_tensor_tensor(att[:, t, :], att[:, t, :], att_rs[:, t:t + 1], att_g, ALU.mult, ALU.mult)\
                               .then_inc(sem("att_normed"), 1)
                        dve.wait_ge(sem("att_normed"), NQ)
                    dve.wait_ge(sem("s_scored"), half + 1)
                    for c in range(4):
                        chosen = rank[:, 8 * c:8 * c + 8].unsqueeze(2).to_broadcast([P, 8, CMP])
                        dve.tensor_tensor(s_sel[:, 512 * c:512 * c + 512].rearrange("p (b n) -> p b n", b=8),
                                          ps[:, c, :].rearrange("p (b n) -> p b n", b=8), chosen, ALU.add)
                    own = con("own")[:, 32 * half:32 * half + 32]
                    dve.tensor_tensor(s_sel[:, PAST:PAST + 32], ps[:, 4, 0:32], own, ALU.add)
                    dve.tensor_tensor(s_win[:, 512:544], ps[:, 4, 32:64], own, ALU.add)
                    chain(dve.tensor_tensor(s_win[:, 0:512], ps[:, 5, :], con("win"), ALU.add))
                    dve.tensor_reduce(st5[:, 2:3], s_win, AX.X, ALU.max, negate=True)
                    dve.tensor_reduce(st5[:, 1:2], s_sel, AX.X, ALU.max, negate=True).then_inc(sem("s_max"), 1)
                    dve.wait_ge(sem("s_exp"), half + 1)
                    chain(dve.reciprocal(st5[:, 10:12], st5[:, 4:6]))
                    chain(dve.tensor_tensor(st5[:, 12:14], st5[:, 10:12], st5[:, 7:9], ALU.mult))
                    dve.tensor_scalar(s_win, s_win, st5[:, 13:14], None, ALU.mult)
                    dve.tensor_scalar(s_sel, s_sel, st5[:, 12:13], None, ALU.mult).then_inc(sem("s_probs"), 1)
                    for n, bank in ((1, 1), (3, 3)):
                        dve.wait_ge(sem("s_turned"), 6 * half + n + 1)
                        dve.tensor_copy(spT[:, 4 * bank:4 * bank + 4, :],
                                        ps[:, bank, :].rearrange("p (s n) -> p s n", n=P)).then_inc(sem("sT_dve"), 1)
                    dve.wait_ge(sem("s_turned"), 6 * half + 6)
                    dve.tensor_copy(spT[:32, OWN_SEL:OWN_SEL + 3, :],
                                    ps[:32, 4, 0:3 * P].rearrange("p (s n) -> p s n", n=P)).then_inc(sem("sT_dve"), 1)
                    dve.wait_ge(sem("sampled"), half + 1)
                    dve.tensor_copy(sample_rows, ps[:, 6, 0:P]).then_inc(sem("sampled_copied"), 1)
                    dve.wait_ge(sem("sampled_turned"), half + 1)
                    for g in range(KV):
                        src = ps[64 * g:64 * g + 64, 7, 0:P].rearrange("p (b g r s) -> p g r b s", b=4, g=KV, r=R)
                        ins = dve.tensor_copy(
                            att_sT[64 * g:64 * g + 64, :, 16 * half:16 * half + 16].rearrange(
                                "p r (b s) -> p r b s", b=4), src[:, g])
                    ins.then_inc(sem("sample_out_copied"), 1)
        reuse_semaphores()


        x_res = flat(AQ, TILES * D).rearrange("p (t n) -> p t n", n=D)
        ln2_g, final_g = gain[:, 0:D], gain[:, D + 512:2 * D + 512]
        w_out = flat(A1, 8192).rearrange("p (k n) -> p k n", k=KT_)
        mixT = flat(A1 + 8192, 2048).rearrange("p (s k n) -> p s k n", s=2, k=KT_)
        xt = flat(A1 + 10240, 2048).rearrange("p (s n) -> p s n", s=2)
        h_sb = flat(A1 + 12288, 2048).rearrange("p (s n) -> p s n", s=2)
        hT = flat(A1 + 14336, 2048).rearrange("p (s k n) -> p s k n", s=2, k=KT_)
        w_router = flat(A1 + 16384, KT_ * 36).rearrange("p (k n) -> p k n", k=KT_)
        junk6 = flat(A3, D)
        logits = flat(A3 + 1024, TILES * 36).rearrange("p (t n) -> p t n", n=36)
        st6 = flat(A3 + 1352, 72).rearrange("p (q n) -> p q n", q=8)
        with nc.Block() as block:
            @block.sync
            def _(sp):
                sp.dma_start(w_out[:, 0:4, :], a["w_out"][0:512].rearrange("(p c) n -> p c n", c=4))\
                  .then_inc(sem("w_out_in"), 16)
                sp.dma_start(w_out[:, 4:8, :], a["w_out"][512:1024].rearrange("(p c) n -> p c n", c=4))\
                  .then_inc(sem("w_out_in"), 16)
                sp.dma_start(ln2_g, a["ln2"].partition_broadcast(P)).then_inc(sem("late_gain_in"), 16)
                sp.dma_start(final_g, a["ln_final"].partition_broadcast(P)).then_inc(sem("late_gain_in"), 16)
                sp.dma_start(w_router, a["w_router"].rearrange("p (k n) -> p k n", k=KT_)).then_inc(sem("w_router_in"), 16)
                def store(t):
                    sp.wait_ge(sem("h_ready"), t + 1)
                    sp.dma_start(scratch_h[P * t:P * t + rows(t), :],
                                 h_sb[:rows(t), t % 2, :]).then_inc(sem(f"h_out{t % 2}"), 16)

                for t in range(TILES):
                    if t >= 2:
                        sp.wait_ge(sem("merged1"), t - 1)
                    sp.dma_start(xt[:rows(t), t % 2, :], x_rows[t]).then_inc(sem(f"xt_in{t % 2}"), 16)
                    if t >= 2:
                        store(t - 2)
                store(TILES - 2)
                store(TILES - 1)
                sp.wait_ge(sem("h_out0"), 16 * 5)
                sp.wait_ge(sem("h_out1"), 16 * 4)

            @block.tensor
            def _(pe):
                def turn_mix(t):
                    n = rows(t)
                    if t == NQ:
                        pe.wait_ge(sem("last_att_normed"), 1)
                    for half, src in enumerate((conv, att)):
                        sv = src[:n, t, :].rearrange("p (m c) -> p c m", c=4)
                        for c in range(4):
                            mm = pe.transpose(ps[:, half, c * P:c * P + n], sv[:, c, :], ident[:n, :n])
                    mm.then_inc(sem("mix_turned"), 1)

                def mix(t, half):
                    n = rows(t)
                    if t >= 1:
                        pe.wait_ge(sem(f"merged{half}"), t)
                    for k in range(KT_):
                        mm = pe.matmul(ps[:n, 2 + half, :], mixT[:, t % 2, k, 0:n],
                                       w_out[:, k, 512 * half:512 * half + 512],
                                       start=(k == 0), stop=(k == KT_ - 1))
                    mm.then_inc(sem(f"mixed{half}"), 1)

                def turn_h(t):
                    n = rows(t)
                    pe.wait_ge(sem("h_ready"), t + 1)
                    hv = h_sb[:n, t % 2, :].rearrange("p (m k) -> p k m", k=KT_)
                    for k in range(KT_):
                        mm = pe.transpose(ps[:, 4 + k // 4, (k % 4) * P:(k % 4) * P + n], hv[:, k, :], ident[:n, :n])
                    mm.then_inc(sem("h_turned"), 1)

                def router(t):
                    n = rows(t)
                    pe.wait_ge(sem("hT_act"), t + 1)
                    pe.wait_ge(sem("hT_dve"), t + 1)
                    if t == 0:
                        pe.wait_ge(sem("w_router_in"), 16)
                    else:
                        pe.wait_ge(sem("logits_taken"), t)
                    for k in range(KT_):
                        mm = pe.matmul(ps[:n, 6, 0:36], hT[:, t % 2, k, 0:n], w_router[:, k, :],
                                       start=(k == 0), stop=(k == KT_ - 1))
                    mm.then_inc(sem("routed"), 1)

                turn_mix(0)
                pe.wait_ge(sem("w_out_in"), 32)
                for t in range(TILES):
                    pe.wait_ge(sem("mixT_act"), t + 1)
                    pe.wait_ge(sem("mixT_dve"), t + 1)
                    mix(t, 0)
                    if t + 1 < TILES:
                        turn_mix(t + 1)
                    if t >= 1:
                        turn_h(t - 1)
                    mix(t, 1)
                    if t >= 1:
                        router(t - 1)
                turn_h(TILES - 1)
                router(TILES - 1)

            @block.scalar
            def _(act):
                chain = Chain(act, sem("act_chain"), count["act"])
                act.wait_ge(sem("st6_set"), 1)
                n = rows(NQ)
                chain(act.activation(junk6[:n, 0:512], att[:n, NQ, :], ACT.Square, scale=512 ** -0.5,
                                     accum_out=att_ss[:n, NQ:TILES]))
                act.activation(att_sd[:n, NQ:TILES], att_ss[:n, NQ:TILES], ACT.Sqrt, bias=con("eps")[:n, 0:1])\
                   .then_inc(sem("last_att_sd"), 1)
                def copy_mix(t):
                    n = rows(t)
                    act.wait_ge(sem("mix_turned"), t + 1)
                    if t >= 2:
                        act.wait_ge(sem("mixed1"), t - 1)
                    act.activation(mixT[:, t % 2, 0:4, 0:n],
                                   ps[:, 0, :].rearrange("p (c m) -> p c m", c=4)[:, :, 0:n], ACT.Copy)\
                       .then_inc(sem("mixT_act"), 1)

                copy_mix(0)
                copy_mix(1)
                for t in range(1, TILES + 1):
                    q, n = t - 1, rows(t - 1)
                    act.wait_ge(sem("merged0"), q + 1)
                    act.wait_ge(sem("merged1"), q + 1)
                    chain(act.activation(junk6[:n, :], x_res[:n, q, :], ACT.Square, scale=1 / 32,
                                         accum_out=st6[:n, 3, q:q + 1]))
                    act.activation(st6[:n, 4, q:q + 1], st6[:n, 3, q:q + 1], ACT.Sqrt,
                                   bias=con("eps")[:n, 0:1]).then_inc(sem("x_sd"), 1)
                    if t + 1 < TILES:
                        copy_mix(t + 1)
                    act.wait_ge(sem("h_turned"), q + 1)
                    if q >= 2:
                        act.wait_ge(sem("routed"), q - 1)
                    act.activation(hT[:, q % 2, 0:4, 0:n],
                                   ps[:, 4, :].rearrange("p (c m) -> p c m", c=4)[:, :, 0:n], ACT.Copy)\
                       .then_inc(sem("hT_act"), 1)

            @block.vector
            def _(dve):
                chain = Chain(dve, sem("dve_chain"), count["dve"])
                dve.memset(logits, 0.0)
                dve.memset(st6, 1.0).then_inc(sem("st6_set"), 1)
                dve.wait_ge(sem("last_att_sd"), 1)
                n = rows(NQ)
                chain(dve.reciprocal(att_rs[:n, NQ:TILES], att_sd[:n, NQ:TILES]))
                dve.scalar_tensor_tensor(att[:n, NQ, :], att[:n, NQ, :], att_rs[:n, NQ:TILES], att_g[:n, :],
                                         ALU.mult, ALU.mult).then_inc(sem("last_att_normed"), 1)
                dve.wait_ge(sem("late_gain_in"), 32)
                def copy_mix(t):
                    n = rows(t)
                    dve.wait_ge(sem("mix_turned"), t + 1)
                    if t >= 2:
                        dve.wait_ge(sem("mixed1"), t - 1)
                    dve.tensor_copy(mixT[:, t % 2, 4:8, 0:n],
                                    ps[:, 1, :].rearrange("p (c m) -> p c m", c=4)[:, :, 0:n])\
                       .then_inc(sem("mixT_dve"), 1)

                def merge(t, half):
                    n, o = rows(t), 512 * half
                    dve.wait_ge(sem(f"mixed{half}"), t + 1)
                    dve.wait_ge(sem(f"xt_in{t % 2}"), 16 * (t // 2 + 1))
                    dve.tensor_tensor(x_res[:n, t, o:o + 512], ps[:n, 2 + half, :], xt[:n, t % 2, o:o + 512],
                                      ALU.add).then_inc(sem(f"merged{half}"), 1)

                def take_logits(t):
                    n = rows(t)
                    dve.wait_ge(sem("routed"), t + 1)
                    dve.tensor_copy(logits[:n, t, :], ps[:n, 6, 0:36]).then_inc(sem("logits_taken"), 1)

                copy_mix(0)
                merge(0, 0)
                copy_mix(1)
                for t in range(1, TILES + 1):
                    q, n = t - 1, rows(t - 1)
                    merge(q, 1)
                    if q >= 1:
                        take_logits(q - 1)
                    dve.wait_ge(sem("x_sd"), q + 1)
                    chain(dve.reciprocal(st6[:n, 5, q:q + 1], st6[:n, 4, q:q + 1]))
                    if q >= 2:
                        dve.wait_ge(sem(f"h_out{q % 2}"), 16 * (q // 2))
                        dve.wait_ge(sem("h_turned"), q - 1)
                    dve.wait_ge(sem("merged0"), q + 1)
                    dve.wait_ge(sem("merged1"), q + 1)
                    dve.scalar_tensor_tensor(h_sb[:n, q % 2, :], x_res[:n, q, :], st6[:n, 5, q:q + 1],
                                             ln2_g[:n, :], ALU.mult, ALU.mult).then_inc(sem("h_ready"), 1)
                    if t < TILES:
                        merge(t, 0)
                    if t + 1 < TILES:
                        copy_mix(t + 1)
                    dve.wait_ge(sem("h_turned"), q + 1)
                    if q >= 2:
                        dve.wait_ge(sem("routed"), q - 1)
                    dve.tensor_copy(hT[:, q % 2, 4:8, 0:n],
                                    ps[:, 5, :].rearrange("p (c m) -> p c m", c=4)[:, :, 0:n])\
                       .then_inc(sem("hT_dve"), 1)
                take_logits(TILES - 1)
                dve.wait_ge(sem("logits_taken"), TILES)

        E_, G_ = EXPERTS, GROUPS
        r7 = [A3 + 1424]

        def tmp7(n, shape=None):
            r7[0] += n
            v = flat(r7[0] - n, n)
            return v if shape is None else v.rearrange("p (t n) -> p t n", n=shape)

        first_w, second_w = stat(TILES), stat(TILES)
        token_of, row_of = ints[:, 0:CHUNKS + 1], ints[:, CHUNKS + 1:2 * CHUNKS + 2]
        wide7 = A4
        one_slot = flat(A3 + 2048, 2 * TILES * P).rearrange("p (q n) -> p q n", n=P)
        by_chunk = flat(A1 + 16384, 4 * TILES * (CHUNKS + 1)).rearrange("p (q n) -> p q n", n=2 * CHUNKS + 2)
        one_token, one_chunk = by_chunk[:, :, 0:CHUNKS + 1], by_chunk[:, :, CHUNKS + 1:2 * CHUNKS + 2]
        lane = flat(A1 + 16384 + 1792, P)
        chosen1 = flat(wide7, 288).rearrange("p (t n) -> p t n", n=E_)
        chosen2 = flat(wide7 + 288, 288).rearrange("p (t n) -> p t n", n=E_)
        le_m = flat(wide7 + 576, 288).rearrange("p (t n) -> p t n", n=E_)
        cand = flat(wide7 + 864, 288).rearrange("p (t n) -> p t n", n=E_)
        both = flat(wide7 + 1152, 288).rearrange("p (t n) -> p t n", n=E_)
        slot = flat(wide7 + 1440, 288).rearrange("p (t n) -> p t n", n=E_)
        base = flat(wide7 + 1728, 320).rearrange("p (t n) -> p t n", n=E_)
        steps7 = flat(wide7 + 2048, 288).rearrange("p (e k) -> p e k", e=E_)
        ends_le = flat(wide7 + 2336, (CHUNKS + 1) * E_).rearrange("p (c e) -> p c e", e=E_)
        group4 = tmp7(36, 4)
        cand4 = tmp7(36, 4)
        exp4 = tmp7(36, 4)
        g_max, c_max, p_top, m1, m2, diff, inv_d, sum4 = (tmp7(TILES) for _ in range(8))
        n_chunk, cum, cum0, ones32 = (tmp7(E_) for _ in range(4))
        valid7 = tmp7(TILES)
        chunk_f = tmp7(CHUNKS + 2)
        destf, dest_q, dest_c = (tmp7(2 * TILES) for _ in range(3))
        w_gate = [flat(A2 + 12288 * s, 4096).rearrange("p (k n) -> p k n", k=KT_) for s in range(2)]
        w_up = [flat(A2 + 12288 * s + 4096, 4096).rearrange("p (k n) -> p k n", k=KT_) for s in range(2)]
        w_down = [flat(A2 + 12288 * s + 8192, 4096).rearrange("p (h k n) -> p h k n", h=2, k=2) for s in range(2)]
        xg = [flat(A3 + 1024 * s, D) for s in range(2)]
        xgT = [flat(A3 + 2048 + 1024 * s, D).rearrange("p (k n) -> p k n", k=KT_) for s in range(2)]
        hid = [flat(A4 + 512 * s, DE) for s in range(2)]
        hidT = flat(A4 + 1024, 512).rearrange("p (k n) -> p k n", k=4)
        y_sb = [flat(A4 + 1536 + 1024 * s, D) for s in range(2)]
        ids = [ints[:, 2 * CHUNKS + 2 + s:2 * CHUNKS + 3 + s] for s in range(2)]
        out_ids = [ints[:, 2 * CHUNKS + 4 + s:2 * CHUNKS + 5 + s] for s in range(2)]
        N_AT = CHUNKS + 1
        HH = DE // 2
        GATE_BANK, UP_BANK = (0, 7), (1, 5)

        def chunk_count(eng):
            eng.wait_ge(sem("plan_ready"), 1)
            return eng.value_load(row_ints[0:1, N_AT:N_AT + 1], min_val=1, max_val=CHUNKS)

        def expert_weights(sp):
            n_chunks = chunk_count(sp)
            with sp.Fori(0, CHUNKS // 2) as i:
                with sp.If(i * 2 < n_chunks):
                    for s in range(2):
                        with sp.If(i * 2 + s < n_chunks):
                            e = sp.value_load(row_ints[0:1, bass.ds(i * 2 + s, 1)], min_val=0, max_val=EXPERTS - 1)
                            sp.wait_ge(sem(f"upped{s}"), i + 1)
                            for w, name in ((w_gate, "w_gate"), (w_up, "w_up")):
                                sp.dma_start(w[s], a[name][bass.ds(e, 1)].rearrange("a (p k) n -> (a p) k n", k=KT_))\
                                  .then_inc(sem(f"{name}_in{s}"), 16)
                            sp.wait_ge(sem(f"downed{s}"), i + 1)
                            sp.dma_start(w_down[s],
                                         a["w_down"][bass.ds(e, 1)].rearrange("a (h p k) n -> (a p) h k n", h=2, k=2))\
                              .then_inc(sem(f"w_down_in{s}"), 16)

        def expert_rows(pool):
            def take_ids(c, s, n):
                pool.tensor_copy(ids[s], token_of[:, bass.ds(c, 1)]).then_inc(sem(f"ids_ready{s}"), 1)
                pool.wait_ge(sem(f"xg_turned{s}"), n + 1)
                pool.wait_ge(sem(f"ids_ready{s}"), n + 1)

            def gather(s, n):
                pool.indirect_dma_start(xg[s], None, scratch_h,
                                        bass.IndirectOffsetOnAxis(ap=ids[s].bitcast(U32), axis=0))\
                    .then_inc(sem(f"xg_in{s}"), 16)
                pool.wait_ge(sem(f"xg_in{s}"), n * 16 + 16)

            for s in range(2):
                pool.dma_start(scratch_first[s:s + 1, :], CON[0:1, 0:16]).then_inc(sem(f"y_out{s}"), 16)
            n_chunks = chunk_count(pool)
            take_ids(0, 0, 0)
            gather(0, 0)
            with pool.Fori(0, CHUNKS // 2) as i:
                with pool.If(i * 2 < n_chunks):
                    for s in range(2):
                        with pool.If(i * 2 + s < n_chunks):
                            take_ids(i * 2 + s + 1, 1 - s, i + s)
                        with pool.If(i * 2 + s < n_chunks):
                            gather(1 - s, i + s)
                            pool.tensor_copy(out_ids[s], row_of[:, bass.ds(i * 2 + s, 1)]).then_inc(sem("out_ids_ready"), 1)
                            pool.wait_ge(sem("out_ids_ready"), i * 2 + s + 1)
                            pool.wait_ge(sem("y_act"), i * 2 + s + 2)
                            pool.wait_ge(sem("y_dve"), i * 2 + s + 2)
                        with pool.If(i * 2 + s < n_chunks):
                            pool.indirect_dma_start(scratch_y,
                                                    bass.IndirectOffsetOnAxis(ap=out_ids[s].bitcast(U32), axis=0),
                                                    y_sb[s], None).then_inc(sem(f"y_out{s}"), 16)
            pool.wait_ge(sem("y_out0"), (n_chunks + 1) // 2 * 16 + 16)
            pool.wait_ge(sem("y_out1"), n_chunks // 2 * 16 + 16)

        def expert_products(pe):
            def turn(s, n):
                pe.wait_ge(sem(f"xg_in{s}"), n * 16 + 16)
                v = xg[s].rearrange("p (m k) -> p k m", k=KT_)
                for k in range(KT_):
                    mm = pe.transpose(ps[:, 2 + k // 4, (k % 4) * P:(k % 4 + 1) * P], v[:, k, :], ident)
                mm.then_inc(sem(f"xg_turned{s}"), 1)

            def project(w, s, half, bank):
                for k in range(KT_):
                    mm = pe.matmul(ps[:, bank, 0:HH], xgT[s][:, k, :], w[s][:, k, HH * half:HH * half + HH],
                                   start=(k == 0), stop=(k == KT_ - 1))
                return mm

            def turn_hidden(s, half, bank):
                v = hid[s][:, HH * half:HH * half + HH].rearrange("p (m k) -> p k m", k=2)
                for k in range(2):
                    mm = pe.transpose(ps[:, bank, k * P:(k + 1) * P], v[:, k, :], ident)
                return mm

            for name in ("upped0", "upped1", "downed0", "downed1", "xg_turned0", "xg_turned1"):
                pe.sem_inc(sem(name), 1)
            n_chunks = chunk_count(pe)
            pe.wait_ge(sem("table_ready"), 1)
            turn(0, 0)
            with pe.Fori(0, CHUNKS // 2) as i:
                with pe.If(i * 2 < n_chunks):
                    for s in range(2):
                        with pe.If(i * 2 + s < n_chunks):
                            pe.wait_ge(sem(f"xgT_act{s}"), i + 1)
                            pe.wait_ge(sem(f"xgT_dve{s}"), i + 1)
                            pe.wait_ge(sem(f"w_gate_in{s}"), i * 16 + 16)
                            project(w_gate, s, 0, GATE_BANK[0]).then_inc(sem("gated"), 1)
                            pe.wait_ge(sem(f"w_up_in{s}"), i * 16 + 16)
                            project(w_up, s, 0, UP_BANK[0]).then_inc(sem("half_upped"), 1)
                            project(w_gate, s, 1, GATE_BANK[1]).then_inc(sem("gated"), 1)
                            pe.wait_ge(sem("y_act"), i * 2 + s + 1)
                            project(w_up, s, 1, UP_BANK[1]).then_inc(sem(f"upped{s}"), 1)
                            pe.wait_ge(sem("hid_done"), i * 4 + 2 * s + 2)
                            turn_hidden(s, 0, 4).then_inc(sem("first_turned"), 1)
                            turn(1 - s, i + s)
                            pe.wait_ge(sem("hid_done"), i * 4 + 2 * s + 3)
                            turn_hidden(s, 1, 0).then_inc(sem("second_turned"), 1)
                            pe.wait_ge(sem("y_dve"), i * 2 + s + 1)
                            pe.wait_ge(sem(f"w_down_in{s}"), i * 16 + 16)
                            for h in range(2):
                                pe.wait_ge(sem("hidT_dve" if h else "hidT_act"), i * 2 + s + 1)
                                for half in range(2):
                                    for k in range(2):
                                        mm = pe.matmul(ps[:, 5 + half, :], hidT[:, 2 * h + k, :],
                                                       w_down[s][:, h, k, 512 * half:512 * half + 512],
                                                       start=(h == 0 and k == 0), stop=(h == 1 and k == 1))
                            mm.then_inc(sem(f"downed{s}"), 1)

        def expert_silu(act):
            def copy_x(s, n):
                act.wait_ge(sem(f"upped{s}"), n + 1)
                act.wait_ge(sem(f"xg_turned{s}"), n + 2)
                act.activation(xgT[s][:, 0:4, :].rearrange("p k n -> p (k n)"), ps[:, 2, :], ACT.Copy)\
                   .then_inc(sem(f"xgT_act{s}"), 1)

            act.sem_inc(sem("y_act"), 1)
            n_chunks = chunk_count(act)
            copy_x(0, 0)
            with act.Fori(0, CHUNKS // 2) as i:
                with act.If(i * 2 < n_chunks):
                    for s in range(2):
                        with act.If(i * 2 + s < n_chunks):
                            for h in range(2):
                                act.wait_ge(sem("gated"), i * 4 + 2 * s + h + 1)
                                act.activation(hid[s][:, HH * h:HH * h + HH], ps[:, GATE_BANK[h], 0:HH], ACT.Silu)\
                                   .then_inc(sem("silu_done"), 1)
                            act.wait_ge(sem("first_turned"), i * 2 + s + 1)
                            act.activation(hidT[:, 0:2, :].rearrange("p k n -> p (k n)"), ps[:, 4, 0:HH], ACT.Copy)\
                               .then_inc(sem("hidT_act"), 1)
                            copy_x(1 - s, i + s)
                            act.wait_ge(sem(f"y_out{s}"), i * 16 + 16)
                            act.wait_ge(sem(f"downed{s}"), i + 2)
                            act.activation(y_sb[s][:, 0:512], ps[:, 5, :], ACT.Copy).then_inc(sem("y_act"), 1)

        def expert_copies(dve):
            def copy_x(s, n):
                dve.wait_ge(sem(f"upped{s}"), n + 1)
                dve.wait_ge(sem(f"xg_turned{s}"), n + 2)
                dve.tensor_copy(xgT[s][:, 4:8, :].rearrange("p k n -> p (k n)"), ps[:, 3, :])\
                   .then_inc(sem(f"xgT_dve{s}"), 1)

            for name in ("hid_done", "y_dve"):
                dve.sem_inc(sem(name), 1)
            n_chunks = chunk_count(dve)
            copy_x(0, 0)
            with dve.Fori(0, CHUNKS // 2) as i:
                with dve.If(i * 2 < n_chunks):
                    for s in range(2):
                        with dve.If(i * 2 + s < n_chunks):
                            for h in range(2):
                                dve.wait_ge(sem(f"upped{s}" if h else "half_upped"), i + 2 if h else i * 2 + s + 1)
                                dve.wait_ge(sem("silu_done"), i * 4 + 2 * s + h + 1)
                                o = hid[s][:, HH * h:HH * h + HH]
                                dve.tensor_tensor(o, o, ps[:, UP_BANK[h], 0:HH], ALU.mult).then_inc(sem("hid_done"), 1)
                            copy_x(1 - s, i + s)
                            dve.wait_ge(sem("second_turned"), i * 2 + s + 1)
                            dve.tensor_copy(hidT[:, 2:4, :].rearrange("p k n -> p (k n)"), ps[:, 0, 0:HH])\
                               .then_inc(sem("hidT_dve"), 1)
                            dve.wait_ge(sem(f"y_out{s}"), i * 16 + 16)
                            dve.wait_ge(sem(f"downed{s}"), i + 2)
                            dve.tensor_copy(y_sb[s][:, 512:1024], ps[:, 6, :]).then_inc(sem("y_dve"), 1)

        with nc.Block() as block:
            @block.sync
            def _(sp):
                o, w = const_at["lane"]
                sp.dma_start(lane, a["consts"][:, o:o + w]).then_inc(sem("lane_in"), 16)
                expert_weights(sp)

            @block.tensor
            def _(pe):
                pe.wait_ge(sem("counted"), 1)
                fb = both.rearrange("p t n -> p (t n)")
                pe.matmul(ps[:, 0, 0:288], con("before"), fb, start=True, stop=True)
                pe.matmul(ps[:, 1, 0:288], con("ones"), fb, start=True, stop=True).then_inc(sem("prefixed"), 1)
                pe.wait_ge(sem("one_hots"), 1)
                for q in range(2 * TILES):
                    n = rows(q % TILES)
                    mm = pe.matmul(ps[:, 2, 0:2 * CHUNKS + 2], one_slot[:n, q, :], by_chunk[:n, q, :],
                                   start=(q == 0), stop=(q == 2 * TILES - 1))
                mm.then_inc(sem("table_made"), 1)
                expert_products(pe)

            @block.scalar
            def _(act):
                act.wait_ge(sem("group_shifted"), 1)
                act.activation(exp4, exp4, ACT.Exp).then_inc(sem("group_exp"), 1)
                act.wait_ge(sem("diff_ready"), 1)
                act.activation(diff, diff, ACT.Exp).then_inc(sem("diff_exp"), 1)
                expert_silu(act)

            @block.vector
            def _(dve):
                chain = Chain(dve, sem("dve_chain"), count["dve"])

                def wide(v, n):
                    return v.unsqueeze(2).to_broadcast([P, TILES, n])

                def first_max(out, vals_, top, order, n):
                    c = cand4 if n == G_ else cand
                    chain(dve.tensor_reduce(top, vals_, AX.X, ALU.max))
                    chain(dve.tensor_tensor(c, vals_, wide(top, n), ALU.is_equal))
                    chain(dve.tensor_tensor(c, c, con(order).unsqueeze(1).to_broadcast([P, TILES, n]), ALU.mult))
                    chain(dve.tensor_reduce(c_max, c, AX.X, ALU.max))
                    chain(dve.tensor_tensor(out, c, wide(c_max, n), ALU.is_equal))

                lg, le = logits[:, :, 0:G_], logits[:, :, G_:G_ + E_]
                first_max(group4, lg, g_max, "down4", G_)
                dve.tensor_tensor(exp4, lg, wide(g_max, G_), ALU.subtract).then_inc(sem("group_shifted"), 1)
                chain(dve.tensor_scalar(cand4, group4, -NEG, NEG, ALU.mult, ALU.add))
                for t in range(TILES):
                    ins = dve.tensor_tensor(le_m[:, t].rearrange("p (g e) -> p g e", g=G_),
                                            le[:, t].rearrange("p (g e) -> p g e", g=G_),
                                            cand4[:, t].unsqueeze(2).to_broadcast([P, G_, E_ // G_]), ALU.add)
                chain(ins)
                first_max(chosen1, le_m, m1, "down32", E_)
                chain(dve.tensor_scalar(slot, chosen1, NEG, None, ALU.mult))
                chain(dve.tensor_tensor(le_m, le_m, slot, ALU.add))
                first_max(chosen2, le_m, m2, "down32", E_)
                dve.tensor_tensor(diff, m2, m1, ALU.subtract).then_inc(sem("diff_ready"), 1)
                chain(dve.tensor_scalar(valid7, con("token"), float(TOKENS), None, ALU.is_lt))
                chain(dve.tensor_tensor(both, chosen1, chosen2, ALU.add))
                dve.tensor_tensor(both, both, wide(valid7, E_), ALU.mult).then_inc(sem("counted"), 1)
                dve.wait_ge(sem("group_exp"), 1)
                chain(dve.tensor_reduce(sum4, exp4, AX.X, ALU.add))
                chain(dve.reciprocal(p_top, sum4))
                dve.wait_ge(sem("diff_exp"), 1)
                chain(dve.tensor_scalar(inv_d, diff, 1.0, None, ALU.add))
                chain(dve.reciprocal(inv_d, inv_d))
                chain(dve.tensor_tensor(first_w, inv_d, p_top, ALU.mult))
                chain(dve.tensor_tensor(second_w, first_w, diff, ALU.mult))
                dve.wait_ge(sem("prefixed"), 1)
                chain(dve.memset(base[:, 0, :], 0.0))
                for t in range(TILES):
                    chain(dve.tensor_tensor(base[:, t + 1, :], base[:, t, :], ps[:, 1, E_ * t:E_ * t + E_], ALU.add))
                chain(dve.tensor_tensor(steps7, base[:, TILES, :].unsqueeze(2).to_broadcast([P, E_, 9]),
                                        con("steps").unsqueeze(1).to_broadcast([P, E_, 9]), ALU.is_gt))
                chain(dve.tensor_reduce(n_chunk, steps7, AX.X, ALU.add))
                chain(dve.memset(ones32, 1.0))
                chain(dve.tensor_tensor_scan(cum, ones32, n_chunk, 0.0, ALU.mult, ALU.add))
                chain(dve.tensor_tensor(cum0, cum, n_chunk, ALU.subtract))
                chain(dve.tensor_scalar(cum0, cum0, float(P), None, ALU.mult))
                chain(dve.tensor_tensor(slot, base[:, 0:TILES, :],
                                        ps[:, 0, 0:288].rearrange("p (t n) -> p t n", n=E_), ALU.add))
                chain(dve.tensor_tensor(slot, slot, cum0.unsqueeze(1).to_broadcast([P, TILES, E_]), ALU.add))
                chain(dve.tensor_tensor(cand, slot, chosen1, ALU.mult))
                chain(dve.tensor_reduce(destf[:, 0:TILES], cand, AX.X, ALU.add))
                chain(dve.tensor_tensor(cand, slot, chosen2, ALU.mult))
                chain(dve.tensor_reduce(destf[:, TILES:2 * TILES], cand, AX.X, ALU.add))
                chain(dve.tensor_scalar(dest_q, destf, 1.0 / P, None, ALU.mult))
                chunks = con("chunk").unsqueeze(1).to_broadcast([P, 2 * TILES, CHUNKS + 1])

                def every(v, n):
                    return v.unsqueeze(2).to_broadcast([P, 2 * TILES, n])

                chain(dve.tensor_tensor(one_chunk, chunks, every(dest_q, CHUNKS + 1), ALU.is_le))
                chain(dve.tensor_reduce(dest_c, one_chunk, AX.X, ALU.add))
                chain(dve.tensor_scalar(dest_c, dest_c, -1.0, None, ALU.add))
                chain(dve.tensor_tensor(one_chunk, chunks, every(dest_c, CHUNKS + 1), ALU.is_equal))
                for j in range(2):
                    o = slice(j * TILES, (j + 1) * TILES)
                    chain(dve.tensor_tensor(one_token[:, o], one_chunk[:, o],
                                            con("token").unsqueeze(2).to_broadcast([P, TILES, CHUNKS + 1]), ALU.mult))
                    dve.scalar_tensor_tensor(one_chunk[:, o], one_chunk[:, o], float(1 + j * TOKENS),
                                             one_token[:, o], ALU.mult, ALU.add)
                chain(dve.scalar_tensor_tensor(dest_q, dest_c, -float(P), destf, ALU.mult, ALU.add))
                dve.wait_ge(sem("lane_in"), 16)
                dve.tensor_tensor(one_slot, lane.unsqueeze(1).to_broadcast([P, 2 * TILES, P]),
                                  every(dest_q, P), ALU.is_equal).then_inc(sem("one_hots"), 1)
                chain(dve.tensor_tensor(ends_le[0:1], cum[0:1].unsqueeze(1).to_broadcast([1, CHUNKS + 1, E_]),
                                        con("chunk", 1).unsqueeze(2).to_broadcast([1, CHUNKS + 1, E_]), ALU.is_le))
                chain(dve.tensor_reduce(chunk_f[0:1, 0:CHUNKS + 1], ends_le[0:1], AX.X, ALU.add))
                chain(dve.tensor_scalar(chunk_f[0:1, 0:CHUNKS + 1], chunk_f[0:1, 0:CHUNKS + 1], float(E_ - 1), None,
                                        ALU.min))
                dve.tensor_copy(row_ints[0:1, CHUNKS + 1:CHUNKS + 2], cum[0:1, E_ - 1:E_])
                dve.tensor_copy(row_ints[0:1, 0:CHUNKS + 1], chunk_f[0:1, 0:CHUNKS + 1]).then_inc(sem("plan_ready"), 1)
                dve.wait_ge(sem("table_made"), 1)
                dve.tensor_copy(ints[:, 0:2 * CHUNKS + 2], ps[:, 2, 0:2 * CHUNKS + 2]).then_inc(sem("table_ready"), 1)
                dve.wait_ge(sem("table_ready"), 1)
                expert_copies(dve)

            @block.gpsimd
            def _(pool):
                pool.wait_ge(sem("table_ready"), 1)
                expert_rows(pool)

        YS = 3
        y_rows = flat(A1, YS * 2048).rearrange("p (s j n) -> p s j n", s=YS, j=2)
        final = flat(A1 + YS * 2048, 2048).rearrange("p (s n) -> p s n", s=2)
        junk9 = flat(A1 + YS * 2048 + 2048, D)
        st9 = flat(A1 + YS * 2048 + 3072, 48).rearrange("p (q n) -> p q n", n=16)
        sd9, rs9, ms9 = st9[:, 0, :], st9[:, 1, :], st9[:, 2, :]
        with nc.Block() as block:
            @block.sync
            def _(sp):
                for t in range(TILES):
                    n = rows(t)
                    if t >= YS:
                        sp.wait_ge(sem("rows_summed"), t - YS + 1)
                    for j in range(2):
                        o = 1 + j * TOKENS + P * t
                        sp.dma_start(y_rows[:n, t % YS, j, :], scratch_y[o:o + n, :])\
                          .then_inc(sem(f"y_rows_in{t % YS}"), 16)

            @block.gpsimd
            def _(pool):
                for t in range(TILES):
                    pool.wait_ge(sem("final_ready"), t + 1)
                    dst = out["out0"][P * t:P * t + P, :] if t < NQ else out["out1"]
                    pool.dma_start(dst, final[:rows(t), t % 2, :]).then_inc(sem(f"final_out{t % 2}"), 16)
                pool.wait_ge(sem("final_out0"), 16 * 5)
                pool.wait_ge(sem("final_out1"), 16 * 4)

            @block.vector
            def _(dve):
                chain = Chain(dve, sem("dve_chain"), count["dve"])
                for t in range(TILES + 1):
                    if t < TILES:
                        n = rows(t)
                        dve.wait_ge(sem(f"y_rows_in{t % YS}"), 32 * (t // YS + 1))
                        for j, w in enumerate((first_w, second_w)):
                            ins = dve.scalar_tensor_tensor(x_res[:n, t, :], y_rows[:n, t % YS, j, :], w[:n, t:t + 1],
                                                           x_res[:n, t, :], ALU.mult, ALU.add)
                            if j == 0:
                                chain(ins)
                        ins.then_inc(sem("rows_summed"), 1)
                    if t >= 1:
                        q, n = t - 1, rows(t - 1)
                        dve.wait_ge(sem("sd9_ready"), q + 1)
                        chain(dve.reciprocal(rs9[:n, q:q + 1], sd9[:n, q:q + 1]))
                        if q >= 2:
                            dve.wait_ge(sem(f"final_out{q % 2}"), 16 * (q // 2))
                        dve.scalar_tensor_tensor(final[:n, q % 2, :], x_res[:n, q, :], rs9[:n, q:q + 1],
                                                 final_g[:n, :], ALU.mult, ALU.mult).then_inc(sem("final_ready"), 1)

            @block.scalar
            def _(act):
                chain = Chain(act, sem("act_chain"), count["act"])
                for t in range(TILES):
                    n = rows(t)
                    act.wait_ge(sem("rows_summed"), t + 1)
                    chain(act.activation(junk9[:n, :], x_res[:n, t, :], ACT.Square, scale=1 / 32,
                                         accum_out=ms9[:n, t:t + 1]))
                    act.activation(sd9[:n, t:t + 1], ms9[:n, t:t + 1], ACT.Sqrt, bias=con("eps")[:n, 0:1])\
                       .then_inc(sem("sd9_ready"), 1)


OUT_SHAPES = {
    "out0": (SEQ, D), "out1": (NB * NS, D),
    "out2": (SEQ, 256), "out3": (NB * NS, 256), "out4": (SEQ, 256), "out5": (NB * NS, 256),
    "out6": (512, 256), "out7": (NB, 512, 256), "out8": (TAPS - 1, CH), "out9": (NB, TAPS - 1, CH),
}


def kernel(**inputs):
    import concourse.bacc as bacc
    from concourse.bass_utils import run_bass_kernel_spmd

    x = {k: np.asarray(v) for k, v in inputs.items()}
    d = {
        "x_prompt": x["x_prompt"], "x_sample": x["x_sample"], "consts": const_table()[0],
        "ln1": x["ln1"][0], "ln2": x["ln2"][0], "ln_final": x["ln_final"],
        "w_in": x["w_in"][0], "w_out": x["w_out"][0],
        "conv_g": x["conv_ln_g"][0], "conv_b": x["conv_ln_b"][0],
        "norm_conv": x["out_norm_conv"][0], "norm_att": x["out_norm_att"][0],
        "w_gate": x["w_exp_gate"][0], "w_up": x["w_exp_up"][0], "w_down": x["w_exp_down"][0],
        "state_conv": x["state_conv"][0], "state_win": x["state_win_kv"][0].reshape(NB, 512, 256),
        "page_table": x["page_table"].reshape(1, NB * PAGES),
    }
    taps = np.concatenate([x["conv_dw_w"][0], x["conv_dw_b"]], axis=0)
    d["dw"] = taps.reshape(TAPS + 1, 4, P).transpose(2, 1, 0).reshape(P, 4 * (TAPS + 1))
    d["state_conv_T"] = d["state_conv"].reshape(NB, TAPS - 1, 4, P).transpose(3, 2, 1, 0).reshape(P, -1)

    w = d["w_in"]
    q = w[:, D:D + 512].reshape(D, KV, R, HD).transpose(0, 2, 1, 3).reshape(D, 512)
    kv = w[:, D + 512:D + 1280].reshape(D, 3, KV, 2, HD).transpose(0, 1, 3, 2, 4).reshape(D, 768)
    d["w_in"] = np.concatenate([w[:, :D], q, kv, w[:, D + 1280:]], axis=1)

    def by_use(kv):
        kv = kv.reshape(-1, P, KV, 2, HD)
        keys = kv[:, :, :, 0].transpose(0, 2, 3, 1).reshape(-1, P, P)
        return np.concatenate([keys, kv[:, :, :, 1].reshape(-1, P, P)], axis=2)

    d["cache_sel"] = by_use(x["cache_sel_kv"][0])
    d["state_win_use"] = by_use(d["state_win"])
    cmp = x["cache_cmp_kv"][0].reshape(-1, 2, CMP // 2, 2, KV, 2, HD)
    d["cache_cmp"] = cmp.transpose(0, 3, 6, 5, 2, 1, 4).reshape(-1, P, 256)
    d["state_win"] = d["state_win"].reshape(NB, 512, KV, 2, HD).transpose(0, 1, 3, 2, 4).reshape(NB, 512, 256)
    w1 = np.stack([x["w_cmp_k1"][0], x["w_cmp_v1"][0]]).reshape(2, CMP // 2, 2, HD, P)
    d["w_cmp1"] = w1.transpose(2, 3, 0, 1, 4).reshape(P, 2 * CMP // 2 * P)
    pe = x["cmp_pos_emb"][0].reshape(CMP // 2, 2, 2, HD).transpose(1, 3, 2, 0).reshape(P, 64)
    d["pos_emb"] = np.repeat(pe, 4, axis=1)
    wk2 = x["w_cmp_k2"][0]
    zero = np.zeros_like(wk2)
    d["w_cmp2"] = np.concatenate([wk2, zero, zero, wk2, x["w_cmp_v2"][0]], axis=1)
    router = np.concatenate([x["w_router_group"][0], x["w_router_expert"][0]], axis=1)
    d["w_router"] = router.reshape(P, KT_ * 36)

    nc = bacc.Bacc("TRN2", target_bir_lowering=False, num_devices=1)
    arrays, args = {}, {}
    for name, v in d.items():
        v = np.ascontiguousarray(v)
        arrays[f"in_{name}"] = v
        args[name] = nc.dram_tensor(f"in_{name}", v.shape, mybir.dt.from_np(v.dtype), kind="ExternalInput").ap()
    for name, shape in OUT_SHAPES.items():
        args[name] = nc.dram_tensor(name, shape, F32, kind="ExternalOutput").ap()
    build(nc, args)
    r = run_bass_kernel_spmd(nc, [arrays], core_ids=[0]).results[0]
    shapes = [(1, SEQ, D), (NB, NS, D), (1, 1, SEQ, KV, 2, HD), (1, NB, NS, KV, 2, HD),
              (1, 1, SEQ, KV, 2, HD), (1, NB, NS, KV, 2, HD), (1, 1, 512, KV, 2, HD),
              (1, NB, 512, KV, 2, HD), (1, 1, TAPS - 1, CH), (1, NB, TAPS - 1, CH)]
    outs = []
    for i, s in enumerate(shapes):
        o = np.asarray(r[f"out{i}"])
        if s[-1] == HD:
            o = o.reshape(s[:-3] + (2, KV, HD)).swapaxes(-3, -2)
        outs.append(o.reshape(s))
    return tuple(outs)
```
